# Optimizing a Trainium2 kernel written in Bass

```python
import math
import jax
import jax.numpy as jnp
from jax import lax
import numpy as np
import jax, jax.numpy as jnp

D_MODEL = 1024
BATCH = 1
SEQ = 256
DEPTH = 2

N_MIXERS = 4
N_PER_MIXER = tuple((DEPTH - m + N_MIXERS - 1) // N_MIXERS for m in range(N_MIXERS))
PLE_DIM = 256
ROPE_THETA = 10000.0
EPS = 1e-6
Q_BLOCK = 128
D_FF = (-((-8 * D_MODEL) // 3) + 255) // 256 * 256

GLA_HEADS = 4
GLA_DK = D_MODEL // 2
GLA_DV = D_MODEL
GLA_HK = GLA_DK // GLA_HEADS
GLA_HV = GLA_DV // GLA_HEADS
GLA_RANK = 16
GLA_TAU = 16.0
GLA_CHUNK = 64
GLA_IN = 2 * GLA_DK + 2 * GLA_DV + 2 * GLA_RANK

DIFF_HEAD_DIM = 64
DIFF_HEADS = D_MODEL // (2 * DIFF_HEAD_DIM)
DIFF_IN = 3 * D_MODEL

SSD_D_INNER = 2 * D_MODEL
SSD_HEAD_DIM = 64
SSD_HEADS = SSD_D_INNER // SSD_HEAD_DIM
SSD_GROUPS = 8
SSD_STATE = 128
SSD_CONV = 5
SSD_CHUNK = 128
SSD_CONV_DIM = SSD_D_INNER + 2 * SSD_GROUPS * SSD_STATE
SSD_IN = SSD_D_INNER + SSD_CONV_DIM + 2 * SSD_HEADS

DIL_PAIRS = ((128, 1), (512, 4), (2048, 16))
DIL_GROUPS = len(DIL_PAIRS)
DIL_HEADS = 16
DIL_HEAD_DIM = 64
DIL_WIDTH = DIL_HEADS * DIL_HEAD_DIM
DIL_IN = 3 * DIL_GROUPS * DIL_WIDTH


F32 = jnp.float32

def split_cols(x, sizes):
    out, start = [], 0
    for s in sizes:
        out.append(x[..., start:start + s])
        start += s
    return out

def rms_norm(x, g):
    xf = x.astype(F32)
    y = xf * lax.rsqrt(jnp.mean(xf * xf, axis=-1, keepdims=True) + EPS)
    return (y * g.astype(F32)).astype(x.dtype)

def rope(x, pos):
    hd = x.shape[-1]
    half = hd // 2
    inv = ROPE_THETA ** (-jnp.arange(half, dtype=F32) * 2.0 / hd)
    ang = pos.astype(F32)[:, None] * inv[None, :]
    cos = jnp.cos(ang)[:, None, :]
    sin = jnp.sin(ang)[:, None, :]
    xf = x.astype(F32)
    x1, x2 = xf[..., :half], xf[..., half:]
    return jnp.concatenate([x1 * cos - x2 * sin, x2 * cos + x1 * sin], axis=-1).astype(x.dtype)

def swiglu(h, w_in, w_out):
    g, u = split_cols(h @ w_in, [D_FF, D_FF])
    return (jax.nn.silu(g) * u) @ w_out

def gla_chunked(q, k, v, log_a, strict):
    bsz, nh, seq, dk = q.shape
    dv = v.shape[-1]
    c = GLA_CHUNK
    n = seq // c
    qf = q.astype(F32).reshape(bsz, nh, n, c, dk)
    kf = k.astype(F32).reshape(bsz, nh, n, c, dk)
    vf = v.astype(F32).reshape(bsz, nh, n, c, dv)
    b = jnp.cumsum(log_a.astype(F32).reshape(bsz, nh, n, c, dk), axis=3)
    b_last = b[:, :, :, -1:, :]
    q_in = qf * jnp.exp(b)
    scores = jnp.einsum('bhncd,bhnjd->bhncj', q_in, kf * jnp.exp(-b))
    mask = jnp.tril(jnp.ones((c, c), dtype=bool), -1 if strict else 0)
    scores = jnp.where(mask, scores, 0.0)
    o_intra = jnp.einsum('bhncj,bhnje->bhnce', scores, vf)
    u = jnp.einsum('bhncd,bhnce->bhnde', kf * jnp.exp(b_last - b), vf)
    decay = jnp.exp(b_last[:, :, :, 0, :])

    def step(s_prev, inp):
        u_n, a_n = inp
        return s_prev * a_n[..., None] + u_n, s_prev

    s0 = jnp.zeros((bsz, nh, dk, dv), F32)
    _, s_prev = lax.scan(step, s0, (jnp.moveaxis(u, 2, 0), jnp.moveaxis(decay, 2, 0)))
    s_prev = jnp.moveaxis(s_prev, 0, 2)
    o_inter = jnp.einsum('bhncd,bhnde->bhnce', q_in, s_prev)
    return (o_intra + o_inter).reshape(bsz, nh, seq, dv)

def gla_mixer(h, w_in, w_gate_f, b_gate_f, w_gate_b, b_gate_b, g_out, w_out):
    bsz, seq, _ = h.shape
    q, k, v, r, zf, zb = split_cols(h @ w_in, [GLA_DK, GLA_DK, GLA_DV, GLA_DV, GLA_RANK, GLA_RANK])

    def heads(t, hd):
        return t.reshape(bsz, seq, GLA_HEADS, hd).transpose(0, 2, 1, 3)

    qh = heads(q, GLA_HK) * (GLA_HK ** -0.5)
    kh = heads(k, GLA_HK)
    vh = heads(v, GLA_HV)
    la_f = heads(jax.nn.log_sigmoid((zf @ w_gate_f + b_gate_f).astype(F32)) / GLA_TAU, GLA_HK)
    la_b = heads(jax.nn.log_sigmoid((zb @ w_gate_b + b_gate_b).astype(F32)) / GLA_TAU, GLA_HK)

    def flip(t):
        return jnp.flip(t, axis=2)

    o = gla_chunked(qh, kh, vh, la_f, False) + flip(
        gla_chunked(flip(qh), flip(kh), flip(vh), flip(la_b), True))
    o = rms_norm(o.transpose(0, 2, 1, 3).astype(h.dtype), g_out).reshape(bsz, seq, GLA_DV)
    return (o * jax.nn.silu(r)) @ w_out

def diff_attn_mixer(h, pos, w_in, g_q, g_k, lam_q1, lam_k1, lam_q2, lam_k2, g_sub, w_out, lambda_init):
    bsz, seq, _ = h.shape
    nh, dh = DIFF_HEADS, DIFF_HEAD_DIM
    q, k, v = split_cols(h @ w_in, [D_MODEL, D_MODEL, D_MODEL])
    q = rms_norm(q.reshape(bsz, seq, nh, 2, dh), g_q)
    k = rms_norm(k.reshape(bsz, seq, nh, 2, dh), g_k)
    q = rope(q.reshape(bsz, seq, 2 * nh, dh), pos).reshape(bsz, seq, nh, 2, dh)
    k = rope(k.reshape(bsz, seq, 2 * nh, dh), pos).reshape(bsz, seq, nh, 2, dh)
    lam = (jnp.exp(jnp.sum(lam_q1.astype(F32) * lam_k1.astype(F32)))
           - jnp.exp(jnp.sum(lam_q2.astype(F32) * lam_k2.astype(F32))) + lambda_init)
    nb = seq // Q_BLOCK
    qb = q.reshape(bsz, nb, Q_BLOCK, nh, 2, dh).transpose(1, 0, 3, 4, 2, 5)
    kt = k.transpose(0, 2, 3, 1, 4)
    vt = v.reshape(bsz, seq, nh, 2 * dh).transpose(0, 2, 1, 3)
    scale = dh ** -0.5

    def block(q_blk):
        s = jnp.einsum('bhtqd,bhtkd->bhtqk', q_blk, kt).astype(F32) * scale
        pr = jax.nn.softmax(s, axis=-1)
        a = pr[:, :, 0] - lam * pr[:, :, 1]
        return jnp.einsum('bhqk,bhkd->bhqd', a.astype(vt.dtype), vt)

    o = lax.map(block, qb)
    o = o.transpose(1, 0, 3, 2, 4).reshape(bsz, seq, nh, 2 * dh)
    o = rms_norm(o, g_sub) * (1.0 - lambda_init)
    return o.reshape(bsz, seq, D_MODEL) @ w_out

def depthwise_conv_centered(x, w, b):
    width, ch = w.shape
    y = lax.conv_general_dilated(
        x, w[:, None, :].astype(x.dtype), window_strides=(1,),
        padding=[((width - 1) // 2, width // 2)],
        dimension_numbers=('NWC', 'WIO', 'NWC'), feature_group_count=ch)
    return y + b

def ssd_chunked(x, dt, a, bm, cm, strict):
    bsz, seq, nh, hp = x.shape
    ng, ns = bm.shape[2], bm.shape[3]
    hg = nh // ng
    c = SSD_CHUNK
    nc = seq // c
    xdt = (x.astype(F32) * dt[..., None]).reshape(bsz, nc, c, ng, hg, hp)
    acum = jnp.cumsum((dt * a).reshape(bsz, nc, c, ng, hg), axis=2)
    bc = bm.astype(F32).reshape(bsz, nc, c, ng, ns)
    cc = cm.astype(F32).reshape(bsz, nc, c, ng, ns)
    mask = jnp.tril(jnp.ones((c, c), dtype=bool), -1 if strict else 0)[:, :, None, None]
    diff = acum[:, :, :, None] - acum[:, :, None, :]
    lmat = jnp.where(mask, jnp.exp(jnp.where(mask, diff, 0.0)), 0.0)
    cb = jnp.einsum('bnigs,bnjgs->bnijg', cc, bc)
    y_diag = jnp.einsum('bnijg,bnijgh,bnjghp->bnighp', cb, lmat, xdt)
    a_last = acum[:, :, -1]
    decay_states = jnp.exp(a_last[:, :, None] - acum)
    states = jnp.einsum('bnjgs,bnjgh,bnjghp->bnghps', bc, decay_states, xdt)

    def step(s_prev, inp):
        st, dec = inp
        return s_prev * dec[..., None, None] + st, s_prev

    s0 = jnp.zeros((bsz, ng, hg, hp, ns), F32)
    _, prev = lax.scan(step, s0, (jnp.moveaxis(states, 1, 0), jnp.moveaxis(jnp.exp(a_last), 1, 0)))
    prev = jnp.moveaxis(prev, 0, 1)
    y_off = jnp.einsum('bnigs,bnigh,bnghps->bnighp', cc, jnp.exp(acum), prev)
    return (y_diag + y_off).reshape(bsz, seq, nh, hp)

def ssd_mixer(h, w_in, conv_w, conv_b, dt_bias_f, a_log_f, dt_bias_b, a_log_b, d_skip, g_norm, w_out):
    bsz, seq, _ = h.shape
    z, xbc, dt_f, dt_b = split_cols(h @ w_in, [SSD_D_INNER, SSD_CONV_DIM, SSD_HEADS, SSD_HEADS])
    xbc = jax.nn.silu(depthwise_conv_centered(xbc, conv_w, conv_b))
    xs, bm, cm = split_cols(xbc, [SSD_D_INNER, SSD_GROUPS * SSD_STATE, SSD_GROUPS * SSD_STATE])
    xs = xs.reshape(bsz, seq, SSD_HEADS, SSD_HEAD_DIM)
    bm = bm.reshape(bsz, seq, SSD_GROUPS, SSD_STATE)
    cm = cm.reshape(bsz, seq, SSD_GROUPS, SSD_STATE)
    dtf = jax.nn.softplus((dt_f + dt_bias_f).astype(F32))
    dtb = jax.nn.softplus((dt_b + dt_bias_b).astype(F32))
    af = -jnp.exp(a_log_f.astype(F32))
    ab = -jnp.exp(a_log_b.astype(F32))

    def flip(t):
        return jnp.flip(t, axis=1)

    y = ssd_chunked(xs, dtf, af, bm, cm, False) + flip(
        ssd_chunked(flip(xs), flip(dtb), ab, flip(bm), flip(cm), True))
    y = y + xs.astype(F32) * d_skip.astype(F32)[:, None]
    y = y.astype(h.dtype).reshape(bsz, seq, SSD_D_INNER) * jax.nn.silu(z)
    y = rms_norm(y.reshape(bsz, seq, SSD_GROUPS, SSD_D_INNER // SSD_GROUPS),
                 g_norm.reshape(SSD_GROUPS, SSD_D_INNER // SSD_GROUPS))
    return y.reshape(bsz, seq, SSD_D_INNER) @ w_out

def dilated_group(q, k, v, window, dilation):
    bsz, seq, nh, hd = q.shape
    n_side = (window // 2) // dilation
    offsets = dilation * jnp.arange(-n_side, n_side + 1, dtype=jnp.int32)
    nb = seq // Q_BLOCK
    qb = q.reshape(bsz, nb, Q_BLOCK, nh, hd).swapaxes(0, 1)
    starts = jnp.arange(nb, dtype=jnp.int32) * Q_BLOCK
    scale = hd ** -0.5

    def block(args):
        q_blk, start = args
        idx = (start + jnp.arange(Q_BLOCK, dtype=jnp.int32))[:, None] + offsets[None, :]
        valid = (idx >= 0) & (idx < seq)
        idx = jnp.clip(idx, 0, seq - 1)
        kg = k[:, idx]
        vg = v[:, idx]
        s = jnp.einsum('bqhd,bqmhd->bqhm', q_blk, kg).astype(F32) * scale
        s = jnp.where(valid[None, :, None, :], s, -jnp.inf)
        m = jnp.max(s, axis=-1, keepdims=True)
        e = jnp.exp(s - m)
        l = jnp.sum(e, axis=-1, keepdims=True)
        o = jnp.einsum('bqhm,bqmhd->bqhd', (e / l).astype(vg.dtype), vg)
        return o, (m + jnp.log(l))[..., 0]

    o, lse = lax.map(block, (qb, starts))
    return (o.swapaxes(0, 1).reshape(bsz, seq, nh, hd),
            lse.swapaxes(0, 1).reshape(bsz, seq, nh))

def dilated_mixer(h, pos, w_in, g_q, g_k, w_out):
    bsz, seq, _ = h.shape
    qkv = (h @ w_in).reshape(bsz, seq, 3, DIL_GROUPS, DIL_HEADS, DIL_HEAD_DIM)
    q = rms_norm(qkv[:, :, 0], g_q[:, None, :])
    k = rms_norm(qkv[:, :, 1], g_k[:, None, :])
    v = qkv[:, :, 2]
    flat = (bsz, seq, DIL_GROUPS * DIL_HEADS, DIL_HEAD_DIM)
    q = rope(q.reshape(flat), pos).reshape(bsz, seq, DIL_GROUPS, DIL_HEADS, DIL_HEAD_DIM)
    k = rope(k.reshape(flat), pos).reshape(bsz, seq, DIL_GROUPS, DIL_HEADS, DIL_HEAD_DIM)
    outs, lses = [], []
    for gi, (window, dilation) in enumerate(DIL_PAIRS):
        o, lse = dilated_group(q[:, :, gi], k[:, :, gi], v[:, :, gi], window, dilation)
        outs.append(o.astype(F32))
        lses.append(lse)
    wts = jax.nn.softmax(jnp.stack(lses, axis=0), axis=0)
    o = jnp.sum(wts[..., None] * jnp.stack(outs, axis=0), axis=0)
    return o.astype(h.dtype).reshape(bsz, seq, DIL_WIDTH) @ w_out

def first_inputs(seed: int = 0) -> dict:
    key = jax.random.key(seed)
    ks = iter(jax.random.split(key, 48))
    n_a, n_b, n_c, n_d = N_PER_MIXER

    def nrm(shape, std):
        return jax.random.normal(next(ks), shape, F32) * std

    def dense(shape):
        return nrm(shape, shape[-2] ** -0.5)

    def gain(shape):
        return 1.0 + nrm(shape, 0.05)

    x = nrm((BATCH, SEQ, D_MODEL), 1.0)
    p = nrm((DEPTH, BATCH, SEQ, PLE_DIM), 1.0)

    def dt_bias(shape):
        dt = jnp.exp(jax.random.uniform(next(ks), shape, F32, math.log(1e-3), math.log(1e-1)))
        return dt + jnp.log(-jnp.expm1(-dt))

    def a_log(shape):
        return jnp.log(jax.random.uniform(next(ks), shape, F32, 1.0, 16.0))

    return {
        'x': x,
        'p': p,
        'norm_mix': gain((DEPTH, D_MODEL)),
        'norm_ffn': gain((DEPTH, D_MODEL)),
        'ffn_w_in': dense((DEPTH, D_MODEL, 2 * D_FF)),
        'ffn_w_out': dense((DEPTH, D_FF, D_MODEL)),
        'ple_norm': gain((DEPTH, D_MODEL)),
        'ple_w_gate': dense((DEPTH, D_MODEL, D_MODEL)),
        'ple_w_proj': dense((DEPTH, PLE_DIM, D_MODEL)),
        'gla_w_in': dense((n_a, D_MODEL, GLA_IN)),
        'gla_w_gate_f': dense((n_a, GLA_RANK, GLA_DK)),
        'gla_b_gate_f': nrm((n_a, GLA_DK), 0.01),
        'gla_w_gate_b': dense((n_a, GLA_RANK, GLA_DK)),
        'gla_b_gate_b': nrm((n_a, GLA_DK), 0.01),
        'gla_g_out': gain((n_a, GLA_HV)),
        'gla_w_out': dense((n_a, GLA_DV, D_MODEL)),
        'diff_w_in': dense((n_b, D_MODEL, DIFF_IN)),
        'diff_g_q': gain((n_b, 2, DIFF_HEAD_DIM)),
        'diff_g_k': gain((n_b, 2, DIFF_HEAD_DIM)),
        'diff_lam_q1': nrm((n_b, DIFF_HEAD_DIM), 0.1),
        'diff_lam_k1': nrm((n_b, DIFF_HEAD_DIM), 0.1),
        'diff_lam_q2': nrm((n_b, DIFF_HEAD_DIM), 0.1),
        'diff_lam_k2': nrm((n_b, DIFF_HEAD_DIM), 0.1),
        'diff_g_sub': gain((n_b, 2 * DIFF_HEAD_DIM)),
        'diff_w_out': dense((n_b, D_MODEL, D_MODEL)),
        'ssd_w_in': dense((n_c, D_MODEL, SSD_IN)),
        'ssd_conv_w': nrm((n_c, SSD_CONV, SSD_CONV_DIM), SSD_CONV ** -0.5),
        'ssd_conv_b': nrm((n_c, SSD_CONV_DIM), 0.01),
        'ssd_dt_bias_f': dt_bias((n_c, SSD_HEADS)),
        'ssd_a_log_f': a_log((n_c, SSD_HEADS)),
        'ssd_dt_bias_b': dt_bias((n_c, SSD_HEADS)),
        'ssd_a_log_b': a_log((n_c, SSD_HEADS)),
        'ssd_d': gain((n_c, SSD_HEADS)),
        'ssd_g_norm': gain((n_c, SSD_D_INNER)),
        'ssd_w_out': dense((n_c, SSD_D_INNER, D_MODEL)),
        'dil_w_in': dense((n_d, D_MODEL, DIL_IN)),
        'dil_g_q': gain((n_d, DIL_GROUPS, DIL_HEAD_DIM)),
        'dil_g_k': gain((n_d, DIL_GROUPS, DIL_HEAD_DIM)),
        'dil_w_out': dense((n_d, DIL_WIDTH, D_MODEL)),
    }

def first_block(x, p, norm_mix, norm_ffn, ffn_w_in, ffn_w_out, ple_norm, ple_w_gate, ple_w_proj,
              gla_w_in, gla_w_gate_f, gla_b_gate_f, gla_w_gate_b, gla_b_gate_b, gla_g_out, gla_w_out,
              diff_w_in, diff_g_q, diff_g_k, diff_lam_q1, diff_lam_k1, diff_lam_q2, diff_lam_k2,
              diff_g_sub, diff_w_out,
              ssd_w_in, ssd_conv_w, ssd_conv_b, ssd_dt_bias_f, ssd_a_log_f, ssd_dt_bias_b,
              ssd_a_log_b, ssd_d, ssd_g_norm, ssd_w_out,
              dil_w_in, dil_g_q, dil_g_k, dil_w_out):
    seq = x.shape[1]
    pos = jnp.arange(seq, dtype=jnp.int32)
    h = x
    for i in range(DEPTH):
        kind = i % N_MIXERS
        j = i // N_MIXERS
        hn = rms_norm(h, norm_mix[i])
        if kind == 0:
            mix = gla_mixer(hn, gla_w_in[j], gla_w_gate_f[j], gla_b_gate_f[j], gla_w_gate_b[j],
                            gla_b_gate_b[j], gla_g_out[j], gla_w_out[j])
        elif kind == 1:
            lambda_init = 0.8 - 0.6 * math.exp(-0.3 * i)
            mix = diff_attn_mixer(hn, pos, diff_w_in[j], diff_g_q[j], diff_g_k[j], diff_lam_q1[j],
                                  diff_lam_k1[j], diff_lam_q2[j], diff_lam_k2[j], diff_g_sub[j],
                                  diff_w_out[j], lambda_init)
        elif kind == 2:
            mix = ssd_mixer(hn, ssd_w_in[j], ssd_conv_w[j], ssd_conv_b[j], ssd_dt_bias_f[j],
                            ssd_a_log_f[j], ssd_dt_bias_b[j], ssd_a_log_b[j], ssd_d[j],
                            ssd_g_norm[j], ssd_w_out[j])
        else:
            mix = dilated_mixer(hn, pos, dil_w_in[j], dil_g_q[j], dil_g_k[j], dil_w_out[j])
        h = h + mix
        h = h + swiglu(rms_norm(h, norm_ffn[i]), ffn_w_in[i], ffn_w_out[i])
        gate = jax.nn.sigmoid(rms_norm(h, ple_norm[i]) @ ple_w_gate[i])
        h = h + gate * (p[i] @ ple_w_proj[i])
    return h


N_MIXERS_2 = 2
CONV_WIDTH = D_MODEL
CONV_K = 3
N_HEADS = 16
HEAD_DIM = D_MODEL // N_HEADS
ATTN_WIDTH = N_HEADS * HEAD_DIM
MOBA_BLOCK = 256
MOBA_TOPK = 3
Q_CHUNK = 64
N_CONV_LAYERS = (DEPTH + 1) // 2
N_ATTN_LAYERS = DEPTH // 2
NEG = -1e30


def rms_norm_2(x, g):
    x32 = x.astype(jnp.float32)
    y = x32 * lax.rsqrt(jnp.mean(x32 * x32, axis=-1, keepdims=True) + EPS)
    return (y * g.astype(jnp.float32)).astype(x.dtype)

def alibi_slopes(n_heads):
    return jnp.asarray(2.0 ** (-8.0 * np.arange(1, n_heads + 1) / n_heads), dtype=jnp.float32)

def short_conv_mixer(h, w_in, conv_w, w_out):
    S = h.shape[1]
    b_gate, c_gate, xv, z = jnp.split(h @ w_in, 4, axis=-1)
    u = c_gate * xv
    u_pad = jnp.pad(u, ((0, 0), (CONV_K - 1, 0), (0, 0)))
    conv = conv_w[0] * u_pad[:, 0:S]
    for k in range(1, CONV_K):
        conv = conv + conv_w[k] * u_pad[:, k:k + S]
    y = b_gate * conv * jax.nn.silu(z)
    return y @ w_out

def moba_mixer(h, w_in, q_gain, k_gain, w_out):
    Bsz, S, _ = h.shape
    q, k, v, z = jnp.split(h @ w_in, 4, axis=-1)

    def heads(t):
        return t.reshape(Bsz, S, N_HEADS, HEAD_DIM).transpose(0, 2, 1, 3)

    q = rms_norm_2(heads(q), q_gain) * (HEAD_DIM ** -0.5)
    k = rms_norm_2(heads(k), k_gain)
    v = heads(v)

    n_blk = -(-S // MOBA_BLOCK)
    s_pad = n_blk * MOBA_BLOCK
    pad = ((0, 0), (0, 0), (0, s_pad - S), (0, 0))
    q, k, v = jnp.pad(q, pad), jnp.pad(k, pad), jnp.pad(v, pad)
    k_blocks = k.reshape(Bsz, N_HEADS, n_blk, MOBA_BLOCK, HEAD_DIM)
    v_blocks = v.reshape(Bsz, N_HEADS, n_blk, MOBA_BLOCK, HEAD_DIM)
    k_mean = jnp.mean(k_blocks.astype(jnp.float32), axis=3).astype(k.dtype)

    topk = min(MOBA_TOPK, n_blk)
    slopes = alibi_slopes(N_HEADS)
    n_chunk = s_pad // Q_CHUNK
    h_ar = jnp.arange(N_HEADS)[:, None, None]
    blk_ar = jnp.arange(n_blk)
    key_off = jnp.arange(MOBA_BLOCK)
    q_off = jnp.arange(Q_CHUNK)

    def chunk(i):
        b = i // n_chunk
        c = i % n_chunk
        t0 = c * Q_CHUNK
        qc = lax.dynamic_slice_in_dim(q[b], t0, Q_CHUNK, axis=1)
        kb = k_blocks[b]
        vb = v_blocks[b]
        q_blk = t0 // MOBA_BLOCK
        t_pos = t0 + q_off
        gate = jnp.einsum('hqd,hnd->hqn', qc, k_mean[b]).astype(jnp.float32)
        gate = jnp.where(blk_ar < q_blk, gate, NEG)
        _, idx = lax.top_k(gate, topk)
        valid = idx < q_blk
        k_sel = kb[h_ar, idx]
        v_sel = vb[h_ar, idx]
        s_past = jnp.einsum('hqd,hqjkd->hqjk', qc, k_sel).astype(jnp.float32)
        past_dist = (t_pos[None, :, None, None] - (idx[..., None] * MOBA_BLOCK + key_off)).astype(jnp.float32)
        s_past = s_past - slopes[:, None, None, None] * past_dist
        s_past = jnp.where(valid[..., None], s_past, NEG)
        k_own = lax.dynamic_index_in_dim(kb, q_blk, axis=1, keepdims=False)
        v_own = lax.dynamic_index_in_dim(vb, q_blk, axis=1, keepdims=False)
        own_dist = t_pos[:, None] - (q_blk * MOBA_BLOCK + key_off)[None, :]
        s_own = jnp.einsum('hqd,hkd->hqk', qc, k_own).astype(jnp.float32)
        s_own = jnp.where(own_dist[None] >= 0,
                          s_own - slopes[:, None, None] * own_dist.astype(jnp.float32)[None], NEG)
        n_past = topk * MOBA_BLOCK
        scores = jnp.concatenate([s_past.reshape(N_HEADS, Q_CHUNK, n_past), s_own], axis=-1)
        p = jax.nn.softmax(scores, axis=-1).astype(v.dtype)
        p_past = p[..., :n_past].reshape(N_HEADS, Q_CHUNK, topk, MOBA_BLOCK)
        p_own = p[..., n_past:]
        return (jnp.einsum('hqjk,hqjkd->hqd', p_past, v_sel)
                + jnp.einsum('hqk,hkd->hqd', p_own, v_own))

    out = lax.map(chunk, jnp.arange(Bsz * n_chunk))
    out = out.reshape(Bsz, n_chunk, N_HEADS, Q_CHUNK, HEAD_DIM).transpose(0, 1, 3, 2, 4)
    out = out.reshape(Bsz, s_pad, ATTN_WIDTH)[:, :S]
    y = out * jax.nn.silu(z)
    return y @ w_out

def second_inputs(seed: int = 0) -> dict:
    key = jax.random.key(seed)
    ks = jax.random.split(key, 10)
    f32 = jnp.float32
    x = jax.random.normal(ks[0], (BATCH, SEQ, D_MODEL), f32)
    norm_g = 1.0 + 0.02 * jax.random.normal(ks[1], (DEPTH, D_MODEL), f32)
    conv_w_in = jax.random.normal(ks[2], (N_CONV_LAYERS, D_MODEL, 4 * CONV_WIDTH), f32) * D_MODEL ** -0.5
    conv_w = jax.random.normal(ks[3], (N_CONV_LAYERS, CONV_K, CONV_WIDTH), f32) * CONV_K ** -0.5
    conv_w_out = jax.random.normal(ks[4], (N_CONV_LAYERS, CONV_WIDTH, D_MODEL), f32) * CONV_WIDTH ** -0.5
    attn_w_in = jax.random.normal(ks[5], (N_ATTN_LAYERS, D_MODEL, 4 * ATTN_WIDTH), f32) * D_MODEL ** -0.5
    q_norm_g = 1.0 + 0.02 * jax.random.normal(ks[6], (N_ATTN_LAYERS, HEAD_DIM), f32)
    k_norm_g = 1.0 + 0.02 * jax.random.normal(ks[7], (N_ATTN_LAYERS, HEAD_DIM), f32)
    attn_w_out = jax.random.normal(ks[8], (N_ATTN_LAYERS, ATTN_WIDTH, D_MODEL), f32) * ATTN_WIDTH ** -0.5
    return {"x": x, "norm_g": norm_g, "conv_w_in": conv_w_in, "conv_w": conv_w,
            "conv_w_out": conv_w_out, "attn_w_in": attn_w_in, "q_norm_g": q_norm_g,
            "k_norm_g": k_norm_g, "attn_w_out": attn_w_out}

def second_block(x, norm_g, conv_w_in, conv_w, conv_w_out, attn_w_in, q_norm_g, k_norm_g, attn_w_out):
    h = x
    for i in range(DEPTH):
        hn = rms_norm_2(h, norm_g[i])
        j = i // N_MIXERS_2
        if i % N_MIXERS_2 == 0:
            h = h + short_conv_mixer(hn, conv_w_in[j], conv_w[j], conv_w_out[j])
        else:
            h = h + moba_mixer(hn, attn_w_in[j], q_norm_g[j], k_norm_g[j], attn_w_out[j])
    return h


def setup_inputs(seed=0):
    out = dict(first_inputs(seed))
    for name, value in second_inputs(seed + 1).items():
        if name != "x":
            out[name + "_2"] = value
    return out


def reference(
    x, p, norm_mix, norm_ffn, ffn_w_in, ffn_w_out, ple_norm, ple_w_gate, ple_w_proj, gla_w_in,
    gla_w_gate_f, gla_b_gate_f, gla_w_gate_b, gla_b_gate_b, gla_g_out, gla_w_out, diff_w_in,
    diff_g_q, diff_g_k, diff_lam_q1, diff_lam_k1, diff_lam_q2, diff_lam_k2, diff_g_sub,
    diff_w_out, ssd_w_in, ssd_conv_w, ssd_conv_b, ssd_dt_bias_f, ssd_a_log_f, ssd_dt_bias_b,
    ssd_a_log_b, ssd_d, ssd_g_norm, ssd_w_out, dil_w_in, dil_g_q, dil_g_k, dil_w_out, norm_g_2,
    conv_w_in_2, conv_w_2, conv_w_out_2, attn_w_in_2, q_norm_g_2, k_norm_g_2, attn_w_out_2,
):
    x = first_block(
        x, p, norm_mix, norm_ffn, ffn_w_in, ffn_w_out, ple_norm, ple_w_gate, ple_w_proj,
        gla_w_in, gla_w_gate_f, gla_b_gate_f, gla_w_gate_b, gla_b_gate_b, gla_g_out, gla_w_out,
        diff_w_in, diff_g_q, diff_g_k, diff_lam_q1, diff_lam_k1, diff_lam_q2, diff_lam_k2,
        diff_g_sub, diff_w_out, ssd_w_in, ssd_conv_w, ssd_conv_b, ssd_dt_bias_f, ssd_a_log_f,
        ssd_dt_bias_b, ssd_a_log_b, ssd_d, ssd_g_norm, ssd_w_out, dil_w_in, dil_g_q, dil_g_k,
        dil_w_out,
    )
    return second_block(
        x, norm_g_2, conv_w_in_2, conv_w_2, conv_w_out_2, attn_w_in_2, q_norm_g_2, k_norm_g_2,
        attn_w_out_2,
    )


_drawn_inputs = setup_inputs


def setup_inputs(seed=0):
    import zlib

    import numpy as np

    out = dict(_drawn_inputs(seed))
    spreads = {}
    factors = {'ple_norm': 4.369,
     'gla_b_gate_f': 8.0,
     'gla_b_gate_b': 8.0,
     'diff_lam_q1': 4.683,
     'diff_lam_k1': 6.922,
     'diff_lam_q2': 3.745,
     'diff_lam_k2': 6.36,
     'norm_g_2': 4.069,
     'q_norm_g_2': 8.0,
     'k_norm_g_2': 8.0}
    for name, (base, spread) in spreads.items():
        noise = np.random.default_rng([zlib.crc32(name.encode()), seed]).standard_normal(out[name].shape)
        drawn = base * np.exp(spread * noise) if base else spread * noise
        out[name] = jnp.asarray(drawn.astype(out[name].dtype))
    for name, factor in factors.items():
        out[name] = (out[name] * factor).astype(out[name].dtype)
    return out
```

```python
import math
from contextlib import ExitStack

import numpy as np

import concourse.bass as bass
from concourse import mybir
from concourse.alu_op_type import AluOpType as ALU

F32 = mybir.dt.float32
F32R = mybir.dt.float32r
U32 = mybir.dt.uint32
ACT = mybir.ActivationFunctionType
AXX = mybir.AxisListType.X

P = 128
SEQ, D = 256, 1024
TT = SEQ // P
KT = D // P
NW = 512
EPS = 1e-6
FF = (-((-8 * D) // 3) + 255) // 256 * 256
FKT = FF // P
FT = FF // 256
PLE = 256
HALF = D // 2

GLA_H, GLA_HK, GLA_HV, GLA_C, GLA_R = 4, 128, 256, 64, 16
GLA_K = GLA_H * GLA_HK
DF_H, DF_HD = 8, 64
LAMBDA_INIT = 0.8 - 0.6 * math.exp(-0.3)
MB_H, MB_HD = 16, 64
CONV_K = 3

TILES = [1] + [KT // 2] * 6 + [KT // 2] * 2 + [KT // 2] * FT + [FKT // 2] * 2 + [KT // 2, 1] * 2
GLA_IN, GLA_OUT, FFN_IN0 = 0, 7, 9
FFN_OUT0 = FFN_IN0 + FT
PLE0 = FFN_OUT0 + 2
DF_IN = PLE0 + 4
TILES += [KT // 2] * 8 + [KT // 2] * FT + [FKT // 2] * 2 + [KT // 2, 1] * 2
DF_OUT = DF_IN + 6
FFN_IN1 = DF_OUT + 2
FFN_OUT1 = FFN_IN1 + FT
PLE1 = FFN_OUT1 + 2
CV_IN = PLE1 + 4
TILES += [KT // 2] * 10
CV_OUT = CV_IN + 8
MB_IN = CV_OUT + 2
TILES += [KT // 2] * 10
MB_OUT = MB_IN + 8
END = [0]
for _n in TILES:
    END.append(END[-1] + _n)
UNITS = END[-1]
RAW, RING = 4, 8
AHEAD = 6

C_NORM, C_GLA, C_DF, C_QG, C_KG, C_CONV, N_COLS = 0, 64, 66, 67, 68, 69, 69 + KT * CONV_K
K_ID, K_TRI, K_MASK, K_COS, K_SIN, K_DIST, N_CONST = 0, 128, 384, 640, 768, 896, 896 + 384
R_GQ, R_GK, R_LAM, N_ROWS = 0, 128, 256, 512

T_BANKS = (4, 5, 6, 7)


class Count:

    def __init__(self, sem):
        self.sem, self.value, self.turn, self.rate = sem, {}, None, {}

    def up(self, name, by=1):
        self.value[name] = self.value.get(name, 0) + by
        return self.value[name]

    def wait(self, eng, name, value):
        if self.turn is not None:
            eng.wait_ge(self.sem(name), self.turn * self.rate[name] + value)
        elif value > 0:
            eng.wait_ge(self.sem(name), value)

    def enter(self, turn, rate):
        self.turn, self.rate, self.before = turn, rate, dict(self.value)

    def leave(self, turns):
        for name, value in self.value.items():
            step = value - self.before.get(name, 0)
            assert step in (0, self.rate.get(name, 0)), (name, step)
            self.value[name] = value + step * (turns - 1)
        self.turn = None


def build(nc, stream, x, p, cols_d, rows_d, consts_d, wgate_d, out):
    ctx = ExitStack()
    with ctx:
        def sb(name, shape, dt=F32, scope=ctx):
            return scope.enter_context(nc.sbuf_tensor(name, shape, dt))

        sems = {}

        def sem(name):
            if name not in sems:
                sems[name] = ctx.enter_context(nc.semaphore(name))
            return sems[name]

        bank = [ctx.enter_context(nc.psum_tensor(f"bank{b}", [P, NW], F32)) for b in range(8)]

        raw = sb("raw", [P, RAW, 2 * NW])
        whi = sb("whi", [P, RING, 2 * NW], F32R)
        wlo = sb("wlo", [P, RING, 2 * NW], F32R)
        h = sb("h", [P, TT, D])
        X = (sb("x_hi", [P, KT, SEQ], F32R), sb("x_lo", [P, KT, SEQ], F32R))
        Y = (sb("y_hi", [P, KT, SEQ], F32R), sb("y_lo", [P, KT, SEQ], F32R))
        PT = (sb("p_hi", [P, 2, SEQ], F32R), sb("p_lo", [P, 2, SEQ], F32R))
        p_tok = sb("p_tok", [P, 2, TT, PLE])
        cols = sb("cols", [P, N_COLS])
        consts = sb("consts", [P, N_CONST])
        rows = sb("rows", [P, N_ROWS])
        junk = sb("junk", [P, NW])
        stats = sb("stats", [P, 8, 2, TT])
        ms = sb("ms", [P, 8, 2, TT])
        rstd = sb("rstd", [P, 8, TT])
        neg_half = sb("neg_half", [P, 16])
        rstd_q = sb("rstd_q", [P, TT])
        ident = consts[:, K_ID:K_ID + P]

        def phase():
            return ExitStack()

        s = phase()
        qk_tok = sb("gla_qk_tok", [P, 2, TT, GLA_K], scope=s)
        la = sb("gla_log_a", [P, TT, 2 * GLA_K], scope=s)
        qkT = sb("gla_qkT", [P, 2, GLA_H * SEQ], scope=s)
        qE = sb("gla_qE", [P, 2, GLA_H * SEQ], scope=s)
        kE = sb("gla_kE", [P, 2, GLA_H * SEQ], scope=s)
        gv = sb("gla_v", [P, TT, D], scope=s)
        gr = sb("gla_r", [P, TT, D], scope=s)
        gtmp = sb("gla_tmp", [P, 4, NW], scope=s)
        wg = sb("gla_wgate", [33, 2 * GLA_K], scope=s)
        zt = sb("gla_z_tok", [P, TT, 2 * GLA_R], scope=s)
        zT = sb("gla_zT", [33, SEQ], scope=s)
        decay = sb("gla_decay", [P, 2, GLA_H * 4], scope=s)
        oss = sb("gla_oss", [P, 3, TT * GLA_H], scope=s)
        s.close()
        kD = qk_tok[:, :, :, :].rearrange("p a t n -> p a (t n)")
        kDt = la[:, :, :].rearrange("p t n -> p (t n)").rearrange("p (d t n) -> p d t n", d=2, t=TT)
        probs = qkT[:, 0, :].rearrange("p (t n) -> p t n", t=TT)
        st_even = kE[:, :, :].rearrange("p a n -> p (a n)").rearrange("p (s n) -> p s n", n=GLA_HV)
        st_odd = gtmp[:, :, :].rearrange("p a n -> p (a n)").rearrange("p (s n) -> p s n", n=GLA_HV)
        states = (st_even, st_odd)
        grown = gtmp[:, :, :].rearrange("p (e a) n -> p e (a n)", e=2)

        s = phase()
        M = (sb("mid_hi", [P, FKT, SEQ], F32R, scope=s), sb("mid_lo", [P, FKT, SEQ], F32R, scope=s))
        sg = sb("ffn_silu", [P, 2, TT, 256], scope=s)
        mid = sb("ffn_mid", [P, 2, TT, 256], scope=s)
        s.close()

        s = phase()
        sig = sb("ple_gate", [P, TT, NW], scope=s)
        gated = sb("ple_gated", [P, TT, NW], scope=s)
        s.close()

        s = phase()
        dtok = sb("df_tok", [P, 2, TT, NW], scope=s)
        dsq = sb("df_sq", [P, TT, NW], scope=s)
        dm2 = sb("df_m2", [P, TT, NW], scope=s)
        dT = sb("df_qkT", [P, 2, DF_H, SEQ], scope=s)
        dv = sb("df_v", [P, TT, D], scope=s)
        do = sb("df_o", [P, TT, D], scope=s)
        rot = sb("df_rot", [P, 2, 2, TT, P], scope=s)
        dss = sb("df_ss", [P, 3, TT * 8], scope=s)
        dstat = sb("df_stat", [P, 2, 16], scope=s)
        lam = sb("df_lam", [P, 8], scope=s)
        s.close()
        dp = dtok[:, :, :, :].rearrange("p a t n -> p (a t n)").rearrange("p (b c q k) -> p b c q k", b=2, c=2, q=TT)
        da = dsq[:, :, :].rearrange("p b (q k) -> p b q k", q=TT)
        daT = dm2

        s = phase()
        cact = sb("cv_act", [P, 2, TT, 2, P], scope=s)
        cprod = sb("cv_prod", [P, 2, TT, 2, P], scope=s)
        cu = sb("cv_u", [P, 2, SEQ + CONV_K - 1], scope=s)
        cc = sb("cv_c", [P, 4, SEQ], scope=s)
        s.close()

        s = phase()
        mtok = sb("mb_tok", [P, 2, TT, NW], scope=s)
        msq = sb("mb_sq", [P, TT, NW], scope=s)
        mT = sb("mb_qkT", [P, 2, KT, SEQ], scope=s)
        mv = sb("mb_v", [P, TT, D], scope=s)
        mz = sb("mb_z", [P, TT, D], scope=s)
        mgain = sb("mb_gain", [P, 2], scope=s)
        mss = sb("mb_ss", [P, 3, TT * 8], scope=s)
        mstat = sb("mb_stat", [P, 2, 4], scope=s)
        msum = sb("mb_sum", [P, TT, MB_H], scope=s)
        mrec = sb("mb_rec", [P, TT, MB_H], scope=s)
        mo = sb("mb_o", [P, TT, NW], scope=s)
        mpT = sb("mb_pT", [P, 2, 3 * P], scope=s)
        s.close()
        ms2 = mtok[:, :, :, :].rearrange("p a t n -> p (a t) n")
        mp = ms2

        block = ctx.enter_context(nc.Block())

        def layer(n):
            return (FFN_IN0, FFN_OUT0, PLE0) if n == 0 else (FFN_IN1, FFN_OUT1, PLE1)

        @block.sync
        def _(sp):
            sp.dma_start(h[:, :, :], x.rearrange("(t p) d -> p t d", p=P)).then_inc(sem("x_in"), 16)
            sp.dma_start(consts[:, :], consts_d).then_inc(sem("consts_in"), 16)
            sp.dma_start(cols[:, :], cols_d).then_inc(sem("cols_in"), 16)
            for u in range(RAW):
                sp.dma_start(raw[:, u, :], stream[u]).then_inc(sem(f"raw{u}"), 16)
            sp.dma_start(wg[:, :], wgate_d).then_inc(sem("wg_in"), 16)
            sp.dma_start(p_tok[:, :, :, :], p.rearrange("l (t p) d -> p l t d", p=P)).then_inc(sem("p_in"), 16)
            sp.dma_start(rows[:, :], rows_d.to_broadcast([P, N_ROWS])).then_inc(sem("rows_in"), 16)
            with sp.Fori(1, UNITS // RAW) as i:
                for u in range(RAW):
                    sp.wait_ge(sem("w_lo"), i * RAW + (u - RAW + 1))
                    sp.dma_start(raw[:, u, :], stream[i * RAW + u]).then_inc(sem(f"raw{u}"), 16)
            for n in range(UNITS // RAW * RAW, UNITS):
                sp.wait_ge(sem("w_lo"), n - RAW + 1)
                sp.dma_start(raw[:, n % RAW, :], stream[n]).then_inc(sem(f"raw{n % RAW}"), 16)
            for half in range(2):
                sp.wait_ge(sem("h_new"), 28 + 2 * (half + 1))
                sp.dma_start(out.rearrange("(t p) d -> p t d", p=P)[:, :, half * HALF:(half + 1) * HALF],
                             h[:, :, half * HALF:(half + 1) * HALF]).then_inc(sem("out_done"), 16)
            sp.wait_ge(sem("out_done"), 32)

        @block.gpsimd
        def _(pool):
            c = Count(sem)

            def power(src, mean, dst, n, scale, gain=None):
                nc.gpsimd.tensor_scalar(mean, src, scale, EPS, ALU.mult, ALU.add).then_inc(sem("pool_step"), 1)
                c.wait(pool, "pool_step", c.up("pool_step"))
                last = nc.gpsimd.tensor_tensor(dst, mean, neg_half[:, 0:n], ALU.pow)
                if gain is not None:
                    last.then_inc(sem("pool_step"), 1)
                    c.wait(pool, "pool_step", c.up("pool_step"))
                    last = nc.gpsimd.tensor_scalar(dst, dst, gain, None, ALU.mult)
                return last

            def row_norm(j):
                pool.wait_ge(sem("stats"), 4 * (j + 1))
                nc.gpsimd.tensor_tensor(ms[:, j, 0, :], stats[:, j, 0, :], stats[:, j, 1, :], ALU.add)\
                    .then_inc(sem("pool_step"), 1)
                c.wait(pool, "pool_step", c.up("pool_step"))
                power(ms[:, j, 0, :], ms[:, j, 1, :], rstd[:, j, :], TT, 1.0 / D).then_inc(sem("rstd"), 1)

            nc.gpsimd.memset(neg_half[:, :], -0.5).then_inc(sem("pool_step"), 1)
            c.wait(pool, "pool_step", c.up("pool_step"))
            row_norm(0)
            pool.wait_ge(sem("rstd"), 1)
            nc.gpsimd.tensor_scalar(rstd_q[:, :], rstd[:, 0, :], GLA_HK ** -0.5, None, ALU.mult)\
                .then_inc(sem("rstd_q"), 1)
            pool.wait_ge(sem("gla_sq"), TT * GLA_H)
            power(oss[:, 0, :], oss[:, 1, :], oss[:, 2, :], TT * GLA_H, 1.0 / GLA_HV).then_inc(sem("gla_rstd"), 1)
            for j in (1, 2, 3):
                row_norm(j)
            for t in range(4):
                pool.wait_ge(sem("df_ss"), TT * (t + 1))
                power(dss[:, 0, :], dss[:, 1, :], dss[:, 2, :], TT * 8, 1.0 / DF_HD).then_inc(sem("df_rstd"), 1)
            for g in range(2):
                pool.wait_ge(sem("df_oss"), TT * (g + 1))
                power(dss[:, 0, 0:8], dss[:, 1, 0:8], dss[:, 2, 0:8], 8, 1.0 / (2 * DF_HD), 1.0 - LAMBDA_INIT)\
                    .then_inc(sem("df_orstd"), 1)
            for j in (4, 5, 6, 7):
                row_norm(j)
            for t in range(4):
                pool.wait_ge(sem("mb_ss"), TT * (t + 1))
                power(mss[:, 0, :], mss[:, 1, :], mss[:, 2, :], TT * 8, 1.0 / MB_HD).then_inc(sem("mb_rstd"), 1)

        @block.scalar
        def _(act):
            c = Count(sem)
            pos = [0]
            A = nc.scalar.activation

            def split_to(end):
                for u in range(pos[0], min(end, UNITS)):
                    c.wait(act, f"raw{u % RAW}", 16 * (u // RAW + 1))
                    if u >= RING:
                        c.wait(act, "w_used", u - RING + 1)
                    w = 256 if u == 0 else 2 * NW
                    A(whi[:, u % RING, 0:w], raw[:, u % RAW, 0:w], ACT.Copy).then_inc(sem("w_hi"), 1)
                pos[0] = max(pos[0], min(end, UNITS))

            def lhs_hi(dst, gain, banks):
                for b in banks:
                    c.wait(act, "lhs_filled", c.up("lhs_filled"))
                    kt = 2 * (b - T_BANKS[0])
                    for k in range(2):
                        scale = 1.0 if gain is None else gain(kt + k)
                        last = A(dst[0][:, kt + k, :], bank[b][:, k * SEQ:(k + 1) * SEQ], ACT.Copy, scale=scale)
                    last.then_inc(sem("lhs_hi"), 1)

            def norm_gain(j):
                return lambda kt: cols[:, C_NORM + j * KT + kt:C_NORM + j * KT + kt + 1]

            def squares(j, half):
                if j:
                    act.wait_ge(sem("h_new"), 4 * (j - 1) + 2 * (half + 1))
                for t in range(TT):
                    c.wait(act, "stats", c.value.get("stats", 0))
                    A(junk[:, :], h[:, t, half * HALF:(half + 1) * HALF], ACT.Square,
                      accum_out=stats[:, j, half, t:t + 1]).then_inc(sem("stats"), 1)
                    c.up("stats")

            def next_lhs(j, dst, tile):
                first = tile + 1
                split_to(END[first] + 2 + AHEAD)
                lhs_hi(dst, norm_gain(j), (4, 5))
                squares(j, 0)
                split_to(END[first + 1] + 1 + AHEAD)
                lhs_hi(dst, norm_gain(j), (6, 7))
                squares(j, 1)

            def evacuate(tile, j, dst, width, signal, func=ACT.Copy, scale=None):
                split_to(END[tile + 1] + AHEAD)
                act.wait_ge(sem("rstd"), j + 1)
                c.wait(act, "w_used", END[tile + 1])
                for t in range(TT):
                    A(dst(t), bank[2 * (tile % 2) + t][:, 0:width], func,
                      scale=(scale if scale is not None else rstd[:, j, :])[:, t:t + 1]).then_inc(sem(signal), 1)

            act.wait_ge(sem("cols_in"), 16)
            act.wait_ge(sem("x_in"), 16)
            lhs_hi(X, norm_gain(0), (4, 5, 6, 7))
            squares(0, 0)
            squares(0, 1)

            evacuate(GLA_IN, 0, lambda t: zt[:, t, :], 2 * GLA_R, "gla_in")
            act.wait_ge(sem("rstd_q"), 1)
            evacuate(GLA_IN + 1, 0, lambda t: qk_tok[:, 0, t, :], NW, "gla_in", scale=rstd_q)
            evacuate(GLA_IN + 2, 0, lambda t: qk_tok[:, 1, t, :], NW, "gla_in")
            for g in range(4):
                act.wait_ge(sem("gla_pre"), g + 1)
                A(gtmp[:, g, :], bank[T_BANKS[g]][:, :], ACT.Abs).then_inc(sem("gla_abs"), 1)
            for g in range(4):
                act.wait_ge(sem("gla_abs"), g + 1)
                A(gtmp[:, g, :], gtmp[:, g, :], ACT.Exp, scale=-1.0).then_inc(sem("gla_expabs"), 1)
            for g in range(4):
                act.wait_ge(sem("gla_expabs"), g + 1)
                A(gtmp[:, g, :], gtmp[:, g, :], ACT.Ln, bias=1.0).then_inc(sem("gla_ln"), 1)
            evacuate(GLA_IN + 3, 0, lambda t: gv[:, t, 0:NW], NW, "gla_in")
            for g in range(4):
                act.wait_ge(sem("gla_qkT_filled"), g + 1)
                A(qkT[:, g // 2, (g % 2) * NW:(g % 2 + 1) * NW], bank[T_BANKS[g]][:, :], ACT.Copy)\
                    .then_inc(sem("gla_qkT"), 1)
            evacuate(GLA_IN + 4, 0, lambda t: gv[:, t, NW:2 * NW], NW, "gla_in")
            for g in range(4):
                act.wait_ge(sem("gla_cum"), g + 1)
                if g == 2:
                    act.wait_ge(sem("gla_gated"), 4)
                for e, sign in enumerate((1.0, -1.0)):
                    A(grown[:, e, (g % 2) * NW:(g % 2 + 1) * NW], bank[T_BANKS[g]][:, :], ACT.Exp, scale=sign)\
                        .then_inc(sem("gla_exp"), 1)
            evacuate(GLA_IN + 5, 0, lambda t: gr[:, t, 0:NW], NW, "gla_in", func=ACT.Silu)
            for g in range(4):
                act.wait_ge(sem("gla_kDt_filled"), g + 1)
                A(kDt[:, g // 2, g % 2, :], bank[T_BANKS[g]][:, :], ACT.Copy).then_inc(sem("gla_kDt"), 1)
            evacuate(GLA_IN + 6, 0, lambda t: gr[:, t, NW:2 * NW], NW, "gla_in", func=ACT.Silu)
            for g in range(4):
                act.wait_ge(sem("gla_head"), 2 * (g // 2) + 2)
                for k in range(2):
                    c.wait(act, "gla_sq", c.value.get("gla_sq", 0))
                    hd = 2 * (g // 2) + k
                    A(junk[:, 0:GLA_HV], bank[2 * (g % 2) + g // 2][:, k * GLA_HV:(k + 1) * GLA_HV], ACT.Square,
                      accum_out=oss[:, 0, (g % 2) * GLA_H + hd:(g % 2) * GLA_H + hd + 1]).then_inc(sem("gla_sq"), 1)
                    c.up("gla_sq")
            lhs_hi(Y, lambda kt: cols[:, C_GLA + kt % 2:C_GLA + kt % 2 + 1], T_BANKS)

            def ffn(n, src):
                tin, tout, tple = layer(n)
                j = 3 * n + 1
                next_lhs(j, src, tin - 2)

                def tile(t):
                    split_to(END[t + 1] + AHEAD)
                    c.wait(act, "w_used", END[t + 1])
                    for k in range(TT):
                        A(sg[:, (t - tin) % 2, k, :], bank[2 * (t % 2) + k][:, 0:256], ACT.Silu,
                          scale=rstd[:, j, k:k + 1]).then_inc(sem("ffn_silu"), 1)
                        c.up("ffn_silu")

                act.wait_ge(sem("rstd"), j + 1)
                for t in range(tin, tin + 3):
                    tile(t)
                turns = (FT - 5) // 2
                with act.Fori(0, turns) as i:
                    c.enter(i, {"w_used": 8, "w_hi": 8, "ffn_silu": 4, **{f"raw{r}": 32 for r in range(RAW)}})
                    tile(tin + 3)
                    tile(tin + 4)
                    c.leave(turns)
                pos[0] += 8 * (turns - 1)
                for t in range(tin + 3 + 2 * turns, tin + FT):
                    tile(t)
                split_to(END[tout] + 5 + AHEAD)
                act.wait_ge(sem("pT_filled"), n + 1)
                A(PT[0][:, :, :], bank[6][:, :].rearrange("p (k s) -> p k s", k=2), ACT.Copy)\
                    .then_inc(sem("pT_hi"), 1)
                j += 1
                split_to(END[tout + 1] + 2 + AHEAD)
                lhs_hi(src, norm_gain(j), (4, 5))
                squares(j, 0)
                split_to(END[tple] + 1 + AHEAD)
                lhs_hi(src, norm_gain(j), (6, 7))
                squares(j, 1)
                act.wait_ge(sem("rstd"), j + 1)
                for half in range(2):
                    t = tple + 2 * half
                    split_to(END[t + 1] + AHEAD)
                    c.wait(act, "w_used", END[t + 1])
                    if half:
                        act.wait_ge(sem("ple_gated"), TT * (2 * n + 1))
                    for k in range(TT):
                        A(sig[:, k, :], bank[2 * (t % 2) + k][:, :], ACT.Sigmoid, scale=rstd[:, j, k:k + 1])\
                            .then_inc(sem("ple_sig"), 1)
                    if half == 0:
                        split_to(END[t + 2] + 2 + AHEAD)
                        lhs_hi(Y if src is X else X, norm_gain(j + 1), (4, 5))
                        squares(j + 1, 0)
                split_to(END[tple + 4] + 1 + AHEAD)
                lhs_hi(Y if src is X else X, norm_gain(j + 1), (6, 7))
                squares(j + 1, 1)

            ffn(0, X)

            for t in range(6):
                dst = (lambda k, t=t: dtok[:, t % 2, k, :]) if t < 4 else \
                    (lambda k, t=t: dv[:, k, (t - 4) * NW:(t - 3) * NW])
                split_to(END[DF_IN + t] + 1 + AHEAD)
                if 2 <= t < 4:
                    act.wait_ge(sem("df_T_filled"), 2 * (t - 1))
                if t >= 2:
                    for b in range(2):
                        g = 2 * (t - 2) + b
                        act.wait_ge(sem("df_T_filled"), g + 1)
                        hd = 4 * ((t - 2) % 2) + 2 * b
                        A(dT[:, (t - 2) // 2, hd:hd + 2, :],
                          bank[T_BANKS[g % 4]][:, :].rearrange("p (a s) -> p a s", a=2), ACT.Copy)\
                            .then_inc(sem("df_T"), 1)
                evacuate(DF_IN + t, 3, dst, NW, "df_in")
                if t < 4:
                    if t:
                        act.wait_ge(sem("df_ss"), TT * t)
                    act.wait_ge(sem("df_in"), TT * (t + 1))
                    for k in range(TT):
                        A(dsq[:, k, :], dtok[:, t % 2, k, :], ACT.Square).then_inc(sem("df_sq"), 1)

            def df_exp(hd):
                act.wait_ge(sem("df_max"), 3 * (hd + 1))
                if hd >= 2:
                    act.wait_ge(sem("df_a"), 2 * (hd - 1))
                for m in range(2):
                    for q in range(TT):
                        A(dp[:, hd % 2, m, q, :], bank[T_BANKS[2 * (hd % 2) + m]][:, q * SEQ:(q + 1) * SEQ], ACT.Exp,
                          scale=DF_HD ** -0.5, bias=dstat[:, hd % 2, 4 + 2 * m + q:5 + 2 * m + q],
                          accum_out=dstat[:, hd % 2, 8 + 2 * m + q:9 + 2 * m + q]).then_inc(sem("df_exp"), 1)

            def df_copy(hd):
                act.wait_ge(sem("df_aT_filled"), hd + 1)
                if hd >= 2:
                    act.wait_ge(sem("df_av"), hd - 1)
                A(daT[:, hd % 2, :], bank[hd % 2][:, :], ACT.Copy).then_inc(sem("df_aT"), 1)

            act.wait_ge(sem("df_lam"), 2)
            A(lam[:, 2:4], lam[:, 0:2], ACT.Exp).then_inc(sem("df_lamexp"), 1)
            df_exp(0)
            for hd in range(DF_H):
                if hd + 1 < DF_H:
                    df_exp(hd + 1)
                df_copy(hd)
                if hd % 4 == 3:
                    act.wait_ge(sem("df_av"), hd + 1)
                    g = hd // 4
                    for q in range(TT):
                        A(do[:, q, g * NW:(g + 1) * NW], bank[2 + q][:, :], ACT.Copy).then_inc(sem("df_o"), 1)
            for g in range(2):
                act.wait_ge(sem("df_a"), 2 * DF_H)
                act.wait_ge(sem("df_o"), TT * (g + 1))
                if g:
                    act.wait_ge(sem("df_oss"), TT * g)
                for q in range(TT):
                    A(dsq[:, q, :], do[:, q, g * NW:(g + 1) * NW], ACT.Square).then_inc(sem("df_osq"), 1)
            lhs_hi(X, lambda kt: cols[:, C_DF:C_DF + 1], T_BANKS)
            ffn(1, Y)

            def conv_tile(t):
                split_to(END[t + 1] + AHEAD)
                c.wait(act, "w_used", END[t + 1])
                for k in range(TT):
                    A(cact[:, (t - CV_IN) % 2, k, 0, :], bank[2 * (t % 2) + k][:, 2 * P:3 * P], ACT.Copy,
                      scale=rstd[:, 6, k:k + 1])
                    A(cact[:, (t - CV_IN) % 2, k, 1, :], bank[2 * (t % 2) + k][:, 3 * P:4 * P], ACT.Silu,
                      scale=rstd[:, 6, k:k + 1]).then_inc(sem("cv_act"), 1)
                    c.up("cv_act")

            act.wait_ge(sem("rstd"), 7)
            for t in range(CV_IN, CV_IN + 3):
                conv_tile(t)
            with act.Fori(0, 2) as i:
                c.enter(i, {"w_used": 8, "w_hi": 8, "cv_act": 4, **{f"raw{r}": 32 for r in range(RAW)}})
                conv_tile(CV_IN + 3)
                conv_tile(CV_IN + 4)
                c.leave(2)
            pos[0] += 8
            conv_tile(CV_IN + 7)
            next_lhs(7, X, CV_OUT)

            for t in range(8):
                split_to(END[MB_IN + t] + 1 + AHEAD)
                if 2 <= t < 6:
                    which = (t - 2) // 2
                    for b in range(2):
                        g = 2 * (t - 2) + b
                        act.wait_ge(sem("mb_T_filled"), g + 1)
                        if g == 0:
                            act.wait_ge(sem("mb_gain"), 1)
                        blk = 4 * ((t - 2) % 2) + 2 * b
                        A(mT[:, which, blk:blk + 2, :],
                          bank[T_BANKS[g % 4]][:, :].rearrange("p (a s) -> p a s", a=2), ACT.Copy,
                          scale=mgain[:, which:which + 1]).then_inc(sem("mb_T"), 1)
                func = ACT.Silu if t >= 6 else ACT.Copy
                dst = (lambda k, t=t: mtok[:, t % 2, k, :]) if t < 4 else \
                    (lambda k, t=t: (mv if t < 6 else mz)[:, k, (t % 2) * NW:(t % 2 + 1) * NW])
                evacuate(MB_IN + t, 7, dst, NW, "mb_in", func=func)
                if t < 4:
                    if t:
                        act.wait_ge(sem("mb_ss"), TT * t)
                    act.wait_ge(sem("mb_in"), TT * (t + 1))
                    for k in range(TT):
                        A(msq[:, k, :], mtok[:, t % 2, k, :], ACT.Square).then_inc(sem("mb_sq"), 1)

            def mb_exp(hd):
                act.wait_ge(sem("mb_max"), hd + 1)
                if hd >= 2:
                    act.wait_ge(sem("mb_pT_filled"), hd - 1)
                for q in range(TT):
                    lo, hi = (0, P) if q == 0 else (P, 3 * P)
                    A(mp[:, 2 + hd % 2, lo:hi], ms2[:, hd % 2, lo:hi], ACT.Exp, bias=mstat[:, hd % 2, 2 + q:3 + q],
                      accum_out=msum[:, q, hd:hd + 1]).then_inc(sem("mb_exp"), 1)

            def mb_copy(hd):
                act.wait_ge(sem("mb_pT_filled"), hd + 1)
                if hd >= 2:
                    act.wait_ge(sem("mb_av"), hd - 1)
                A(mpT[:, hd % 2, :], bank[hd % 2][:, 0:3 * P], ACT.Copy).then_inc(sem("mb_pT"), 1)

            mb_exp(0)
            for hd in range(MB_H):
                if hd + 1 < MB_H:
                    mb_exp(hd + 1)
                mb_copy(hd)
            lhs_hi(Y, None, T_BANKS)
            split_to(UNITS)

        @block.vector
        def _(dve):
            c = Count(sem)
            pos = [0]
            V = nc.vector

            def split_to(end):
                for u in range(pos[0], min(end, UNITS)):
                    c.wait(dve, "w_hi", u + 1)
                    w = 256 if u == 0 else 2 * NW
                    V.tensor_tensor(wlo[:, u % RING, 0:w], raw[:, u % RAW, 0:w],
                                    whi[:, u % RING, 0:w].bitcast(F32), ALU.subtract).then_inc(sem("w_lo"), 1)
                pos[0] = max(pos[0], min(end, UNITS))

            def lhs_lo(dst, gain, banks):
                for b in banks:
                    c.wait(dve, "lhs_hi", c.up("lhs_hi"))
                    kt = 2 * (b - T_BANKS[0])
                    if gain is None:
                        V.tensor_tensor(dst[1][:, kt:kt + 2, :], bank[b][:, :].rearrange("p (k s) -> p k s", k=2),
                                        dst[0][:, kt:kt + 2, :].bitcast(F32), ALU.subtract)\
                            .then_inc(sem("lhs"), 1)
                        continue
                    for k in range(2):
                        last = V.scalar_tensor_tensor(dst[1][:, kt + k, :], bank[b][:, k * SEQ:(k + 1) * SEQ],
                                                      gain(kt + k), dst[0][:, kt + k, :].bitcast(F32),
                                                      ALU.mult, ALU.subtract)
                    last.then_inc(sem("lhs"), 1)

            def norm_gain(j):
                return lambda kt: cols[:, C_NORM + j * KT + kt:C_NORM + j * KT + kt + 1]

            def residual(tile, half):
                split_to(END[tile + 1] + AHEAD - 2)
                c.wait(dve, "w_used", END[tile + 1])
                for t in range(TT):
                    V.tensor_tensor(h[:, t, half * HALF:(half + 1) * HALF], h[:, t, half * HALF:(half + 1) * HALF],
                                    bank[2 * (tile % 2) + t][:, :], ALU.add).then_inc(sem("h_new"), 1)

            def mixer_out(tile, j, dst):
                residual(tile, 0)
                split_to(END[tile + 1] + 2 + AHEAD)
                lhs_lo(dst, norm_gain(j), (4, 5))
                residual(tile + 1, 1)
                split_to(END[tile + 2] + 1 + AHEAD)
                lhs_lo(dst, norm_gain(j), (6, 7))

            dve.wait_ge(sem("cols_in"), 16)
            lhs_lo(X, norm_gain(0), T_BANKS)
            V.memset(zT[32:33, :], 1.0).then_inc(sem("gla_ones"), 1)

            split_to(END[2] + AHEAD)
            dve.wait_ge(sem("gla_zT_filled"), 1)
            V.tensor_copy(zT[0:32, :], bank[4][0:32, 0:SEQ]).then_inc(sem("gla_zT"), 1)
            split_to(END[3] + AHEAD)
            for g in range(4):
                dve.wait_ge(sem("gla_ln"), g + 1)
                V.scalar_tensor_tensor(la[:, g % 2, (g // 2) * GLA_K:(g // 2 + 1) * GLA_K], bank[T_BANKS[g]][:, :],
                                       0.0, gtmp[:, g, :], ALU.min, ALU.subtract).then_inc(sem("gla_la"), 1)
            split_to(END[5] + AHEAD)
            dve.wait_ge(sem("gla_qkT"), 4)
            for d in range(2):
                dve.wait_ge(sem("gla_exp"), 4 * (d + 1))
                V.tensor_tensor(qE[:, d, :], qkT[:, 0, :], grown[:, 0, :], ALU.mult).then_inc(sem("gla_gated"), 1)
                V.tensor_tensor(kE[:, d, :], qkT[:, 1, :], grown[:, 1, :], ALU.mult).then_inc(sem("gla_gated"), 1)
                edge = GLA_C - 1 if d == 0 else 0
                V.tensor_copy(decay[:, d, :], grown[:, 0, :].rearrange("p (a i) -> p a i", i=GLA_C)[:, :, edge])\
                    .then_inc(sem("gla_gated"), 1)
                dve.wait_ge(sem("gla_gated"), 4 * d + 3)
                V.tensor_tensor(kD[:, d, :].rearrange("p (a i) -> p a i", i=GLA_C),
                                kE[:, d, :].rearrange("p (a i) -> p a i", i=GLA_C),
                                decay[:, d, :].unsqueeze(2).to_broadcast([P, GLA_H * 4, GLA_C]), ALU.mult)\
                    .then_inc(sem("gla_gated"), 1)
            V.memset(probs, 0.0).then_inc(sem("gla_zero"), 1)
            split_to(END[7] + AHEAD - 2)
            dve.wait_ge(sem("gla_zero"), 1)
            for g in range(4):
                dve.wait_ge(sem("gla_scores"), g + 1)
                if g >= 2:
                    dve.wait_ge(sem("gla_probs"), g - 1)
                d, t = divmod(g, 2)
                mask = consts[:, K_MASK + d * P:K_MASK + (d + 1) * P].bitcast(U32).unsqueeze(1)\
                    .to_broadcast([P, GLA_H, P])
                V.copy_predicated(probs[:, t, :].rearrange("p (a i) -> p a i", a=GLA_H), mask,
                                  bank[T_BANKS[g]][:, :].rearrange("p (a i) -> p a i", a=GLA_H))\
                    .then_inc(sem("gla_probs"), 1)
            for hd in range(GLA_H):
                st = states[hd % 2]

                def dec(d, ch, hd=hd):
                    return decay[:, d, hd * 4 + ch:hd * 4 + ch + 1]
                base = 6 * hd
                dve.wait_ge(sem("gla_u"), 4 * (hd + 1))
                if hd >= 2:
                    dve.wait_ge(sem("gla_head"), hd - 1)
                V.tensor_copy(st[:, 0, :], bank[4][:, 0:256]).then_inc(sem("gla_state"), 1)
                V.tensor_copy(st[:, 3, :], bank[7][:, 0:256]).then_inc(sem("gla_state"), 1)
                dve.wait_ge(sem("gla_state"), base + 1)
                V.scalar_tensor_tensor(st[:, 1, :], st[:, 0, :], dec(0, 1), bank[6][:, 0:256], ALU.mult, ALU.add)\
                    .then_inc(sem("gla_state"), 1)
                dve.wait_ge(sem("gla_state"), base + 2)
                V.scalar_tensor_tensor(st[:, 4, :], st[:, 3, :], dec(1, 2), bank[5][:, 0:256], ALU.mult, ALU.add)\
                    .then_inc(sem("gla_state"), 1)
                dve.wait_ge(sem("gla_state"), base + 3)
                V.scalar_tensor_tensor(st[:, 2, :], st[:, 1, :], dec(0, 2), bank[4][:, 256:512], ALU.mult, ALU.add)\
                    .then_inc(sem("gla_state"), 1)
                dve.wait_ge(sem("gla_state"), base + 4)
                V.scalar_tensor_tensor(st[:, 5, :], st[:, 4, :], dec(1, 1), bank[6][:, 256:512], ALU.mult, ALU.add)\
                    .then_inc(sem("gla_state"), 1)
            dve.wait_ge(sem("gla_rstd"), 1)
            dve.wait_ge(sem("gla_in"), 14)
            for g in range(4):
                for k in range(2):
                    hd, t = 2 * (g // 2) + k, g % 2
                    V.scalar_tensor_tensor(gr[:, t, hd * GLA_HV:(hd + 1) * GLA_HV],
                                           bank[2 * t + g // 2][:, k * GLA_HV:(k + 1) * GLA_HV],
                                           oss[:, 2, t * GLA_H + hd:t * GLA_H + hd + 1],
                                           gr[:, t, hd * GLA_HV:(hd + 1) * GLA_HV], ALU.mult, ALU.mult)\
                        .then_inc(sem("gla_y"), 1)
            lhs_lo(Y, lambda kt: cols[:, C_GLA + kt % 2:C_GLA + kt % 2 + 1], T_BANKS)
            mixer_out(GLA_OUT, 1, X)

            def ffn(n, src):
                tin, tout, tple = layer(n)
                j = 3 * n + 1

                def product(t):
                    split_to(END[t + 1] + AHEAD)
                    for k in range(TT):
                        c.wait(dve, "ffn_silu", c.up("ffn_silu"))
                        V.scalar_tensor_tensor(mid[:, (t - tin) % 2, k, :], bank[2 * (t % 2) + k][:, 256:512],
                                               rstd[:, j, k:k + 1], sg[:, (t - tin) % 2, k, :],
                                               ALU.mult, ALU.mult).then_inc(sem("ffn_mid"), 1)

                def parts(t, kt, at):
                    b = T_BANKS[(t - tin) % 2]
                    src_ap = bank[b][:, :].rearrange("p (k s) -> p k s", k=2)
                    split_to(at + AHEAD)
                    c.wait(dve, "ffn_T_filled", c.up("ffn_T_filled"))
                    V.tensor_scalar(M[0][:, bass.ds(kt, 2), :], src_ap, 1.0, None, ALU.mult)\
                        .then_inc(sem("ffn_hi"), 1)
                    c.wait(dve, "ffn_hi", c.up("ffn_hi"))
                    V.tensor_tensor(M[1][:, bass.ds(kt, 2), :], src_ap, M[0][:, bass.ds(kt, 2), :].bitcast(F32),
                                    ALU.subtract).then_inc(sem("ffn_lhs"), 1)

                product(tin)
                for t in range(tin + 1, tin + 3):
                    parts(t - 1, 2 * (t - 1 - tin), END[t] + 2)
                    product(t)
                turns = (FT - 5) // 2
                with dve.Fori(0, turns) as i:
                    c.enter(i, {"w_hi": 8, "w_lo": 8, "ffn_silu": 4, "ffn_mid": 4, "ffn_T_filled": 2, "ffn_hi": 2,
                                "ffn_lhs": 2})
                    for t in (tin + 3, tin + 4):
                        parts(t - 1, i * 4 + 2 * (t - 1 - tin), END[t] + 2)
                        product(t)
                    c.leave(turns)
                pos[0] += 8 * (turns - 1)
                for t in range(tin + 3 + 2 * turns, tin + FT):
                    parts(t - 1, 2 * (t - 1 - tin), END[t] + 2)
                    product(t)
                parts(tin + FT - 1, FKT - 2, END[tout] + 2)
                split_to(END[tout] + 5 + AHEAD)
                dve.wait_ge(sem("pT_hi"), n + 1)
                V.tensor_tensor(PT[1][:, :, :], bank[6][:, :].rearrange("p (k s) -> p k s", k=2),
                                PT[0][:, :, :].bitcast(F32), ALU.subtract).then_inc(sem("pT"), 1)
                j += 1
                mixer_out(tout, j, src)
                for half in range(2):
                    t = tple + 2 * half
                    split_to(END[t + 2] + AHEAD - 2)
                    dve.wait_ge(sem("ple_sig"), TT * (2 * n + half + 1))
                    c.wait(dve, "w_used", END[t + 2])
                    for k in range(TT):
                        V.tensor_tensor(gated[:, k, :], sig[:, k, :], bank[2 * ((t + 1) % 2) + k][:, :], ALU.mult)\
                            .then_inc(sem("ple_gated"), 1)
                    for k in range(TT):
                        dve.wait_ge(sem("ple_gated"), TT * (2 * n + half) + k + 1)
                        V.tensor_tensor(h[:, k, half * HALF:(half + 1) * HALF], h[:, k, half * HALF:(half + 1) * HALF],
                                        gated[:, k, :], ALU.add).then_inc(sem("h_new"), 1)
                    split_to(END[t + 2] + (2 if half == 0 else 1) + AHEAD)
                    lhs_lo(Y if src is X else X, norm_gain(j + 1), (4, 5) if half == 0 else (6, 7))

            ffn(0, X)

            dve.wait_ge(sem("rows_in"), 16)
            cos = consts[:, K_COS:K_COS + 2 * DF_HD].rearrange("p (t e) -> p t e", t=TT)
            sin = consts[:, K_SIN:K_SIN + 2 * DF_HD].rearrange("p (t e) -> p t e", t=TT)
            HD2 = DF_HD // 2
            for w in range(2):
                for m in range(2):
                    g = rows[:, (R_GQ, R_GK)[w] + m * DF_HD:(R_GQ, R_GK)[w] + (m + 1) * DF_HD]
                    lo, hi = m * DF_HD, (m + 1) * DF_HD
                    V.tensor_tensor(rot[:, w, 0, :, lo:hi], cos, g.unsqueeze(1).to_broadcast([P, TT, DF_HD]), ALU.mult)
                    V.tensor_tensor(rot[:, w, 1, :, lo:lo + HD2], sin[:, :, 0:HD2],
                                    g[:, HD2:DF_HD].unsqueeze(1).to_broadcast([P, TT, HD2]), ALU.mult)
                    V.tensor_tensor(rot[:, w, 1, :, lo + HD2:hi], sin[:, :, HD2:DF_HD],
                                    g[:, 0:HD2].unsqueeze(1).to_broadcast([P, TT, HD2]), ALU.mult)\
                        .then_inc(sem("df_rot"), 1)
            lrow = rows[:, R_LAM:R_LAM + 4 * DF_HD].rearrange("p (a b e) -> p a b e", a=2, b=2)
            V.tensor_tensor(do[:, 0, 0:2 * DF_HD].rearrange("p (a e) -> p a e", a=2),
                            lrow[:, :, 0, :], lrow[:, :, 1, :], ALU.mult).then_inc(sem("df_lam"), 1)
            dve.wait_ge(sem("df_lam"), 1)
            V.tensor_reduce(lam[:, 0:2], do[:, 0, 0:2 * DF_HD].rearrange("p (a e) -> p a e", a=2), AXX, ALU.add)\
                .then_inc(sem("df_lam"), 1)

            def head_norm(base, t, tok, sq, ss, sig_sq, sig_ss, sig_rstd, signal):
                c.wait(dve, sig_sq, TT * (t + 1))
                for k in range(TT):
                    V.tensor_reduce(ss[:, 0, k * 8:(k + 1) * 8], sq[:, k, :].rearrange("p (a e) -> p a e", a=8),
                                    AXX, ALU.add).then_inc(sem(sig_ss), 1)
                split_to(END[base + t + 1] + AHEAD + 1)
                dve.wait_ge(sem(sig_rstd), t + 1)
                for k in range(TT):
                    x3 = tok[:, t % 2, k, :].rearrange("p (a e) -> p a e", a=8)
                    V.tensor_tensor(x3, x3, ss[:, 2, k * 8:(k + 1) * 8].unsqueeze(2).to_broadcast([P, 8, NW // 8]),
                                    ALU.mult).then_inc(sem(signal), 1)

            dve.wait_ge(sem("df_rot"), 4)
            for t in range(4):
                split_to(END[DF_IN + t + 1] + AHEAD)
                head_norm(DF_IN, t, dtok, dsq, dss, "df_sq", "df_ss", "df_rstd", "df_unit")
                w = t // 2
                for k in range(TT):
                    xt = dtok[:, t % 2, k, :]
                    x4 = xt.rearrange("p (a u e) -> p a u e", a=8, u=2)
                    m4 = dm2[:, k, :].rearrange("p (a u e) -> p a u e", a=8, u=2)
                    sn = rot[:, w, 1, k, :].rearrange("p (m u e) -> p m u e", m=2, u=2)
                    dve.wait_ge(sem("df_unit"), TT * t + k + 1)
                    for u in range(2):
                        for m in range(2):
                            last = V.tensor_tensor(m4[:, m:8:2, u, :], x4[:, m:8:2, 1 - u, :],
                                                   sn[:, m, u, :].unsqueeze(1).to_broadcast([P, 4, HD2]), ALU.mult)
                    last.then_inc(sem("df_swap"), 1)
                    dve.wait_ge(sem("df_swap"), TT * t + k + 1)
                    V.tensor_tensor(xt.rearrange("p (a e) -> p a e", a=4), xt.rearrange("p (a e) -> p a e", a=4),
                                    rot[:, w, 0, k, :].unsqueeze(1).to_broadcast([P, 4, P]), ALU.mult)\
                        .then_inc(sem("df_cos"), 1)
                for k in range(TT):
                    dve.wait_ge(sem("df_cos"), TT * t + k + 1)
                    V.tensor_tensor(dtok[:, t % 2, k, :], dtok[:, t % 2, k, :], dm2[:, k, :], ALU.add)\
                        .then_inc(sem("df_rope"), 1)
            split_to(END[DF_IN + 6] + AHEAD - 2)
            dve.wait_ge(sem("df_lamexp"), 1)
            V.tensor_tensor(lam[:, 4:5], lam[:, 3:4], lam[:, 2:3], ALU.subtract).then_inc(sem("df_lam"), 1)
            dve.wait_ge(sem("df_lam"), 3)
            V.tensor_scalar(lam[:, 5:6], lam[:, 4:5], LAMBDA_INIT, None, ALU.subtract).then_inc(sem("df_lam"), 1)
            dve.wait_ge(sem("df_lam"), 4)

            def df_max(hd):
                stt = dstat[:, hd % 2, :]
                if hd >= 2:
                    dve.wait_ge(sem("df_recip"), 2 * (hd - 1))
                for m in range(2):
                    dve.wait_ge(sem("df_scores"), 2 * hd + m + 1)
                    V.tensor_reduce(stt[:, 2 * m:2 * m + 2],
                                    bank[T_BANKS[2 * (hd % 2) + m]][:, :].rearrange("p (q k) -> p q k", q=TT),
                                    AXX, ALU.max).then_inc(sem("df_max"), 1)
                dve.wait_ge(sem("df_max"), 3 * hd + 2)
                V.tensor_scalar(stt[:, 4:8], stt[:, 0:4], -DF_HD ** -0.5, None, ALU.mult).then_inc(sem("df_max"), 1)

            def df_a(hd):
                stt = dstat[:, hd % 2, :]
                dve.wait_ge(sem("df_exp"), 4 * (hd + 1))
                V.reciprocal(stt[:, 12:16], stt[:, 8:12]).then_inc(sem("df_recip"), 1)
                dve.wait_ge(sem("df_recip"), 2 * hd + 1)
                V.tensor_scalar(stt[:, 0:2], stt[:, 14:16], lam[:, 5:6], None, ALU.mult).then_inc(sem("df_recip"), 1)
                dve.wait_ge(sem("df_recip"), 2 * hd + 2)
                for q in range(TT):
                    V.tensor_scalar(dp[:, hd % 2, 1, q, :], dp[:, hd % 2, 1, q, :], stt[:, q:q + 1], None, ALU.mult)\
                        .then_inc(sem("df_p1"), 1)
                if hd >= 2:
                    dve.wait_ge(sem("df_aT_filled"), hd - 1)
                for q in range(TT):
                    dve.wait_ge(sem("df_p1"), TT * hd + q + 1)
                    V.scalar_tensor_tensor(da[:, hd % 2, q, :], dp[:, hd % 2, 0, q, :], stt[:, 12 + q:13 + q],
                                           dp[:, hd % 2, 1, q, :], ALU.mult, ALU.add).then_inc(sem("df_a"), 1)

            df_max(0)
            for hd in range(DF_H):
                if hd + 1 < DF_H:
                    df_max(hd + 1)
                df_a(hd)
            for g in range(2):
                dve.wait_ge(sem("df_osq"), TT * (g + 1))
                for q in range(TT):
                    V.tensor_reduce(dss[:, 0, q * 4:(q + 1) * 4], dsq[:, q, :].rearrange("p (a e) -> p a e", a=4),
                                    AXX, ALU.add).then_inc(sem("df_oss"), 1)
                dve.wait_ge(sem("df_orstd"), g + 1)
                for q in range(TT):
                    o3 = do[:, q, g * NW:(g + 1) * NW].rearrange("p (a e) -> p a e", a=4)
                    V.tensor_tensor(o3, o3, dss[:, 2, q * 4:(q + 1) * 4].unsqueeze(2).to_broadcast([P, 4, P]),
                                    ALU.mult).then_inc(sem("df_y"), 1)
            lhs_lo(X, lambda kt: cols[:, C_DF:C_DF + 1], T_BANKS)
            mixer_out(DF_OUT, 4, Y)
            ffn(1, Y)

            V.memset(cu[:, :, 0:CONV_K - 1], 0.0).then_inc(sem("cv_pad"), 1)

            def conv_product(t):
                split_to(END[t + 1] + AHEAD)
                for k in range(TT):
                    c.wait(dve, "cv_act", c.up("cv_act"))
                    for m in range(2):
                        src = bank[2 * (t % 2) + k][:, (1 - m) * P:(2 - m) * P]
                        last = V.scalar_tensor_tensor(cprod[:, (t - CV_IN) % 2, k, m, :], src, rstd[:, 6, k:k + 1],
                                                      cact[:, (t - CV_IN) % 2, k, m, :], ALU.mult, ALU.mult)
                    last.then_inc(sem("cv_prod"), 1)

            def conv_parts(t, blk, at):
                par = (t - CV_IN) % 2
                b = T_BANKS[par]
                split_to(at + AHEAD)
                c.wait(dve, "cv_T_filled", c.up("cv_T_filled"))

                def tap(k):
                    return cols[:, bass.ds(blk * CONV_K + (C_CONV + k), 1)]

                def step(ins):
                    ins.then_inc(sem("cv_step"), 1)
                    c.wait(dve, "cv_step", c.up("cv_step"))

                step(V.tensor_copy(cu[:, par, CONV_K - 1:], bank[b][:, 0:SEQ]))
                step(V.tensor_scalar(cc[:, 0, :], cu[:, par, 0:SEQ], tap(0), None, ALU.mult))
                step(V.scalar_tensor_tensor(cc[:, 1, :], cu[:, par, 1:SEQ + 1], tap(1), cc[:, 0, :],
                                            ALU.mult, ALU.add))
                step(V.scalar_tensor_tensor(cc[:, 2, :], cu[:, par, 2:SEQ + 2], tap(2), cc[:, 1, :],
                                            ALU.mult, ALU.add))
                step(V.tensor_tensor(cc[:, 3, :], cc[:, 2, :], bank[b][:, SEQ:2 * SEQ], ALU.mult))
                step(V.tensor_scalar(Y[0][:, bass.ds(blk, 1), :], cc[:, 3, :].unsqueeze(1), 1.0, None, ALU.mult))
                V.tensor_tensor(Y[1][:, bass.ds(blk, 1), :], cc[:, 3, :].unsqueeze(1),
                                Y[0][:, bass.ds(blk, 1), :].bitcast(F32), ALU.subtract).then_inc(sem("cv_lhs"), 1)

            dve.wait_ge(sem("cv_pad"), 1)
            conv_product(CV_IN)
            for t in range(CV_IN + 1, CV_IN + 3):
                conv_parts(t - 1, t - 1 - CV_IN, END[t] + 2)
                conv_product(t)
            with dve.Fori(0, 2) as i:
                c.enter(i, {"w_hi": 8, "w_lo": 8, "cv_act": 4, "cv_prod": 4, "cv_T_filled": 2, "cv_step": 12,
                            "cv_lhs": 2})
                for t in (CV_IN + 3, CV_IN + 4):
                    conv_parts(t - 1, i * 2 + (t - 1 - CV_IN), END[t] + 2)
                    conv_product(t)
                c.leave(2)
            pos[0] += 8
            conv_parts(CV_IN + 6, 6, END[CV_IN + 7] + 2)
            conv_product(CV_IN + 7)
            conv_parts(CV_IN + 7, 7, END[CV_OUT] + 2)
            mixer_out(CV_OUT, 7, X)

            V.tensor_scalar(mgain[:, 0:1], cols[:, C_QG:C_QG + 1], MB_HD ** -0.5, None, ALU.mult)
            V.tensor_copy(mgain[:, 1:2], cols[:, C_KG:C_KG + 1]).then_inc(sem("mb_gain"), 1)
            for t in range(4):
                split_to(END[MB_IN + t + 1] + AHEAD)
                head_norm(MB_IN, t, mtok, msq, mss, "mb_sq", "mb_ss", "mb_rstd", "mb_unit")
            split_to(END[MB_IN + 8] + AHEAD - 2)

            def mb_max(hd):
                slope = 2.0 ** (-8.0 * (hd + 1) / MB_H)
                dve.wait_ge(sem("mb_scores"), hd + 1)
                if hd >= 2:
                    dve.wait_ge(sem("mb_exp"), TT * (hd - 1))
                V.scalar_tensor_tensor(ms2[:, hd % 2, 0:3 * P], consts[:, K_DIST:K_DIST + 3 * P], slope,
                                       bank[T_BANKS[hd % 4]][:, 0:3 * P], ALU.mult, ALU.add)\
                    .then_inc(sem("mb_biased"), 1)
                dve.wait_ge(sem("mb_biased"), hd + 1)
                V.tensor_reduce(mstat[:, hd % 2, 0:1], ms2[:, hd % 2, 0:P], AXX, ALU.max)
                V.tensor_reduce(mstat[:, hd % 2, 1:2], ms2[:, hd % 2, P:3 * P], AXX, ALU.max)\
                    .then_inc(sem("mb_rowmax"), 1)
                dve.wait_ge(sem("mb_rowmax"), hd + 1)
                V.tensor_scalar(mstat[:, hd % 2, 2:4], mstat[:, hd % 2, 0:2], -1.0, None, ALU.mult)\
                    .then_inc(sem("mb_max"), 1)

            def mb_out(g):
                dve.wait_ge(sem("mb_exp"), TT * 8 * (g + 1))
                V.reciprocal(mrec[:, :, 8 * g:8 * g + 8], msum[:, :, 8 * g:8 * g + 8]).then_inc(sem("mb_recip"), 1)
                dve.wait_ge(sem("mb_recip"), g + 1)
                dve.wait_ge(sem("mb_av"), 8 * (g + 1))
                for q in range(TT):
                    V.tensor_tensor(mo[:, q, :].rearrange("p (a e) -> p a e", a=8),
                                    bank[2 + q][:, :].rearrange("p (a e) -> p a e", a=8),
                                    mrec[:, q, 8 * g:8 * g + 8].unsqueeze(2).to_broadcast([P, 8, MB_HD]), ALU.mult)\
                        .then_inc(sem("mb_o"), 1)
                for q in range(TT):
                    dve.wait_ge(sem("mb_o"), TT * g + q + 1)
                    V.tensor_tensor(mz[:, q, g * NW:(g + 1) * NW], mz[:, q, g * NW:(g + 1) * NW], mo[:, q, :],
                                    ALU.mult).then_inc(sem("mb_y"), 1)

            for hd in range(MB_H):
                mb_max(hd)
                if hd == 10:
                    mb_out(0)
            mb_out(1)
            lhs_lo(Y, None, T_BANKS)
            residual(MB_OUT, 0)
            split_to(UNITS)
            residual(MB_OUT + 1, 1)

        @block.tensor
        def _(pe):
            c = Count(sem)
            T = nc.tensor
            free = {}

            def claim(b):
                if b in free:
                    c.wait(pe, *free[b])

            def product(tile, lhs, signal, kt0=0, need=None, hooks=(), width=NW, by=1):
                pair = 2 * (tile % 2)
                hooks = dict(hooks)
                n = TILES[tile]
                for k in range(n):
                    if k in hooks:
                        hooks[k]()
                    if k == 0:
                        claim(pair)
                        claim(pair + 1)
                    if need is not None and need[k] is not None:
                        c.wait(pe, *need[k])
                    u = END[tile] + k
                    c.wait(pe, "w_lo", u + 1)
                    each = 2 if width == NW else KT
                    for t in range(TT):
                        for kk in range(each):
                            kt = kt0 + 2 * k + kk
                            for i, (a, w) in enumerate(((0, whi), (0, wlo), (1, whi))):
                                last = T.matmul(bank[pair + t][:, 0:width],
                                                lhs[a][:, kt, t * P:(t + 1) * P],
                                                w[:, u % RING, kk * width:(kk + 1) * width],
                                                start=k == kk == i == 0,
                                                stop=k == n - 1 and kk == each - 1 and i == 2)
                    last.then_inc(sem("w_used"), 1)
                if signal is not None:
                    for t in range(TT):
                        free[pair + t] = (signal, c.up(signal, by))

            def lhs_T(src, banks):
                need = []
                for b in banks:
                    claim(b)
                    for k in range(2):
                        for t in range(TT):
                            kt = 2 * (b - T_BANKS[0]) + k
                            last = T.transpose(bank[b][:, k * SEQ + t * P:k * SEQ + (t + 1) * P],
                                               src[:, t, kt * P:(kt + 1) * P], ident)
                    last.then_inc(sem("lhs_filled"), 1)
                    free[b] = ("lhs", c.up("lhs"))
                    need.append(free[b])
                return need

            def h_T(half, version):
                pe.wait_ge(sem("h_new"), 4 * (version - 1) + 2 * (half + 1))
                return lhs_T(h, (4, 5) if half == 0 else (6, 7))

            def chained(tile, lhs, signal, version, need=None, hooks=()):
                got = []
                product(tile, lhs, signal, need=need, hooks=hooks)
                product(tile + 1, lhs, signal, hooks=[(2, lambda: got.extend(h_T(0, version)))])
                return got

            pe.wait_ge(sem("consts_in"), 16)
            pe.wait_ge(sem("x_in"), 16)
            need = lhs_T(h, T_BANKS)

            def z_T():
                pe.wait_ge(sem("gla_in"), 2)
                claim(4)
                for t in range(TT):
                    last = T.transpose(bank[4][0:32, t * P:(t + 1) * P], zt[:, t, :], ident)
                last.then_inc(sem("gla_zT_filled"), 1)
                free[4] = ("gla_zT", 1)

            def pre_gates():
                pe.wait_ge(sem("gla_zT"), 1)
                pe.wait_ge(sem("gla_ones"), 1)
                pe.wait_ge(sem("wg_in"), 16)
                for g in range(4):
                    claim(T_BANKS[g])
                    T.matmul(bank[T_BANKS[g]][:, :], zT[0:33, (g % 2) * P:(g % 2 + 1) * P],
                             wg[0:33, (g // 2) * GLA_K:(g // 2 + 1) * GLA_K], start=True, stop=True)\
                        .then_inc(sem("gla_pre"), 1)
                    free[T_BANKS[g]] = ("gla_la", g + 1)

            def qk_T():
                pe.wait_ge(sem("gla_in"), 6)
                for g in range(4):
                    claim(T_BANKS[g])
                    for k in range(2):
                        for t in range(TT):
                            hd = 2 * (g % 2) + k
                            last = T.transpose(bank[T_BANKS[g]][:, k * SEQ + t * P:k * SEQ + (t + 1) * P],
                                               qk_tok[:, g // 2, t, hd * P:(hd + 1) * P], ident)
                    last.then_inc(sem("gla_qkT_filled"), 1)
                    free[T_BANKS[g]] = ("gla_qkT", g + 1)

            def cumulate():
                pe.wait_ge(sem("gla_la"), 4)
                for g in range(4):
                    d = g // 2
                    claim(T_BANKS[g])
                    for k in range(2):
                        for t in range(TT):
                            hd = 2 * (g % 2) + k
                            last = T.matmul(bank[T_BANKS[g]][:, k * SEQ + t * P:k * SEQ + (t + 1) * P],
                                            la[:, t, d * GLA_K + hd * P:d * GLA_K + (hd + 1) * P],
                                            consts[:, K_TRI + d * P:K_TRI + (d + 1) * P], start=True, stop=True)
                    last.then_inc(sem("gla_cum"), 1)
                    free[T_BANKS[g]] = ("gla_exp", 2 * (g + 1))

            def kD_T():
                pe.wait_ge(sem("gla_gated"), 8)
                for g in range(4):
                    d, t = divmod(g, 2)
                    claim(T_BANKS[g])
                    for hd in range(GLA_H):
                        last = T.transpose(bank[T_BANKS[g]][:, hd * P:(hd + 1) * P],
                                           kD[:, d, hd * SEQ + t * P:hd * SEQ + (t + 1) * P], ident)
                    last.then_inc(sem("gla_kDt_filled"), 1)
                    free[T_BANKS[g]] = ("gla_kDt", g + 1)

            def gla_scores():
                for g in range(4):
                    d, t = divmod(g, 2)
                    claim(T_BANKS[g])
                    for hd in range(GLA_H):
                        at = slice(hd * SEQ + t * P, hd * SEQ + (t + 1) * P)
                        last = T.matmul(bank[T_BANKS[g]][:, hd * P:(hd + 1) * P], kE[:, d, at], qE[:, d, at],
                                        start=True, stop=True)
                    last.then_inc(sem("gla_scores"), 1)
                    free[T_BANKS[g]] = ("gla_probs", g + 1)

            pe.wait_ge(*[sem(need[3][0]), need[3][1]])
            product(GLA_IN, X, "gla_in", width=2 * GLA_R)
            stages = {1: z_T, 2: pre_gates, 3: qk_T, 4: cumulate, 5: kD_T, 6: gla_scores}
            for t in range(1, 7):
                product(GLA_IN + t, X, "gla_in", hooks=[(2, stages[t])])

            def gla_u(hd):
                plan = ((4, 0, 0, 0), (4, 1, 0, 2), (5, 0, 1, 2), (6, 0, 0, 1), (6, 1, 1, 1), (7, 0, 1, 3))
                for b in T_BANKS:
                    claim(b)
                for n, (b, at, d, ch) in enumerate(plan):
                    t, r = ch // 2, (ch % 2) * GLA_C
                    last = T.matmul(bank[b][:, at * GLA_HV:(at + 1) * GLA_HV],
                                    kDt[r:r + GLA_C, d, t, hd * P:(hd + 1) * P],
                                    gv[r:r + GLA_C, t, hd * GLA_HV:(hd + 1) * GLA_HV], start=True, stop=True)
                    if n == len(plan) - 1 or plan[n + 1][0] != b:
                        last.then_inc(sem("gla_u"), 1)
                for b, after in ((4, 5), (5, 4), (6, 6), (7, 2)):
                    free[b] = ("gla_state", 6 * hd + after)

            def gla_o(hd):
                st = states[hd % 2]
                pe.wait_ge(sem("gla_state"), 6 * (hd + 1))
                pe.wait_ge(sem("gla_probs"), 4)
                at = slice((hd % 2) * GLA_HV, (hd % 2 + 1) * GLA_HV)
                for t in range(TT):
                    b = 2 * t + hd // 2
                    if hd % 2 == 0:
                        claim(b)
                    T.matmul(bank[b][:, at], probs[:, t, hd * P:(hd + 1) * P],
                             gv[:, t, hd * GLA_HV:(hd + 1) * GLA_HV], start=True, stop=True)
                    inter = [(ch, d) for ch in (2 * t, 2 * t + 1) for d in range(2)
                             if (ch > 0 if d == 0 else ch < 3)]
                    for n, (ch, d) in enumerate(inter):
                        r = (ch % 2) * GLA_C
                        last = T.matmul(bank[b][r:r + GLA_C, at],
                                        qE[:, d, hd * SEQ + ch * GLA_C:hd * SEQ + (ch + 1) * GLA_C],
                                        st[:, ch - 1 if d == 0 else 5 - ch, :], start=False, stop=True,
                                        skip_group_check=True)
                    if t == TT - 1:
                        last.then_inc(sem("gla_head"), 1)

            pe.wait_ge(sem("gla_kDt"), 4)
            pe.wait_ge(sem("gla_in"), 14)
            gla_u(0)
            for hd in range(GLA_H):
                if hd + 1 < GLA_H:
                    gla_u(hd + 1)
                gla_o(hd)
            for t in range(TT):
                for pair in range(2):
                    free[2 * t + pair] = ("gla_y", 4 * pair + 2 * t + 2)
            pe.wait_ge(sem("gla_y"), 8)
            need = lhs_T(gr, T_BANKS)
            got = []
            product(GLA_OUT, Y, None, need=need)
            for t in range(TT):
                free[2 * (GLA_OUT % 2) + t] = ("h_new", t + 1)
            product(GLA_OUT + 1, Y, None, hooks=[(2, lambda: got.extend(h_T(0, 1)))])
            for t in range(TT):
                free[2 * ((GLA_OUT + 1) % 2) + t] = ("h_new", TT + t + 1)
            c.up("h_new", 4)

            def ffn(n, src, got):
                tin, tout, tple = layer(n)
                other = Y if src is X else X

                def mid_T(t):
                    b = T_BANKS[(t - tin) % 2]
                    c.wait(pe, "ffn_mid", TT * (t - tin + 1) + TT * FT * n)
                    claim(b)
                    for k in range(2):
                        for tt in range(TT):
                            last = T.transpose(bank[b][:, k * SEQ + tt * P:k * SEQ + (tt + 1) * P],
                                               mid[:, (t - tin) % 2, tt, k * P:(k + 1) * P], ident)
                    last.then_inc(sem("ffn_T_filled"), 1)
                    free[b] = ("ffn_lhs", c.up("ffn_lhs"))

                more = list(got) + [None, None]

                def second_half():
                    more[2:4] = h_T(1, 3 * n + 1)

                product(tin, src, "ffn_mid", need=more, hooks=[(1, second_half)])
                for t in range(tin + 1, tin + 3):
                    product(t, src, "ffn_mid", hooks=[(2, lambda t=t: mid_T(t - 1))])
                turns = (FT - 5) // 2
                with pe.Fori(0, turns) as i:
                    c.enter(i, {"w_lo": 8, "w_used": 8, "ffn_mid": 4, "ffn_lhs": 2})
                    for t in (tin + 3, tin + 4):
                        product(t, src, "ffn_mid", hooks=[(2, lambda t=t: mid_T(t - 1))])
                    c.leave(turns)
                for b, (name, value) in list(free.items()):
                    free[b] = (name, value + (turns - 1) * {"ffn_mid": 4, "ffn_lhs": 2}.get(name, 0))
                for t in range(tin + 3 + 2 * turns, tin + FT):
                    product(t, src, "ffn_mid", hooks=[(2, lambda t=t: mid_T(t - 1))])

                def p_T():
                    pe.wait_ge(sem("p_in"), 16)
                    claim(6)
                    for k in range(2):
                        for t in range(TT):
                            last = T.transpose(bank[6][:, k * SEQ + t * P:k * SEQ + (t + 1) * P],
                                               p_tok[:, n, t, k * P:(k + 1) * P], ident)
                    last.then_inc(sem("pT_filled"), 1)
                    free[6] = ("pT", n + 1)

                half0 = []
                need = [("ffn_lhs", FT * n + k + 1) for k in range(FT)]
                product(tout, M, "h_new", need=need, hooks=[(2, lambda: mid_T(tin + FT - 1)), (5, p_T)])
                product(tout + 1, M, "h_new", hooks=[(2, lambda: half0.extend(h_T(0, 3 * n + 2)))])
                more2 = list(half0) + [None, None]

                def second_half2():
                    more2[2:4] = h_T(1, 3 * n + 2)

                product(tple, src, "ple_sig", need=more2, hooks=[(1, second_half2)])
                product(tple + 1, PT, "ple_gated", need=[("pT", n + 1)])
                half1 = []
                product(tple + 2, src, "ple_sig", hooks=[(2, lambda: half1.extend(h_T(0, 3 * n + 3)))])
                product(tple + 3, PT, "ple_gated")
                c.up("h_new", 4)
                return half1

            half = ffn(0, X, got)

            def df_T(t):
                pe.wait_ge(sem("df_rope"), TT * (t + 1))
                for b in range(2):
                    g = 2 * t + b
                    claim(T_BANKS[g % 4])
                    for k in range(2):
                        for tt in range(TT):
                            last = T.transpose(bank[T_BANKS[g % 4]][:, k * SEQ + tt * P:k * SEQ + (tt + 1) * P],
                                               dtok[:, t % 2, tt, (2 * b + k) * P:(2 * b + k + 1) * P], ident)
                    last.then_inc(sem("df_T_filled"), 1)
                    free[T_BANKS[g % 4]] = ("df_T", g + 1)

            more = list(half) + [None, None]

            def df_second():
                more[2:4] = h_T(1, 3)

            product(DF_IN, Y, "df_in", need=more, hooks=[(1, df_second)])
            product(DF_IN + 1, Y, "df_in")
            for t in range(2, 6):
                product(DF_IN + t, Y, "df_in", hooks=[(1, lambda t=t: df_T(t - 2))])

            def df_scores(hd):
                for m in range(2):
                    b = T_BANKS[2 * (hd % 2) + m]
                    claim(b)
                    r = slice(m * DF_HD, (m + 1) * DF_HD)
                    for q in range(TT):
                        last = T.matmul(bank[b][:, q * SEQ:(q + 1) * SEQ], dT[r, 0, hd, q * P:(q + 1) * P],
                                        dT[r, 1, hd, :], start=True, stop=True)
                    last.then_inc(sem("df_scores"), 1)
                    free[b] = ("df_exp", 4 * hd + 2 * (m + 1))

            def df_aT(hd):
                pe.wait_ge(sem("df_a"), TT * (hd + 1))
                claim(hd % 2)
                for k in range(TT):
                    for q in range(TT):
                        last = T.transpose(bank[hd % 2][:, k * SEQ + q * P:k * SEQ + (q + 1) * P],
                                           da[:, hd % 2, q, k * P:(k + 1) * P], ident)
                last.then_inc(sem("df_aT_filled"), 1)
                free[hd % 2] = ("df_aT", hd + 1)

            def df_av(hd):
                pe.wait_ge(sem("df_aT"), hd + 1)
                for q in range(TT):
                    if hd % 4 == 0:
                        claim(2 + q)
                    for k in range(TT):
                        last = T.matmul(bank[2 + q][:, (hd % 4) * P:(hd % 4 + 1) * P],
                                        daT[:, hd % 2, k * SEQ + q * P:k * SEQ + (q + 1) * P],
                                        dv[:, k, hd * P:(hd + 1) * P], start=k == 0, stop=k == TT - 1)
                    if hd % 4 == 3:
                        free[2 + q] = ("df_o", TT * (hd // 4) + q + 1)
                last.then_inc(sem("df_av"), 1)

            pe.wait_ge(sem("df_T"), 8)
            pe.wait_ge(sem("df_in"), 12)
            df_scores(0)
            df_scores(1)
            for hd in range(DF_H):
                df_aT(hd)
                if hd + 2 < DF_H:
                    df_scores(hd + 2)
                df_av(hd)
            pe.wait_ge(sem("df_y"), 4)
            need = lhs_T(do, T_BANKS)
            got = chained(DF_OUT, X, "h_new", 4, need=need)
            half = ffn(1, Y, got)

            def cv_T(t):
                b = T_BANKS[(t - CV_IN) % 2]
                c.wait(pe, "cv_prod", TT * (t - CV_IN + 1))
                claim(b)
                for m in range(2):
                    for tt in range(TT):
                        last = T.transpose(bank[b][:, m * SEQ + tt * P:m * SEQ + (tt + 1) * P],
                                           cprod[:, (t - CV_IN) % 2, tt, m, :], ident)
                last.then_inc(sem("cv_T_filled"), 1)
                free[b] = ("cv_lhs", c.up("cv_lhs"))

            more3 = list(half) + [None, None]

            def cv_second():
                more3[2:4] = h_T(1, 6)

            product(CV_IN, X, "cv_prod", need=more3, hooks=[(1, cv_second)])
            for t in (CV_IN + 1, CV_IN + 2):
                product(t, X, "cv_prod", hooks=[(2, lambda t=t: cv_T(t - 1))])
            with pe.Fori(0, 2) as i:
                c.enter(i, {"w_lo": 8, "w_used": 8, "cv_prod": 4, "cv_lhs": 2})
                for t in (CV_IN + 3, CV_IN + 4):
                    product(t, X, "cv_prod", hooks=[(2, lambda t=t: cv_T(t - 1))])
                c.leave(2)
            for b, (name, value) in list(free.items()):
                free[b] = (name, value + {"cv_prod": 4, "cv_lhs": 2}.get(name, 0))
            product(CV_IN + 7, X, "cv_prod", hooks=[(2, lambda: cv_T(CV_IN + 6))])
            got = chained(CV_OUT, Y, "h_new", 7, need=[("cv_lhs", 2 * (k + 1)) for k in range(4)],
                          hooks=[(2, lambda: cv_T(CV_IN + 7))])

            def mb_T(t):
                pe.wait_ge(sem("mb_unit"), TT * (t + 1))
                for b in range(2):
                    g = 2 * t + b
                    claim(T_BANKS[g % 4])
                    for k in range(2):
                        for tt in range(TT):
                            last = T.transpose(bank[T_BANKS[g % 4]][:, k * SEQ + tt * P:k * SEQ + (tt + 1) * P],
                                               mtok[:, t % 2, tt, (2 * b + k) * P:(2 * b + k + 1) * P], ident)
                    last.then_inc(sem("mb_T_filled"), 1)
                    free[T_BANKS[g % 4]] = ("mb_T", g + 1)

            more4 = list(got) + [None, None]

            def mb_second():
                more4[2:4] = h_T(1, 7)

            product(MB_IN, X, "mb_in", need=more4, hooks=[(1, mb_second)])
            product(MB_IN + 1, X, "mb_in")
            for t in range(2, 8):
                product(MB_IN + t, X, "mb_in", hooks=[(1, lambda t=t: mb_T(t - 2))] if t < 6 else ())

            def mb_scores(hd):
                b = T_BANKS[hd % 4]
                claim(b)
                r, blk = slice((hd % 2) * MB_HD, (hd % 2 + 1) * MB_HD), hd // 2
                T.matmul(bank[b][:, 0:P], mT[r, 0, blk, 0:P], mT[r, 1, blk, 0:P], start=True, stop=True)
                T.matmul(bank[b][:, P:3 * P], mT[r, 0, blk, P:SEQ], mT[r, 1, blk, :], start=True, stop=True)\
                    .then_inc(sem("mb_scores"), 1)
                free[b] = ("mb_biased", hd + 1)

            def mb_pT(hd):
                pe.wait_ge(sem("mb_exp"), TT * (hd + 1))
                claim(hd % 2)
                for n in range(3):
                    last = T.transpose(bank[hd % 2][:, n * P:(n + 1) * P], mp[:, 2 + hd % 2, n * P:(n + 1) * P], ident)
                last.then_inc(sem("mb_pT_filled"), 1)
                free[hd % 2] = ("mb_pT", hd + 1)

            def mb_av(hd):
                pe.wait_ge(sem("mb_pT"), hd + 1)
                at = slice((hd % 8) * MB_HD, (hd % 8 + 1) * MB_HD)
                if hd % 8 == 0:
                    claim(2)
                    claim(3)
                T.matmul(bank[2][:, at], mpT[:, hd % 2, 0:P], mv[:, 0, hd * MB_HD:(hd + 1) * MB_HD],
                         start=True, stop=True)
                for k in range(2):
                    last = T.matmul(bank[3][:, at], mpT[:, hd % 2, (k + 1) * P:(k + 2) * P],
                                    mv[:, k, hd * MB_HD:(hd + 1) * MB_HD], start=k == 0, stop=k == 1)
                last.then_inc(sem("mb_av"), 1)
                if hd % 8 == 7:
                    for q in range(TT):
                        free[2 + q] = ("mb_o", TT * (hd // 8) + q + 1)

            pe.wait_ge(sem("mb_T"), 8)
            pe.wait_ge(sem("mb_in"), 16)
            mb_scores(0)
            mb_scores(1)
            for hd in range(MB_H):
                if hd + 2 < MB_H:
                    mb_scores(hd + 2)
                mb_pT(hd)
                if hd:
                    mb_av(hd - 1)
            mb_av(MB_H - 1)
            pe.wait_ge(sem("mb_y"), 4)
            need = lhs_T(mz, T_BANKS)
            product(MB_OUT, Y, "h_new", need=need)
            product(MB_OUT + 1, Y, "h_new")


def _units(w, tiles):
    k = w.shape[0]
    return np.concatenate([w[:, t].reshape(k // 256, 2, P, NW).transpose(0, 2, 1, 3).reshape(k // 256, P, 2 * NW)
                           for t in tiles])


def _plain(n):
    return [slice(t, t + NW) for t in range(0, n, NW)]


def _grouped(n, parts, of):
    size = n // parts
    return [np.concatenate([np.arange(q * size + j, q * size + j + of) for q in range(parts)])
            for j in range(0, size, of)]


def _constants():
    i = np.arange(P)
    same = (i[:, None] // GLA_C) == (i[None, :] // GLA_C)
    up = same & (i[:, None] <= i[None, :])
    down = same & (i[:, None] >= i[None, :])
    strict = same & (i[:, None] > i[None, :])
    half = DF_HD // 2
    inv = np.float32(10000.0) ** (-np.arange(half, dtype=np.float32) * np.float32(2.0) / np.float32(DF_HD))
    ang = np.arange(SEQ, dtype=np.float32)[:, None] * inv[None, :].astype(np.float32)
    cos, sin = np.cos(ang), np.sin(ang)
    cos = np.concatenate([cos, cos], 1).reshape(TT, P, DF_HD).transpose(1, 0, 2).reshape(P, -1)
    sin = np.concatenate([-sin, sin], 1).reshape(TT, P, DF_HD).transpose(1, 0, 2).reshape(P, -1)
    k = np.arange(SEQ)
    dist = [np.where(k[None, :n] <= i[:, None] + q0, k[None, :n] - i[:, None] - q0, -1e32)
            for q0, n in ((0, P), (P, SEQ))]
    return np.concatenate([np.eye(P), up / 16.0, down / 16.0, up, strict, cos, sin] + dist, 1).astype(np.float32)


def kernel(**inputs):
    import concourse.bacc as _bacc
    from concourse.bass_utils import run_bass_kernel_spmd as _run

    a = {name: np.asarray(value) for name, value in inputs.items()}
    gla = a["gla_w_in"][0]
    z = gla[:, 3 * D:3 * D + 2 * GLA_R].reshape(KT, P, 2 * GLA_R).transpose(1, 0, 2).reshape(P, -1)
    first = np.zeros((1, P, 2 * NW), np.float32)
    first[0, :, :z.shape[1]] = z

    def layer(n):
        gate, proj = _units(a["ple_w_gate"][n], _plain(D)), _units(a["ple_w_proj"][n], _plain(D))
        return [_units(a["ffn_w_in"][n], _grouped(2 * FF, 2, 256)), _units(a["ffn_w_out"][n], _plain(D)),
                gate[:KT // 2], proj[:1], gate[KT // 2:], proj[1:]]

    stream = np.concatenate(
        [first, _units(gla, _plain(3 * D)), _units(a["gla_w_out"][0], _plain(D))] + layer(0)
        + [_units(a["diff_w_in"][0], _plain(3 * D)), _units(a["diff_w_out"][0], _plain(D))] + layer(1)
        + [_units(a["conv_w_in_2"][0], _grouped(4 * D, 4, P)), _units(a["conv_w_out_2"][0], _plain(D)),
           _units(a["attn_w_in_2"][0], _plain(4 * D)), _units(a["attn_w_out_2"][0], _plain(D))])
    norms = [a["norm_mix"][0], a["norm_ffn"][0], a["ple_norm"][0], a["norm_mix"][1], a["norm_ffn"][1],
             a["ple_norm"][1], a["norm_g_2"][0], a["norm_g_2"][1]]
    cols = np.concatenate(
        [g.reshape(-1, P).T for g in norms + [a["gla_g_out"][0], a["diff_g_sub"][0]]]
        + [np.concatenate([a[g][0]] * 2)[:, None] for g in ("q_norm_g_2", "k_norm_g_2")]
        + [a["conv_w_2"][0].reshape(CONV_K, KT, P).transpose(2, 1, 0).reshape(P, -1)], 1)
    rows = np.concatenate([a["diff_g_q"][0].ravel(), a["diff_g_k"][0].ravel()]
                          + [a[f"diff_lam_{n}"][0] for n in ("q1", "k1", "q2", "k2")])[None]
    wgate = np.zeros((33, 2 * GLA_K), np.float32)
    wgate[0:GLA_R, :GLA_K], wgate[GLA_R:2 * GLA_R, GLA_K:] = a["gla_w_gate_f"][0], a["gla_w_gate_b"][0]
    wgate[32, :GLA_K], wgate[32, GLA_K:] = a["gla_b_gate_f"][0], a["gla_b_gate_b"][0]
    arrays = {"stream": stream, "x": a["x"][0], "p": a["p"][:, 0], "cols": cols, "rows": rows,
              "consts": _constants(), "wgate": wgate}
    arrays = {name: np.ascontiguousarray(value) for name, value in arrays.items()}
    nc = _bacc.Bacc("TRN2", target_bir_lowering=False, num_devices=1)
    args = [nc.dram_tensor(f"{name}_dram", value.shape, F32, kind="ExternalInput").ap() for name, value in arrays.items()]
    out = nc.dram_tensor("out", (SEQ, D), F32, kind="ExternalOutput").ap()
    stream_, x_, p_, cols_, rows_, consts_, wgate_ = args
    build(nc, stream_, x_, p_, cols_, rows_, consts_, wgate_, out)
    r = _run(nc, [{f"{name}_dram": value for name, value in arrays.items()}], core_ids=[0])
    return r.results[0]["out"].reshape(1, SEQ, D)
```

```python
import math
from contextlib import ExitStack

import numpy as np

import concourse.bass as bass
from concourse import mybir
from concourse.alu_op_type import AluOpType as ALU

F32 = mybir.dt.float32
F32R = mybir.dt.float32r
U32 = mybir.dt.uint32
ACT = mybir.ActivationFunctionType
AXX = mybir.AxisListType.X

P = 128
SEQ, D = 256, 1024
TT = SEQ // P
KT = D // P
NW = 512
EPS = 1e-6
FF = (-((-8 * D) // 3) + 255) // 256 * 256
FKT = FF // P
FT = FF // 256
PLE = 256
HALF = D // 2

GLA_H, GLA_HK, GLA_HV, GLA_C, GLA_R = 4, 128, 256, 64, 16
GLA_K = GLA_H * GLA_HK
DF_H, DF_HD = 8, 64
LAMBDA_INIT = 0.8 - 0.6 * math.exp(-0.3)
MB_H, MB_HD = 16, 64
CONV_K = 3

IN, OUT = KT // 2, [KT // 4] * 4
LAYER = [IN] * FT + [FKT // 2] * 2 + [IN, 1] * 2
TILES = [1] + [IN] * 6 + [IN] * 2 + LAYER
GLA_IN, GLA_OUT, FFN_IN0 = 0, 7, 9
FFN_OUT0 = FFN_IN0 + FT
PLE0 = FFN_OUT0 + 2
DF_IN = PLE0 + 4
TILES += [IN] * 6 + OUT + LAYER
DF_OUT = DF_IN + 6
FFN_IN1 = DF_OUT + 4
FFN_OUT1 = FFN_IN1 + FT
PLE1 = FFN_OUT1 + 2
CV_IN = PLE1 + 4
TILES += [IN] * 8 + [IN] * 2
CV_OUT = CV_IN + 8
MB_IN = CV_OUT + 2
TILES += [IN] * 8 + OUT
MB_OUT = MB_IN + 8
END = [0]
for _n in TILES:
    END.append(END[-1] + _n)
UNITS = END[-1]
RAW, RING = 4, 8
AHEAD = 6


def plan(first, tiles, steps):
    base = END[first]
    found = [(base + u, 1, n, step, arg) for u, row in steps.items() for n, (step, arg) in enumerate(row)]
    found += [(END[first + t + 1], 2, 0, "tile", t) for t in range(tiles)]
    return [(u, step, arg) for u, _, _, step, arg in sorted(found, key=lambda x: x[:3])]


_steps = {1: [("second", 0)]}
for _n, _u in enumerate(((5, 6, 8), (8, 10, 13), (13, 15, 17))):
    for _step, _at in zip(("sums", "rope", "qkT"), _u):
        _steps.setdefault(_at, []).append((_step, _n))
_steps.setdefault(21, []).extend([("av", _h) for _h in range(4)] + [("osq", 0)])
_steps.setdefault(25, [])
for _h in range(DF_H):
    _u = 14 + _h if _h < 4 else 15 + _h
    for _step, _at in (("scores", _u), ("soft", _u + 1), ("aT", _u + 2)):
        _steps.setdefault(_at, []).append((_step, _h))
for _u, _step in ((16, "rope"), (18, "sums"), (18, "qkT")):
    _steps[_u].append((_step, 3))
_steps.setdefault(22, []).append(("osums", 0))
_steps.setdefault(23, []).append(("norm", 0))
_steps.setdefault(24, []).append(("half", 0))
_steps[25].extend([("av", _h) for _h in range(4, DF_H)] + [("osq", 1)])
_steps.setdefault(26, []).append(("osums", 1))
_steps.setdefault(27, []).append(("norm", 1))
_steps.setdefault(28, []).append(("half", 1))
DF_PLAN = plan(DF_IN, 6, _steps)

_steps = {1: [("second", 0)]}
for _h in range(MB_H):
    _u = 12 + _h if _h < 8 else 16 + _h
    _pT = _u + (3 if _h < 12 else 2)
    for _step, _at in (("scores", _u), ("exp", _u + 1), ("pT", _pT), ("av", _pT + (2 if _h < 14 else 1))):
        _steps.setdefault(_at, []).append((_step, _h))
for _n, _u in enumerate(((4, 6, 8), (8, 10, 11), (17, 19, 20), (20, 22, 23))):
    for _step, _at in zip(("sums", "unit", "qkT"), _u):
        _steps.setdefault(_at, []).append((_step, _n))
for _u, _step in ((29, ("z", 0)), (31, ("half", 0)), (34, ("z", 1)), (35, ("half", 1))):
    _steps.setdefault(_u, []).append(_step)
MB_PLAN = plan(MB_IN, 8, _steps)
MB_QK = (0, 1, 3, 4)

C_NORM, C_GLA, C_DF, C_QG, C_KG, C_CONV, N_COLS = 0, 64, 66, 67, 68, 69, 69 + KT * CONV_K
K_ID, K_TRI, K_MASK, K_COS, K_SIN, K_DIST, N_CONST = 0, 128, 384, 640, 768, 896, 896 + 384
R_GQ, R_GK, R_LAM, N_ROWS = 0, 128, 256, 512

T_BANKS = (4, 5, 6, 7)


class Count:

    def __init__(self, sem):
        self.sem, self.value, self.turn, self.rate = sem, {}, None, {}

    def up(self, name, by=1):
        self.value[name] = self.value.get(name, 0) + by
        return self.value[name]

    def wait(self, eng, name, value):
        if self.turn is not None:
            eng.wait_ge(self.sem(name), self.turn * self.rate[name] + value)
        elif value > 0:
            eng.wait_ge(self.sem(name), value)

    def enter(self, turn, rate):
        self.turn, self.rate, self.before = turn, rate, dict(self.value)

    def leave(self, turns):
        for name, value in self.value.items():
            step = value - self.before.get(name, 0)
            assert step in (0, self.rate.get(name, 0)), (name, step)
            self.value[name] = value + step * (turns - 1)
        self.turn = None


def build(nc, stream, x, p, cols_d, rows_d, consts_d, wgate_d, out):
    ctx = ExitStack()
    with ctx:
        def sb(name, shape, dt=F32, scope=ctx):
            return scope.enter_context(nc.sbuf_tensor(name, shape, dt))

        sems = {}

        def sem(name):
            if name not in sems:
                sems[name] = ctx.enter_context(nc.semaphore(name))
            return sems[name]

        bank = [ctx.enter_context(nc.psum_tensor(f"bank{b}", [P, NW], F32)) for b in range(8)]

        raw = sb("raw", [P, RAW, 2 * NW])
        whi = sb("whi", [P, RING, 2 * NW], F32R)
        wlo = sb("wlo", [P, RING, 2 * NW], F32R)
        h = sb("h", [P, TT, D])
        X = (sb("x_hi", [P, KT, SEQ], F32R), sb("x_lo", [P, KT, SEQ], F32R))
        Y = (sb("y_hi", [P, KT, SEQ], F32R), sb("y_lo", [P, KT, SEQ], F32R))
        PT = (sb("p_hi", [P, 2, SEQ], F32R), sb("p_lo", [P, 2, SEQ], F32R))
        p_tok = sb("p_tok", [P, 2, TT, PLE])
        cols = sb("cols", [P, N_COLS])
        consts = sb("consts", [P, N_CONST])
        rows = sb("rows", [P, N_ROWS])
        junk = sb("junk", [P, NW])
        stats = sb("stats", [P, 8, 2, TT])
        ms = sb("ms", [P, 8, 2, TT])
        rstd = sb("rstd", [P, 8, TT])
        neg_half = sb("neg_half", [P, 16])
        rstd_q = sb("rstd_q", [P, TT])
        ident = consts[:, K_ID:K_ID + P]

        def phase():
            return ExitStack()

        s = phase()
        qk_tok = sb("gla_qk_tok", [P, 2, TT, GLA_K], scope=s)
        la = sb("gla_log_a", [P, TT, 2 * GLA_K], scope=s)
        qkT = sb("gla_qkT", [P, 2, GLA_H * SEQ], scope=s)
        qE = sb("gla_qE", [P, 2, GLA_H * SEQ], scope=s)
        kE = sb("gla_kE", [P, 2, GLA_H * SEQ], scope=s)
        gv = sb("gla_v", [P, TT, D], scope=s)
        gr = sb("gla_r", [P, TT, D], scope=s)
        gtmp = sb("gla_tmp", [P, 4, NW], scope=s)
        wg = sb("gla_wgate", [33, 2 * GLA_K], scope=s)
        zt = sb("gla_z_tok", [P, TT, 2 * GLA_R], scope=s)
        zT = sb("gla_zT", [33, SEQ], scope=s)
        decay = sb("gla_decay", [P, 2, GLA_H * 4], scope=s)
        oss = sb("gla_oss", [P, 3, TT * GLA_H], scope=s)
        s.close()
        kD = qk_tok[:, :, :, :].rearrange("p a t n -> p a (t n)")
        kDt = la[:, :, :].rearrange("p t n -> p (t n)").rearrange("p (d t n) -> p d t n", d=2, t=TT)
        probs = qkT[:, 0, :].rearrange("p (t n) -> p t n", t=TT)
        st_even = kE[:, :, :].rearrange("p a n -> p (a n)").rearrange("p (s n) -> p s n", n=GLA_HV)
        st_odd = gtmp[:, :, :].rearrange("p a n -> p (a n)").rearrange("p (s n) -> p s n", n=GLA_HV)
        states = (st_even, st_odd)
        grown = gtmp[:, :, :].rearrange("p (e a) n -> p e (a n)", e=2)

        s = phase()
        M = (sb("mid_hi", [P, FKT, SEQ], F32R, scope=s), sb("mid_lo", [P, FKT, SEQ], F32R, scope=s))
        sg = sb("ffn_silu", [P, 2, TT, 256], scope=s)
        mid = sb("ffn_mid", [P, 2, TT, 256], scope=s)
        s.close()

        s = phase()
        sig = sb("ple_gate", [P, TT, NW], scope=s)
        gated = sb("ple_gated", [P, TT, NW], scope=s)
        s.close()

        s = phase()
        dtok = sb("df_tok", [P, 2, TT, NW], scope=s)
        dsq = sb("df_sq", [P, TT, NW], scope=s)
        dp = sb("df_p", [P, 2, 2, TT, SEQ], scope=s)
        daT = sb("df_aT", [P, 4, NW], scope=s)
        dm2 = sb("df_m2", [P, NW], scope=s)
        dT = sb("df_qkT", [P, 2, DF_H, SEQ], scope=s)
        dv = sb("df_v", [P, TT, D], scope=s)
        do = sb("df_o", [P, TT, D], scope=s)
        rot = sb("df_rot", [P, 2, 2, TT, P], scope=s)
        dss = sb("df_ss", [P, 3, TT * 8], scope=s)
        dqr = sb("df_q_rstd", [P, 2, TT * 8], scope=s)
        dstat = sb("df_stat", [P, DF_H, 16], scope=s)
        lam = sb("df_lam", [P, 8], scope=s)
        s.close()

        s = phase()
        cact = sb("cv_act", [P, 2, TT, 2, P], scope=s)
        cprod = sb("cv_prod", [P, 2, TT, 2, P], scope=s)
        cu = sb("cv_u", [P, 2, SEQ + CONV_K - 1], scope=s)
        cc = sb("cv_c", [P, 4, SEQ], scope=s)
        s.close()

        s = phase()
        mtok = sb("mb_tok", [P, 2, TT, NW], scope=s)
        msq = sb("mb_sq", [P, TT, NW], scope=s)
        mT = sb("mb_qkT", [P, 2, KT, SEQ], scope=s)
        mv = sb("mb_v", [P, TT, D], scope=s)
        mz = sb("mb_z", [P, TT, D], scope=s)
        mgain = sb("mb_gain", [P, 2], scope=s)
        mss = sb("mb_ss", [P, 3, TT * 8], scope=s)
        mstat = sb("mb_stat", [P, 2, 4], scope=s)
        msum = sb("mb_sum", [P, TT, MB_H], scope=s)
        mrec = sb("mb_rec", [P, TT, MB_H], scope=s)
        mo = sb("mb_o", [P, TT, D], scope=s)
        ms2 = sb("mb_s", [P, 2, 3 * P], scope=s)
        mp = sb("mb_p", [P, 4, 3 * P], scope=s)
        mpT = sb("mb_pT", [P, 3, 3 * P], scope=s)
        s.close()

        block = ctx.enter_context(nc.Block())

        def layer(n):
            return (FFN_IN0, FFN_OUT0, PLE0) if n == 0 else (FFN_IN1, FFN_OUT1, PLE1)

        @block.sync
        def _(sp):
            sp.dma_start(h[:, :, :], x.rearrange("(t p) d -> p t d", p=P)).then_inc(sem("x_in"), 16)
            sp.dma_start(consts[:, :], consts_d).then_inc(sem("consts_in"), 16)
            sp.dma_start(cols[:, :], cols_d).then_inc(sem("cols_in"), 16)
            for u in range(RAW):
                sp.dma_start(raw[:, u, :], stream[u]).then_inc(sem(f"raw{u}"), 16)
            sp.dma_start(wg[:, :], wgate_d).then_inc(sem("wg_in"), 16)
            sp.dma_start(p_tok[:, :, :, :], p.rearrange("l (t p) d -> p l t d", p=P)).then_inc(sem("p_in"), 16)
            sp.dma_start(rows[:, :], rows_d.to_broadcast([P, N_ROWS])).then_inc(sem("rows_in"), 16)
            with sp.Fori(1, UNITS // RAW) as i:
                for u in range(RAW):
                    sp.wait_ge(sem("w_lo"), i * RAW + (u - RAW + 1))
                    sp.dma_start(raw[:, u, :], stream[i * RAW + u]).then_inc(sem(f"raw{u}"), 16)
            for n in range(UNITS // RAW * RAW, UNITS):
                sp.wait_ge(sem("w_lo"), n - RAW + 1)
                sp.dma_start(raw[:, n % RAW, :], stream[n]).then_inc(sem(f"raw{n % RAW}"), 16)
            for half in range(2):
                sp.wait_ge(sem("h_new"), 28 + 2 * (half + 1))
                sp.dma_start(out.rearrange("(t p) d -> p t d", p=P)[:, :, half * HALF:(half + 1) * HALF],
                             h[:, :, half * HALF:(half + 1) * HALF]).then_inc(sem("out_done"), 16)
            sp.wait_ge(sem("out_done"), 32)

        @block.gpsimd
        def _(pool):
            c = Count(sem)

            def step(ins):
                ins.then_inc(sem("pool_step"), 1)
                c.wait(pool, "pool_step", c.up("pool_step"))

            def power(src, mean, dst, n, scale, eps=EPS):
                step(nc.gpsimd.tensor_scalar(mean, src, scale, eps, ALU.mult, ALU.add))
                return nc.gpsimd.tensor_tensor(dst, mean, neg_half[:, 0:n], ALU.pow)

            def row_norm(j):
                pool.wait_ge(sem("stats"), 4 * (j + 1))
                nc.gpsimd.tensor_tensor(ms[:, j, 0, :], stats[:, j, 0, :], stats[:, j, 1, :], ALU.add)\
                    .then_inc(sem("pool_step"), 1)
                c.wait(pool, "pool_step", c.up("pool_step"))
                power(ms[:, j, 0, :], ms[:, j, 1, :], rstd[:, j, :], TT, 1.0 / D).then_inc(sem("rstd"), 1)

            nc.gpsimd.memset(neg_half[:, :], -0.5).then_inc(sem("pool_step"), 1)
            c.wait(pool, "pool_step", c.up("pool_step"))
            row_norm(0)
            pool.wait_ge(sem("rstd"), 1)
            nc.gpsimd.tensor_scalar(rstd_q[:, :], rstd[:, 0, :], GLA_HK ** -0.5, None, ALU.mult)\
                .then_inc(sem("rstd_q"), 1)
            pool.wait_ge(sem("gla_sq"), TT * GLA_H)
            power(oss[:, 0, :], oss[:, 1, :], oss[:, 2, :], TT * GLA_H, 1.0 / GLA_HV).then_inc(sem("gla_rstd"), 1)
            for j in (1, 2, 3):
                row_norm(j)
            for m in range(4):
                pool.wait_ge(sem("df_ss"), TT * (m + 1))
                dst, by = (dqr[:, m // 3, :], DF_HD ** 0.5) if m in (0, 3) else (dss[:, 2, :], 1.0)
                power(dss[:, 0, :], dss[:, 1, :], dst, TT * 8, by * by / DF_HD, by * by * EPS)\
                    .then_inc(sem("df_rstd"), 1)
            for g in range(2):
                r0 = dstat[:, 4 * g:4 * g + 4, 12:14].rearrange("p a q -> p q a")
                view = [dss[:, n, 0:8].rearrange("p (q a) -> p q a", q=TT) for n in range(3)]
                pool.wait_ge(sem("df_recip"), 2 * 4 * (g + 1))
                if g == 0:
                    pool.wait_ge(sem("df_rstd"), 4)
                else:
                    pool.wait_ge(sem("df_y"), 1)
                step(nc.gpsimd.tensor_tensor(view[1], r0, r0, ALU.mult))
                pool.wait_ge(sem("df_oss"), TT * (g + 1))
                step(nc.gpsimd.tensor_tensor(view[0], view[0], view[1], ALU.mult))
                by = 1.0 / (1.0 - LAMBDA_INIT)
                step(power(dss[:, 0, 0:8], dss[:, 1, 0:8], dss[:, 2, 0:8], 8, by * by / (2 * DF_HD), by * by * EPS))
                nc.gpsimd.tensor_tensor(view[2], view[2], r0, ALU.mult).then_inc(sem("df_orstd"), 1)
            for j in (4, 5, 6, 7):
                row_norm(j)
            for t in range(4):
                pool.wait_ge(sem("mb_ss"), TT * (t + 1))
                power(mss[:, 0, :], mss[:, 1, :], mss[:, 2, :], TT * 8, 1.0 / MB_HD).then_inc(sem("mb_rstd"), 1)

        @block.scalar
        def _(act):
            c = Count(sem)
            pos = [0]
            A = nc.scalar.activation

            def split_to(end):
                for u in range(pos[0], min(end, UNITS)):
                    c.wait(act, f"raw{u % RAW}", 16 * (u // RAW + 1))
                    if u >= RING:
                        c.wait(act, "w_used", u - RING + 1)
                    w = 256 if u == 0 else 2 * NW
                    A(whi[:, u % RING, 0:w], raw[:, u % RAW, 0:w], ACT.Copy).then_inc(sem("w_hi"), 1)
                pos[0] = max(pos[0], min(end, UNITS))

            def lhs_hi(dst, gain, banks):
                for b in banks:
                    c.wait(act, "lhs_filled", c.up("lhs_filled"))
                    kt = 2 * (b - T_BANKS[0])
                    for k in range(2):
                        scale = 1.0 if gain is None else gain(kt + k)
                        last = A(dst[0][:, kt + k, :], bank[b][:, k * SEQ:(k + 1) * SEQ], ACT.Copy, scale=scale)
                    last.then_inc(sem("lhs_hi"), 1)

            def norm_gain(j):
                return lambda kt: cols[:, C_NORM + j * KT + kt:C_NORM + j * KT + kt + 1]

            def mixer_lhs(j, dst, out):
                split_to(END[out + 4] - 1 + AHEAD + 1)
                lhs_hi(dst, norm_gain(j), (4, 5))
                squares(j, 0)
                split_to(END[out + 4] + 1 + AHEAD)
                lhs_hi(dst, norm_gain(j), (6, 7))
                squares(j, 1)

            def squares(j, half):
                if j:
                    act.wait_ge(sem("h_new"), 4 * (j - 1) + 2 * (half + 1))
                for t in range(TT):
                    c.wait(act, "stats", c.value.get("stats", 0))
                    A(junk[:, :], h[:, t, half * HALF:(half + 1) * HALF], ACT.Square,
                      accum_out=stats[:, j, half, t:t + 1]).then_inc(sem("stats"), 1)
                    c.up("stats")

            def next_lhs(j, dst, tile):
                first = tile + 1
                split_to(END[first] + 2 + AHEAD)
                lhs_hi(dst, norm_gain(j), (4, 5))
                squares(j, 0)
                split_to(END[first + 1] + 1 + AHEAD)
                lhs_hi(dst, norm_gain(j), (6, 7))
                squares(j, 1)

            def evacuate(tile, j, dst, width, signal, func=ACT.Copy, scale=None):
                split_to(END[tile + 1] + AHEAD)
                act.wait_ge(sem("rstd"), j + 1)
                c.wait(act, "w_used", END[tile + 1])
                for t in range(TT):
                    A(dst(t), bank[2 * (tile % 2) + t][:, 0:width], func,
                      scale=(scale if scale is not None else rstd[:, j, :])[:, t:t + 1]).then_inc(sem(signal), 1)

            act.wait_ge(sem("cols_in"), 16)
            act.wait_ge(sem("x_in"), 16)
            lhs_hi(X, norm_gain(0), (4, 5, 6, 7))
            squares(0, 0)
            squares(0, 1)

            evacuate(GLA_IN, 0, lambda t: zt[:, t, :], 2 * GLA_R, "gla_in")
            act.wait_ge(sem("rstd_q"), 1)
            evacuate(GLA_IN + 1, 0, lambda t: qk_tok[:, 0, t, :], NW, "gla_in", scale=rstd_q)
            evacuate(GLA_IN + 2, 0, lambda t: qk_tok[:, 1, t, :], NW, "gla_in")
            for g in range(4):
                act.wait_ge(sem("gla_pre"), g + 1)
                A(gtmp[:, g, :], bank[T_BANKS[g]][:, :], ACT.Abs).then_inc(sem("gla_abs"), 1)
            for g in range(4):
                act.wait_ge(sem("gla_abs"), g + 1)
                A(gtmp[:, g, :], gtmp[:, g, :], ACT.Exp, scale=-1.0).then_inc(sem("gla_expabs"), 1)
            for g in range(4):
                act.wait_ge(sem("gla_expabs"), g + 1)
                A(gtmp[:, g, :], gtmp[:, g, :], ACT.Ln, bias=1.0).then_inc(sem("gla_ln"), 1)
            evacuate(GLA_IN + 3, 0, lambda t: gv[:, t, 0:NW], NW, "gla_in")
            for g in range(4):
                act.wait_ge(sem("gla_qkT_filled"), g + 1)
                A(qkT[:, g // 2, (g % 2) * NW:(g % 2 + 1) * NW], bank[T_BANKS[g]][:, :], ACT.Copy)\
                    .then_inc(sem("gla_qkT"), 1)
            evacuate(GLA_IN + 4, 0, lambda t: gv[:, t, NW:2 * NW], NW, "gla_in")
            for g in range(4):
                act.wait_ge(sem("gla_cum"), g + 1)
                if g == 2:
                    act.wait_ge(sem("gla_gated"), 4)
                for e, sign in enumerate((1.0, -1.0)):
                    A(grown[:, e, (g % 2) * NW:(g % 2 + 1) * NW], bank[T_BANKS[g]][:, :], ACT.Exp, scale=sign)\
                        .then_inc(sem("gla_exp"), 1)
            evacuate(GLA_IN + 5, 0, lambda t: gr[:, t, 0:NW], NW, "gla_in", func=ACT.Silu)
            for g in range(4):
                act.wait_ge(sem("gla_kDt_filled"), g + 1)
                A(kDt[:, g // 2, g % 2, :], bank[T_BANKS[g]][:, :], ACT.Copy).then_inc(sem("gla_kDt"), 1)
            evacuate(GLA_IN + 6, 0, lambda t: gr[:, t, NW:2 * NW], NW, "gla_in", func=ACT.Silu)
            for g in range(4):
                act.wait_ge(sem("gla_head"), 2 * (g // 2) + 2)
                for k in range(2):
                    c.wait(act, "gla_sq", c.value.get("gla_sq", 0))
                    hd = 2 * (g // 2) + k
                    A(junk[:, 0:GLA_HV], bank[2 * (g % 2) + g // 2][:, k * GLA_HV:(k + 1) * GLA_HV], ACT.Square,
                      accum_out=oss[:, 0, (g % 2) * GLA_H + hd:(g % 2) * GLA_H + hd + 1]).then_inc(sem("gla_sq"), 1)
                    c.up("gla_sq")
            lhs_hi(Y, lambda kt: cols[:, C_GLA + kt % 2:C_GLA + kt % 2 + 1], T_BANKS)

            def ffn(n, src):
                tin, tout, tple = layer(n)
                j = 3 * n + 1
                if n == 0:
                    next_lhs(j, src, tin - 2)
                else:
                    mixer_lhs(j, src, tin - 4)

                def tile(t):
                    split_to(END[t + 1] + AHEAD)
                    c.wait(act, "w_used", END[t + 1])
                    for k in range(TT):
                        A(sg[:, (t - tin) % 2, k, :], bank[2 * (t % 2) + k][:, 0:256], ACT.Silu,
                          scale=rstd[:, j, k:k + 1]).then_inc(sem("ffn_silu"), 1)
                        c.up("ffn_silu")

                act.wait_ge(sem("rstd"), j + 1)
                for t in range(tin, tin + 3):
                    tile(t)
                turns = (FT - 5) // 2
                with act.Fori(0, turns) as i:
                    c.enter(i, {"w_used": 8, "w_hi": 8, "ffn_silu": 4, **{f"raw{r}": 32 for r in range(RAW)}})
                    tile(tin + 3)
                    tile(tin + 4)
                    c.leave(turns)
                pos[0] += 8 * (turns - 1)
                for t in range(tin + 3 + 2 * turns, tin + FT):
                    tile(t)
                split_to(END[tout] + 5 + AHEAD)
                act.wait_ge(sem("pT_filled"), n + 1)
                A(PT[0][:, :, :], bank[6][:, :].rearrange("p (k s) -> p k s", k=2), ACT.Copy)\
                    .then_inc(sem("pT_hi"), 1)
                j += 1
                split_to(END[tout + 1] + 2 + AHEAD)
                lhs_hi(src, norm_gain(j), (4, 5))
                squares(j, 0)
                split_to(END[tple] + 1 + AHEAD)
                lhs_hi(src, norm_gain(j), (6, 7))
                squares(j, 1)
                act.wait_ge(sem("rstd"), j + 1)
                for half in range(2):
                    t = tple + 2 * half
                    split_to(END[t + 1] + AHEAD)
                    c.wait(act, "w_used", END[t + 1])
                    if half:
                        act.wait_ge(sem("ple_gated"), TT * (2 * n + 1))
                    for k in range(TT):
                        A(sig[:, k, :], bank[2 * (t % 2) + k][:, :], ACT.Sigmoid, scale=rstd[:, j, k:k + 1])\
                            .then_inc(sem("ple_sig"), 1)
                    if half == 0:
                        split_to(END[t + 2] + 2 + AHEAD)
                        lhs_hi(Y if src is X else X, norm_gain(j + 1), (4, 5))
                        squares(j + 1, 0)
                split_to(END[tple + 4] + 1 + AHEAD)
                lhs_hi(Y if src is X else X, norm_gain(j + 1), (6, 7))
                squares(j + 1, 1)

            ffn(0, X)

            def df_tile(t):
                if t >= 4:
                    evacuate(DF_IN + t, 3, lambda k: dv[:, k, (t - 4) * NW:(t - 3) * NW], NW, "df_in")
                    return
                if t >= 2:
                    act.wait_ge(sem("df_T_filled"), 2 * (t - 1))
                evacuate(DF_IN + t, 3, lambda k: dtok[:, t % 2, k, :], NW, "df_in")
                if t:
                    act.wait_ge(sem("df_ss"), TT * t)
                act.wait_ge(sem("df_in"), TT * (t + 1))
                for k in range(TT):
                    A(dsq[:, k, :], dtok[:, t % 2, k, :], ACT.Square).then_inc(sem("df_sq"), 1)

            def df_qkT(t):
                for b in range(2):
                    act.wait_ge(sem("df_T_filled"), 2 * t + b + 1)
                    hd = 4 * (t // 2) + 2 * b
                    A(dT[:, (0, 1, 1, 0)[t], hd:hd + 2, :], bank[6 + b][:, :].rearrange("p (a s) -> p a s", a=2),
                      ACT.Copy).then_inc(sem("df_T"), 1)

            def df_exp(hd):
                if hd >= 2:
                    act.wait_ge(sem("df_aT_filled"), hd - 1)
                for m in range(2):
                    act.wait_ge(sem("df_max"), 4 * hd + 2 * (m + 1))
                    for q in range(TT):
                        col = q * 8 + 2 * (hd % 4) + m
                        A(dp[:, hd % 2, m, q, :], bank[4 + m][:, q * SEQ:(q + 1) * SEQ], ACT.Exp,
                          scale=dqr[:, hd // 4, col:col + 1], bias=dstat[:, hd, 4 + 2 * m + q:5 + 2 * m + q],
                          accum_out=dstat[:, hd, 8 + 2 * m + q:9 + 2 * m + q]).then_inc(sem("df_exp"), 1)

            def df_copy(hd):
                act.wait_ge(sem("df_aT_filled"), hd + 1)
                if hd >= 4:
                    act.wait_ge(sem("df_av"), hd - 3)
                A(daT[:, hd % 4, :], bank[6][:, :], ACT.Copy).then_inc(sem("df_aT"), 1)

            def df_out(hd):
                act.wait_ge(sem("df_av"), hd + 1)
                A(do[:, :, (hd - 1) * P:(hd + 1) * P], bank[7 - hd // 2 % 2][:, :].rearrange("p (q n) -> p q n", q=TT),
                  ACT.Copy).then_inc(sem("df_o"), 1)

            def df_osq(g):
                act.wait_ge(sem("df_ss"), TT * 4)
                act.wait_ge(sem("df_o"), 2 * (g + 1))
                if g:
                    act.wait_ge(sem("df_oss"), TT * g)
                for q in range(TT):
                    A(dsq[:, q, :], do[:, q, g * NW:(g + 1) * NW], ACT.Square).then_inc(sem("df_osq"), 1)

            act.wait_ge(sem("df_lam"), 2)
            A(lam[:, 2:4], lam[:, 0:2], ACT.Exp).then_inc(sem("df_lamexp"), 1)
            for u, step, arg in DF_PLAN:
                split_to(u + AHEAD + 1)
                if step == "tile":
                    df_tile(arg)
                elif step == "qkT":
                    df_qkT(arg)
                elif step == "scores":
                    df_exp(arg)
                elif step == "aT":
                    df_copy(arg)
                elif step == "av" and arg % 2 == 1:
                    df_out(arg)
                elif step == "osq":
                    df_osq(arg)
                elif step == "half":
                    lhs_hi(X, lambda kt: cols[:, C_DF:C_DF + 1], (4, 5) if arg == 0 else (6, 7))
            ffn(1, Y)

            def conv_tile(t):
                split_to(END[t + 1] + AHEAD)
                c.wait(act, "w_used", END[t + 1])
                for k in range(TT):
                    A(cact[:, (t - CV_IN) % 2, k, 0, :], bank[2 * (t % 2) + k][:, 2 * P:3 * P], ACT.Copy,
                      scale=rstd[:, 6, k:k + 1])
                    A(cact[:, (t - CV_IN) % 2, k, 1, :], bank[2 * (t % 2) + k][:, 3 * P:4 * P], ACT.Silu,
                      scale=rstd[:, 6, k:k + 1]).then_inc(sem("cv_act"), 1)
                    c.up("cv_act")

            act.wait_ge(sem("rstd"), 7)
            for t in range(CV_IN, CV_IN + 3):
                conv_tile(t)
            with act.Fori(0, 2) as i:
                c.enter(i, {"w_used": 8, "w_hi": 8, "cv_act": 4, **{f"raw{r}": 32 for r in range(RAW)}})
                conv_tile(CV_IN + 3)
                conv_tile(CV_IN + 4)
                c.leave(2)
            pos[0] += 8
            conv_tile(CV_IN + 7)
            next_lhs(7, X, CV_OUT)

            def mb_tile(t):
                m = MB_QK.index(t) if t in MB_QK else None
                if m is not None:
                    if m >= 2:
                        act.wait_ge(sem("mb_T_filled"), 2 * (m - 1))
                    evacuate(MB_IN + t, 7, lambda k: mtok[:, m % 2, k, :], NW, "mb_in")
                    if m:
                        act.wait_ge(sem("mb_ss"), TT * m)
                    act.wait_ge(sem("mb_in"), TT * (t + 1))
                    for k in range(TT):
                        A(msq[:, k, :], mtok[:, m % 2, k, :], ACT.Square).then_inc(sem("mb_sq"), 1)
                elif t < 6:
                    evacuate(MB_IN + t, 7, lambda k: mv[:, k, t // 3 * NW:(t // 3 + 1) * NW], NW, "mb_in")
                else:
                    evacuate(MB_IN + t, 7, lambda k: mz[:, k, (t - 6) * NW:(t - 5) * NW], NW, "mb_in",
                             func=ACT.Silu)

            def mb_qkT(m):
                for b in range(2):
                    act.wait_ge(sem("mb_T_filled"), 2 * m + b + 1)
                    blk = 4 * (m // 2) + 2 * b
                    A(mT[:, m % 2, blk:blk + 2, :], bank[4 + b][:, :].rearrange("p (a s) -> p a s", a=2),
                      ACT.Copy, scale=mgain[:, m % 2:m % 2 + 1]).then_inc(sem("mb_T"), 1)

            def mb_exp(hd):
                act.wait_ge(sem("mb_max"), hd + 1)
                if hd >= 4:
                    act.wait_ge(sem("mb_pT_filled"), hd - 3)
                for q in range(TT):
                    lo, hi = (0, P) if q == 0 else (P, 3 * P)
                    A(mp[:, hd % 4, lo:hi], ms2[:, hd % 2, lo:hi], ACT.Exp, bias=mstat[:, hd % 2, 2 + q:3 + q],
                      accum_out=msum[:, q, hd:hd + 1]).then_inc(sem("mb_exp"), 1)

            def mb_copy(hd):
                act.wait_ge(sem("mb_pT_filled"), hd + 1)
                if hd >= 3:
                    act.wait_ge(sem("mb_av"), hd - 2)
                A(mpT[:, hd % 3, :], bank[6][:, 0:3 * P], ACT.Copy).then_inc(sem("mb_pT"), 1)

            act.wait_ge(sem("mb_gain"), 1)
            for u, step, arg in MB_PLAN:
                split_to(u + AHEAD + 1)
                if step == "tile":
                    mb_tile(arg)
                elif step == "qkT":
                    mb_qkT(arg)
                elif step == "exp":
                    mb_exp(arg)
                elif step == "pT":
                    mb_copy(arg)
                elif step == "half":
                    lhs_hi(Y, None, (4, 5) if arg == 0 else (6, 7))
            split_to(UNITS)

        @block.vector
        def _(dve):
            c = Count(sem)
            pos = [0]
            V = nc.vector

            def split_to(end):
                for u in range(pos[0], min(end, UNITS)):
                    c.wait(dve, "w_hi", u + 1)
                    w = 256 if u == 0 else 2 * NW
                    V.tensor_tensor(wlo[:, u % RING, 0:w], raw[:, u % RAW, 0:w],
                                    whi[:, u % RING, 0:w].bitcast(F32), ALU.subtract).then_inc(sem("w_lo"), 1)
                pos[0] = max(pos[0], min(end, UNITS))

            def lhs_lo(dst, gain, banks):
                for b in banks:
                    c.wait(dve, "lhs_hi", c.up("lhs_hi"))
                    kt = 2 * (b - T_BANKS[0])
                    if gain is None:
                        V.tensor_tensor(dst[1][:, kt:kt + 2, :], bank[b][:, :].rearrange("p (k s) -> p k s", k=2),
                                        dst[0][:, kt:kt + 2, :].bitcast(F32), ALU.subtract)\
                            .then_inc(sem("lhs"), 1)
                        continue
                    for k in range(2):
                        last = V.scalar_tensor_tensor(dst[1][:, kt + k, :], bank[b][:, k * SEQ:(k + 1) * SEQ],
                                                      gain(kt + k), dst[0][:, kt + k, :].bitcast(F32),
                                                      ALU.mult, ALU.subtract)
                    last.then_inc(sem("lhs"), 1)

            def norm_gain(j):
                return lambda kt: cols[:, C_NORM + j * KT + kt:C_NORM + j * KT + kt + 1]

            def residual(tile, half):
                split_to(END[tile + 1] + AHEAD - 2)
                c.wait(dve, "w_used", END[tile + 1])
                for t in range(TT):
                    V.tensor_tensor(h[:, t, half * HALF:(half + 1) * HALF], h[:, t, half * HALF:(half + 1) * HALF],
                                    bank[2 * (tile % 2) + t][:, :], ALU.add).then_inc(sem("h_new"), 1)

            def mixer_out(tile, j, dst):
                residual(tile, 0)
                split_to(END[tile + 1] + 2 + AHEAD)
                lhs_lo(dst, norm_gain(j), (4, 5))
                residual(tile + 1, 1)
                split_to(END[tile + 2] + 1 + AHEAD)
                lhs_lo(dst, norm_gain(j), (6, 7))

            def parts_out(out, j, dst):
                residual(out + 2, 0)
                split_to(END[out + 4] - 1 + AHEAD)
                lhs_lo(dst, norm_gain(j), (4, 5))
                residual(out + 3, 1)
                split_to(END[out + 4] + 1 + AHEAD)
                lhs_lo(dst, norm_gain(j), (6, 7))

            dve.wait_ge(sem("cols_in"), 16)
            lhs_lo(X, norm_gain(0), T_BANKS)
            V.memset(zT[32:33, :], 1.0).then_inc(sem("gla_ones"), 1)

            split_to(END[2] + AHEAD)
            dve.wait_ge(sem("gla_zT_filled"), 1)
            V.tensor_copy(zT[0:32, :], bank[4][0:32, 0:SEQ]).then_inc(sem("gla_zT"), 1)
            split_to(END[3] + AHEAD)
            for g in range(4):
                dve.wait_ge(sem("gla_ln"), g + 1)
                V.scalar_tensor_tensor(la[:, g % 2, (g // 2) * GLA_K:(g // 2 + 1) * GLA_K], bank[T_BANKS[g]][:, :],
                                       0.0, gtmp[:, g, :], ALU.min, ALU.subtract).then_inc(sem("gla_la"), 1)
            split_to(END[5] + AHEAD)
            dve.wait_ge(sem("gla_qkT"), 4)
            for d in range(2):
                dve.wait_ge(sem("gla_exp"), 4 * (d + 1))
                V.tensor_tensor(qE[:, d, :], qkT[:, 0, :], grown[:, 0, :], ALU.mult).then_inc(sem("gla_gated"), 1)
                V.tensor_tensor(kE[:, d, :], qkT[:, 1, :], grown[:, 1, :], ALU.mult).then_inc(sem("gla_gated"), 1)
                edge = GLA_C - 1 if d == 0 else 0
                V.tensor_copy(decay[:, d, :], grown[:, 0, :].rearrange("p (a i) -> p a i", i=GLA_C)[:, :, edge])\
                    .then_inc(sem("gla_gated"), 1)
                dve.wait_ge(sem("gla_gated"), 4 * d + 3)
                V.tensor_tensor(kD[:, d, :].rearrange("p (a i) -> p a i", i=GLA_C),
                                kE[:, d, :].rearrange("p (a i) -> p a i", i=GLA_C),
                                decay[:, d, :].unsqueeze(2).to_broadcast([P, GLA_H * 4, GLA_C]), ALU.mult)\
                    .then_inc(sem("gla_gated"), 1)
            V.memset(probs, 0.0).then_inc(sem("gla_zero"), 1)
            split_to(END[7] + AHEAD - 2)
            dve.wait_ge(sem("gla_zero"), 1)
            for g in range(4):
                dve.wait_ge(sem("gla_scores"), g + 1)
                if g >= 2:
                    dve.wait_ge(sem("gla_probs"), g - 1)
                d, t = divmod(g, 2)
                mask = consts[:, K_MASK + d * P:K_MASK + (d + 1) * P].bitcast(U32).unsqueeze(1)\
                    .to_broadcast([P, GLA_H, P])
                V.copy_predicated(probs[:, t, :].rearrange("p (a i) -> p a i", a=GLA_H), mask,
                                  bank[T_BANKS[g]][:, :].rearrange("p (a i) -> p a i", a=GLA_H))\
                    .then_inc(sem("gla_probs"), 1)
            for hd in range(GLA_H):
                st = states[hd % 2]

                def dec(d, ch, hd=hd):
                    return decay[:, d, hd * 4 + ch:hd * 4 + ch + 1]
                base = 6 * hd
                dve.wait_ge(sem("gla_u"), 4 * (hd + 1))
                if hd >= 2:
                    dve.wait_ge(sem("gla_head"), hd - 1)
                V.tensor_copy(st[:, 0, :], bank[4][:, 0:256]).then_inc(sem("gla_state"), 1)
                V.tensor_copy(st[:, 3, :], bank[7][:, 0:256]).then_inc(sem("gla_state"), 1)
                dve.wait_ge(sem("gla_state"), base + 1)
                V.scalar_tensor_tensor(st[:, 1, :], st[:, 0, :], dec(0, 1), bank[6][:, 0:256], ALU.mult, ALU.add)\
                    .then_inc(sem("gla_state"), 1)
                dve.wait_ge(sem("gla_state"), base + 2)
                V.scalar_tensor_tensor(st[:, 4, :], st[:, 3, :], dec(1, 2), bank[5][:, 0:256], ALU.mult, ALU.add)\
                    .then_inc(sem("gla_state"), 1)
                dve.wait_ge(sem("gla_state"), base + 3)
                V.scalar_tensor_tensor(st[:, 2, :], st[:, 1, :], dec(0, 2), bank[4][:, 256:512], ALU.mult, ALU.add)\
                    .then_inc(sem("gla_state"), 1)
                dve.wait_ge(sem("gla_state"), base + 4)
                V.scalar_tensor_tensor(st[:, 5, :], st[:, 4, :], dec(1, 1), bank[6][:, 256:512], ALU.mult, ALU.add)\
                    .then_inc(sem("gla_state"), 1)
            dve.wait_ge(sem("gla_rstd"), 1)
            dve.wait_ge(sem("gla_in"), 14)
            for g in range(4):
                for k in range(2):
                    hd, t = 2 * (g // 2) + k, g % 2
                    V.scalar_tensor_tensor(gr[:, t, hd * GLA_HV:(hd + 1) * GLA_HV],
                                           bank[2 * t + g // 2][:, k * GLA_HV:(k + 1) * GLA_HV],
                                           oss[:, 2, t * GLA_H + hd:t * GLA_H + hd + 1],
                                           gr[:, t, hd * GLA_HV:(hd + 1) * GLA_HV], ALU.mult, ALU.mult)\
                        .then_inc(sem("gla_y"), 1)
            lhs_lo(Y, lambda kt: cols[:, C_GLA + kt % 2:C_GLA + kt % 2 + 1], T_BANKS)
            mixer_out(GLA_OUT, 1, X)

            def ffn(n, src):
                tin, tout, tple = layer(n)
                j = 3 * n + 1

                def product(t):
                    split_to(END[t + 1] + AHEAD)
                    for k in range(TT):
                        c.wait(dve, "ffn_silu", c.up("ffn_silu"))
                        V.scalar_tensor_tensor(mid[:, (t - tin) % 2, k, :], bank[2 * (t % 2) + k][:, 256:512],
                                               rstd[:, j, k:k + 1], sg[:, (t - tin) % 2, k, :],
                                               ALU.mult, ALU.mult).then_inc(sem("ffn_mid"), 1)

                def parts(t, kt, at):
                    b = T_BANKS[(t - tin) % 2]
                    src_ap = bank[b][:, :].rearrange("p (k s) -> p k s", k=2)
                    split_to(at + AHEAD)
                    c.wait(dve, "ffn_T_filled", c.up("ffn_T_filled"))
                    V.tensor_scalar(M[0][:, bass.ds(kt, 2), :], src_ap, 1.0, None, ALU.mult)\
                        .then_inc(sem("ffn_hi"), 1)
                    c.wait(dve, "ffn_hi", c.up("ffn_hi"))
                    V.tensor_tensor(M[1][:, bass.ds(kt, 2), :], src_ap, M[0][:, bass.ds(kt, 2), :].bitcast(F32),
                                    ALU.subtract).then_inc(sem("ffn_lhs"), 1)

                product(tin)
                for t in range(tin + 1, tin + 3):
                    parts(t - 1, 2 * (t - 1 - tin), END[t] + 2)
                    product(t)
                turns = (FT - 5) // 2
                with dve.Fori(0, turns) as i:
                    c.enter(i, {"w_hi": 8, "w_lo": 8, "ffn_silu": 4, "ffn_mid": 4, "ffn_T_filled": 2, "ffn_hi": 2,
                                "ffn_lhs": 2})
                    for t in (tin + 3, tin + 4):
                        parts(t - 1, i * 4 + 2 * (t - 1 - tin), END[t] + 2)
                        product(t)
                    c.leave(turns)
                pos[0] += 8 * (turns - 1)
                for t in range(tin + 3 + 2 * turns, tin + FT):
                    parts(t - 1, 2 * (t - 1 - tin), END[t] + 2)
                    product(t)
                parts(tin + FT - 1, FKT - 2, END[tout] + 2)
                split_to(END[tout] + 5 + AHEAD)
                dve.wait_ge(sem("pT_hi"), n + 1)
                V.tensor_tensor(PT[1][:, :, :], bank[6][:, :].rearrange("p (k s) -> p k s", k=2),
                                PT[0][:, :, :].bitcast(F32), ALU.subtract).then_inc(sem("pT"), 1)
                j += 1
                mixer_out(tout, j, src)
                for half in range(2):
                    t = tple + 2 * half
                    split_to(END[t + 2] + AHEAD - 2)
                    dve.wait_ge(sem("ple_sig"), TT * (2 * n + half + 1))
                    c.wait(dve, "w_used", END[t + 2])
                    for k in range(TT):
                        V.tensor_tensor(gated[:, k, :], sig[:, k, :], bank[2 * ((t + 1) % 2) + k][:, :], ALU.mult)\
                            .then_inc(sem("ple_gated"), 1)
                    for k in range(TT):
                        dve.wait_ge(sem("ple_gated"), TT * (2 * n + half) + k + 1)
                        V.tensor_tensor(h[:, k, half * HALF:(half + 1) * HALF], h[:, k, half * HALF:(half + 1) * HALF],
                                        gated[:, k, :], ALU.add).then_inc(sem("h_new"), 1)
                    split_to(END[t + 2] + (2 if half == 0 else 1) + AHEAD)
                    lhs_lo(Y if src is X else X, norm_gain(j + 1), (4, 5) if half == 0 else (6, 7))

            ffn(0, X)

            dve.wait_ge(sem("rows_in"), 16)
            cos = consts[:, K_COS:K_COS + 2 * DF_HD].rearrange("p (t e) -> p t e", t=TT)
            sin = consts[:, K_SIN:K_SIN + 2 * DF_HD].rearrange("p (t e) -> p t e", t=TT)
            HD2 = DF_HD // 2
            for w in range(2):
                for m in range(2):
                    g = rows[:, (R_GQ, R_GK)[w] + m * DF_HD:(R_GQ, R_GK)[w] + (m + 1) * DF_HD]
                    lo, hi = m * DF_HD, (m + 1) * DF_HD
                    V.tensor_tensor(rot[:, w, 0, :, lo:hi], cos, g.unsqueeze(1).to_broadcast([P, TT, DF_HD]), ALU.mult)
                    V.tensor_tensor(rot[:, w, 1, :, lo:lo + HD2], sin[:, :, 0:HD2],
                                    g[:, HD2:DF_HD].unsqueeze(1).to_broadcast([P, TT, HD2]), ALU.mult)
                    V.tensor_tensor(rot[:, w, 1, :, lo + HD2:hi], sin[:, :, HD2:DF_HD],
                                    g[:, 0:HD2].unsqueeze(1).to_broadcast([P, TT, HD2]), ALU.mult)\
                        .then_inc(sem("df_rot"), 1)
            lrow = rows[:, R_LAM:R_LAM + 4 * DF_HD].rearrange("p (a b e) -> p a b e", a=2, b=2)
            V.tensor_tensor(do[:, 0, 0:2 * DF_HD].rearrange("p (a e) -> p a e", a=2),
                            lrow[:, :, 0, :], lrow[:, :, 1, :], ALU.mult).then_inc(sem("df_lam"), 1)
            dve.wait_ge(sem("df_lam"), 1)
            V.tensor_reduce(lam[:, 0:2], do[:, 0, 0:2 * DF_HD].rearrange("p (a e) -> p a e", a=2), AXX, ALU.add)\
                .then_inc(sem("df_lam"), 1)

            def head_sums(t, sq, ss, sig_sq, sig_ss, sig_rstd):
                if t:
                    dve.wait_ge(sem(sig_rstd), t)
                dve.wait_ge(sem(sig_sq), TT * (t + 1))
                for k in range(TT):
                    V.tensor_reduce(ss[:, 0, k * 8:(k + 1) * 8], sq[:, k, :].rearrange("p (a e) -> p a e", a=8),
                                    AXX, ALU.add).then_inc(sem(sig_ss), 1)

            def head_unit(t, tok, ss, sig_rstd, signal):
                dve.wait_ge(sem(sig_rstd), t + 1)
                for k in range(TT):
                    x3 = tok[:, t % 2, k, :].rearrange("p (a e) -> p a e", a=8)
                    V.tensor_tensor(x3, x3, ss[:, 2, k * 8:(k + 1) * 8].unsqueeze(2).to_broadcast([P, 8, NW // 8]),
                                    ALU.mult).then_inc(sem(signal), 1)

            def df_rope(t):
                w = (0, 1, 1, 0)[t]
                if w:
                    head_unit(t, dtok, dss, "df_rstd", "df_unit")
                else:
                    dve.wait_ge(sem("df_sq"), TT * (t + 1))
                for k in range(TT):
                    xt = dtok[:, t % 2, k, :]
                    x4 = xt.rearrange("p (a u e) -> p a u e", a=8, u=2)
                    m4 = dm2[:, :].rearrange("p (a u e) -> p a u e", a=8, u=2)
                    sn = rot[:, w, 1, k, :].rearrange("p (m u e) -> p m u e", m=2, u=2)
                    if w:
                        dve.wait_ge(sem("df_unit"), TT * (t - 1) + k + 1)
                    for u in range(2):
                        for m in range(2):
                            last = V.tensor_tensor(m4[:, m:8:2, u, :], x4[:, m:8:2, 1 - u, :],
                                                   sn[:, m, u, :].unsqueeze(1).to_broadcast([P, 4, HD2]), ALU.mult)
                    last.then_inc(sem("df_swap"), 1)
                    dve.wait_ge(sem("df_swap"), TT * t + k + 1)
                    V.tensor_tensor(xt.rearrange("p (a e) -> p a e", a=4), xt.rearrange("p (a e) -> p a e", a=4),
                                    rot[:, w, 0, k, :].unsqueeze(1).to_broadcast([P, 4, P]), ALU.mult)\
                        .then_inc(sem("df_cos"), 1)
                    dve.wait_ge(sem("df_cos"), TT * t + k + 1)
                    V.tensor_tensor(xt, xt, dm2[:, :], ALU.add).then_inc(sem("df_rope"), 1)
                    dve.wait_ge(sem("df_rope"), TT * t + k + 1)

            def df_lambda():
                dve.wait_ge(sem("df_lamexp"), 1)
                V.tensor_tensor(lam[:, 4:5], lam[:, 3:4], lam[:, 2:3], ALU.subtract).then_inc(sem("df_lam"), 1)
                dve.wait_ge(sem("df_lam"), 3)
                V.tensor_scalar(lam[:, 5:6], lam[:, 4:5], LAMBDA_INIT, None, ALU.subtract).then_inc(sem("df_lam"), 1)
                dve.wait_ge(sem("df_lam"), 4)

            def df_max(hd):
                stt = dstat[:, hd, :]
                factors = dqr[:, hd // 4, :].rearrange("p (q a m) -> p q a m", q=TT, a=4)
                if hd % 4 == 0:
                    dve.wait_ge(sem("df_rstd"), (1, 4)[hd // 4])
                for m in range(2):
                    dve.wait_ge(sem("df_scores"), 2 * hd + m + 1)
                    V.tensor_reduce(stt[:, 2 * m:2 * m + 2], bank[4 + m][:, :].rearrange("p (q k) -> p q k", q=TT),
                                    AXX, ALU.max).then_inc(sem("df_max"), 1)
                    dve.wait_ge(sem("df_max"), 4 * hd + 2 * m + 1)
                    V.scalar_tensor_tensor(stt[:, 4 + 2 * m:6 + 2 * m], stt[:, 2 * m:2 * m + 2], -1.0,
                                           factors[:, :, hd % 4, m], ALU.mult, ALU.mult).then_inc(sem("df_max"), 1)

            def df_soft(hd):
                stt = dstat[:, hd, :]
                dve.wait_ge(sem("df_exp"), 4 * (hd + 1))
                V.reciprocal(stt[:, 12:16], stt[:, 8:12]).then_inc(sem("df_recip"), 1)
                dve.wait_ge(sem("df_recip"), 2 * hd + 1)
                V.scalar_tensor_tensor(stt[:, 0:2], stt[:, 14:16], lam[:, 5:6], stt[:, 8:10], ALU.mult, ALU.mult)\
                    .then_inc(sem("df_recip"), 1)
                dve.wait_ge(sem("df_recip"), 2 * hd + 2)
                for q in range(TT):
                    V.scalar_tensor_tensor(dp[:, hd % 2, 0, q, :], dp[:, hd % 2, 1, q, :], stt[:, q:q + 1],
                                           dp[:, hd % 2, 0, q, :], ALU.mult, ALU.add).then_inc(sem("df_a"), 1)

            def df_osums(g):
                dve.wait_ge(sem("df_osq"), TT * (g + 1))
                dve.wait_ge(sem("df_rstd"), 4)
                if g:
                    dve.wait_ge(sem("df_orstd"), g)
                for q in range(TT):
                    V.tensor_reduce(dss[:, 0, q * 4:(q + 1) * 4], dsq[:, q, :].rearrange("p (a e) -> p a e", a=4),
                                    AXX, ALU.add).then_inc(sem("df_oss"), 1)

            def df_y(g):
                dve.wait_ge(sem("df_orstd"), g + 1)
                o4 = do[:, :, g * NW:(g + 1) * NW].rearrange("p q (a e) -> p q a e", a=4)
                f4 = dss[:, 2, 0:8].rearrange("p (q a) -> p q a", q=TT)
                V.tensor_tensor(o4, o4, f4.unsqueeze(3).to_broadcast([P, TT, 4, P]), ALU.mult)\
                    .then_inc(sem("df_y"), 1)

            dve.wait_ge(sem("df_rot"), 4)
            df_lambda()
            for u, step, arg in DF_PLAN:
                split_to(u + AHEAD)
                if step == "sums":
                    head_sums(arg, dsq, dss, "df_sq", "df_ss", "df_rstd")
                elif step == "rope":
                    df_rope(arg)
                elif step == "scores":
                    df_max(arg)
                elif step == "soft":
                    df_soft(arg)
                elif step == "osums":
                    df_osums(arg)
                elif step == "norm":
                    df_y(arg)
                elif step == "half":
                    lhs_lo(X, lambda kt: cols[:, C_DF:C_DF + 1], (4, 5) if arg == 0 else (6, 7))
            parts_out(DF_OUT, 4, Y)
            ffn(1, Y)

            V.memset(cu[:, :, 0:CONV_K - 1], 0.0).then_inc(sem("cv_pad"), 1)

            def conv_product(t):
                split_to(END[t + 1] + AHEAD)
                for k in range(TT):
                    c.wait(dve, "cv_act", c.up("cv_act"))
                    for m in range(2):
                        src = bank[2 * (t % 2) + k][:, (1 - m) * P:(2 - m) * P]
                        last = V.scalar_tensor_tensor(cprod[:, (t - CV_IN) % 2, k, m, :], src, rstd[:, 6, k:k + 1],
                                                      cact[:, (t - CV_IN) % 2, k, m, :], ALU.mult, ALU.mult)
                    last.then_inc(sem("cv_prod"), 1)

            def conv_parts(t, blk, at):
                par = (t - CV_IN) % 2
                b = T_BANKS[par]
                split_to(at + AHEAD)
                c.wait(dve, "cv_T_filled", c.up("cv_T_filled"))

                def tap(k):
                    return cols[:, bass.ds(blk * CONV_K + (C_CONV + k), 1)]

                def step(ins):
                    ins.then_inc(sem("cv_step"), 1)
                    c.wait(dve, "cv_step", c.up("cv_step"))

                step(V.tensor_copy(cu[:, par, CONV_K - 1:], bank[b][:, 0:SEQ]))
                step(V.tensor_scalar(cc[:, 0, :], cu[:, par, 0:SEQ], tap(0), None, ALU.mult))
                step(V.scalar_tensor_tensor(cc[:, 1, :], cu[:, par, 1:SEQ + 1], tap(1), cc[:, 0, :],
                                            ALU.mult, ALU.add))
                step(V.scalar_tensor_tensor(cc[:, 2, :], cu[:, par, 2:SEQ + 2], tap(2), cc[:, 1, :],
                                            ALU.mult, ALU.add))
                step(V.tensor_tensor(cc[:, 3, :], cc[:, 2, :], bank[b][:, SEQ:2 * SEQ], ALU.mult))
                step(V.tensor_scalar(Y[0][:, bass.ds(blk, 1), :], cc[:, 3, :].unsqueeze(1), 1.0, None, ALU.mult))
                V.tensor_tensor(Y[1][:, bass.ds(blk, 1), :], cc[:, 3, :].unsqueeze(1),
                                Y[0][:, bass.ds(blk, 1), :].bitcast(F32), ALU.subtract).then_inc(sem("cv_lhs"), 1)

            dve.wait_ge(sem("cv_pad"), 1)
            conv_product(CV_IN)
            for t in range(CV_IN + 1, CV_IN + 3):
                conv_parts(t - 1, t - 1 - CV_IN, END[t] + 2)
                conv_product(t)
            with dve.Fori(0, 2) as i:
                c.enter(i, {"w_hi": 8, "w_lo": 8, "cv_act": 4, "cv_prod": 4, "cv_T_filled": 2, "cv_step": 12,
                            "cv_lhs": 2})
                for t in (CV_IN + 3, CV_IN + 4):
                    conv_parts(t - 1, i * 2 + (t - 1 - CV_IN), END[t] + 2)
                    conv_product(t)
                c.leave(2)
            pos[0] += 8
            conv_parts(CV_IN + 6, 6, END[CV_IN + 7] + 2)
            conv_product(CV_IN + 7)
            conv_parts(CV_IN + 7, 7, END[CV_OUT] + 2)
            mixer_out(CV_OUT, 7, X)

            V.tensor_scalar(mgain[:, 0:1], cols[:, C_QG:C_QG + 1], MB_HD ** -0.5, None, ALU.mult)
            V.tensor_copy(mgain[:, 1:2], cols[:, C_KG:C_KG + 1]).then_inc(sem("mb_gain"), 1)

            def mb_max(hd):
                slope = 2.0 ** (-8.0 * (hd + 1) / MB_H)
                dve.wait_ge(sem("mb_scores"), hd + 1)
                if hd >= 2:
                    dve.wait_ge(sem("mb_exp"), TT * (hd - 1))
                V.scalar_tensor_tensor(ms2[:, hd % 2, 0:3 * P], consts[:, K_DIST:K_DIST + 3 * P], slope,
                                       bank[4 + hd % 2][:, 0:3 * P], ALU.mult, ALU.add)\
                    .then_inc(sem("mb_biased"), 1)
                dve.wait_ge(sem("mb_biased"), hd + 1)
                V.tensor_reduce(mstat[:, hd % 2, 0:1], ms2[:, hd % 2, 0:P], AXX, ALU.max)
                V.tensor_reduce(mstat[:, hd % 2, 1:2], ms2[:, hd % 2, P:3 * P], AXX, ALU.max)\
                    .then_inc(sem("mb_rowmax"), 1)
                dve.wait_ge(sem("mb_rowmax"), hd + 1)
                V.tensor_scalar(mstat[:, hd % 2, 2:4], mstat[:, hd % 2, 0:2], -1.0, None, ALU.mult)\
                    .then_inc(sem("mb_max"), 1)

            def mb_o(hd):
                g = hd // 4
                dve.wait_ge(sem("mb_exp"), TT * (hd + 1))
                V.reciprocal(mrec[:, :, 4 * g:4 * g + 4], msum[:, :, 4 * g:4 * g + 4]).then_inc(sem("mb_recip"), 1)
                dve.wait_ge(sem("mb_recip"), g + 1)
                dve.wait_ge(sem("mb_av"), hd + 1)
                V.tensor_tensor(mo[:, :, g * SEQ:(g + 1) * SEQ].rearrange("p q (a e) -> p q a e", a=4),
                                bank[7][:, :].rearrange("p (q a e) -> p q a e", q=TT, a=4),
                                mrec[:, :, 4 * g:4 * g + 4].unsqueeze(3).to_broadcast([P, TT, 4, MB_HD]), ALU.mult)\
                    .then_inc(sem("mb_o"), 1)

            def mb_y(g):
                dve.wait_ge(sem("mb_o"), 2 * (g + 1))
                dve.wait_ge(sem("mb_in"), TT * (7 + g))
                V.tensor_tensor(mz[:, :, g * NW:(g + 1) * NW], mz[:, :, g * NW:(g + 1) * NW],
                                mo[:, :, g * NW:(g + 1) * NW], ALU.mult).then_inc(sem("mb_y"), 1)

            for u, step, arg in MB_PLAN:
                split_to(u + AHEAD)
                if step == "sums":
                    head_sums(arg, msq, mss, "mb_sq", "mb_ss", "mb_rstd")
                elif step == "unit":
                    head_unit(arg, mtok, mss, "mb_rstd", "mb_unit")
                elif step == "scores":
                    mb_max(arg)
                elif step == "av" and arg % 4 == 3:
                    mb_o(arg)
                elif step == "z":
                    mb_y(arg)
                elif step == "half":
                    lhs_lo(Y, None, (4, 5) if arg == 0 else (6, 7))
            split_to(UNITS)
            residual(MB_OUT + 2, 0)
            residual(MB_OUT + 3, 1)

        @block.tensor
        def _(pe):
            c = Count(sem)
            T = nc.tensor
            free = {}

            def claim(b):
                if b in free:
                    c.wait(pe, *free[b])

            def product(tile, lhs, signal, kt0=0, need=None, hooks=(), width=NW, by=1, beside=None, part=None):
                pair = 2 * (tile % 2)
                hooks = dict(hooks)
                n = TILES[tile]
                for k in range(n):
                    if beside is not None:
                        beside(END[tile] + k)
                    if k in hooks:
                        hooks[k]()
                    if k == 0 and part != 1:
                        claim(pair)
                        claim(pair + 1)
                    if need is not None and need[kt0 // 2 + k] is not None:
                        c.wait(pe, *need[kt0 // 2 + k])
                    u = END[tile] + k
                    c.wait(pe, "w_lo", u + 1)
                    each = 2 if width == NW else KT
                    for t in range(TT):
                        for kk in range(each):
                            kt = kt0 + 2 * k + kk
                            for i, (a, w) in enumerate(((0, whi), (0, wlo), (1, whi))):
                                last = T.matmul(bank[pair + t][:, 0:width],
                                                lhs[a][:, kt, t * P:(t + 1) * P],
                                                w[:, u % RING, kk * width:(kk + 1) * width],
                                                start=part != 1 and k == kk == i == 0,
                                                stop=part != 0 and k == n - 1 and kk == each - 1 and i == 2)
                    last.then_inc(sem("w_used"), 1)
                if signal is not None:
                    for t in range(TT):
                        free[pair + t] = (signal, c.up(signal, by))

            def lhs_T(src, banks):
                need = []
                for b in banks:
                    claim(b)
                    for k in range(2):
                        for t in range(TT):
                            kt = 2 * (b - T_BANKS[0]) + k
                            last = T.transpose(bank[b][:, k * SEQ + t * P:k * SEQ + (t + 1) * P],
                                               src[:, t, kt * P:(kt + 1) * P], ident)
                    last.then_inc(sem("lhs_filled"), 1)
                    free[b] = ("lhs", c.up("lhs"))
                    need.append(free[b])
                return need

            def h_T(half, version):
                pe.wait_ge(sem("h_new"), 4 * (version - 1) + 2 * (half + 1))
                return lhs_T(h, (4, 5) if half == 0 else (6, 7))

            def parts(tile, lhs, need, beside, version=None):
                got = []
                for part in range(2):
                    for t in range(2):
                        hooks = [(1, lambda: got.extend(h_T(0, version)))] if version and part == t == 1 else ()
                        product(tile + 2 * part + t, lhs, "h_new" if part else None, kt0=4 * part, part=part,
                                need=need if t == 0 else None, beside=beside, hooks=hooks)
                return got

            def chained(tile, lhs, signal, version, need=None, hooks=()):
                got = []
                product(tile, lhs, signal, need=need, hooks=hooks)
                product(tile + 1, lhs, signal, hooks=[(2, lambda: got.extend(h_T(0, version)))])
                return got

            pe.wait_ge(sem("consts_in"), 16)
            pe.wait_ge(sem("x_in"), 16)
            need = lhs_T(h, T_BANKS)

            def z_T():
                pe.wait_ge(sem("gla_in"), 2)
                claim(4)
                for t in range(TT):
                    last = T.transpose(bank[4][0:32, t * P:(t + 1) * P], zt[:, t, :], ident)
                last.then_inc(sem("gla_zT_filled"), 1)
                free[4] = ("gla_zT", 1)

            def pre_gates():
                pe.wait_ge(sem("gla_zT"), 1)
                pe.wait_ge(sem("gla_ones"), 1)
                pe.wait_ge(sem("wg_in"), 16)
                for g in range(4):
                    claim(T_BANKS[g])
                    T.matmul(bank[T_BANKS[g]][:, :], zT[0:33, (g % 2) * P:(g % 2 + 1) * P],
                             wg[0:33, (g // 2) * GLA_K:(g // 2 + 1) * GLA_K], start=True, stop=True)\
                        .then_inc(sem("gla_pre"), 1)
                    free[T_BANKS[g]] = ("gla_la", g + 1)

            def qk_T():
                pe.wait_ge(sem("gla_in"), 6)
                for g in range(4):
                    claim(T_BANKS[g])
                    for k in range(2):
                        for t in range(TT):
                            hd = 2 * (g % 2) + k
                            last = T.transpose(bank[T_BANKS[g]][:, k * SEQ + t * P:k * SEQ + (t + 1) * P],
                                               qk_tok[:, g // 2, t, hd * P:(hd + 1) * P], ident)
                    last.then_inc(sem("gla_qkT_filled"), 1)
                    free[T_BANKS[g]] = ("gla_qkT", g + 1)

            def cumulate():
                pe.wait_ge(sem("gla_la"), 4)
                for g in range(4):
                    d = g // 2
                    claim(T_BANKS[g])
                    for k in range(2):
                        for t in range(TT):
                            hd = 2 * (g % 2) + k
                            last = T.matmul(bank[T_BANKS[g]][:, k * SEQ + t * P:k * SEQ + (t + 1) * P],
                                            la[:, t, d * GLA_K + hd * P:d * GLA_K + (hd + 1) * P],
                                            consts[:, K_TRI + d * P:K_TRI + (d + 1) * P], start=True, stop=True)
                    last.then_inc(sem("gla_cum"), 1)
                    free[T_BANKS[g]] = ("gla_exp", 2 * (g + 1))

            def kD_T():
                pe.wait_ge(sem("gla_gated"), 8)
                for g in range(4):
                    d, t = divmod(g, 2)
                    claim(T_BANKS[g])
                    for hd in range(GLA_H):
                        last = T.transpose(bank[T_BANKS[g]][:, hd * P:(hd + 1) * P],
                                           kD[:, d, hd * SEQ + t * P:hd * SEQ + (t + 1) * P], ident)
                    last.then_inc(sem("gla_kDt_filled"), 1)
                    free[T_BANKS[g]] = ("gla_kDt", g + 1)

            def gla_scores():
                for g in range(4):
                    d, t = divmod(g, 2)
                    claim(T_BANKS[g])
                    for hd in range(GLA_H):
                        at = slice(hd * SEQ + t * P, hd * SEQ + (t + 1) * P)
                        last = T.matmul(bank[T_BANKS[g]][:, hd * P:(hd + 1) * P], kE[:, d, at], qE[:, d, at],
                                        start=True, stop=True)
                    last.then_inc(sem("gla_scores"), 1)
                    free[T_BANKS[g]] = ("gla_probs", g + 1)

            pe.wait_ge(*[sem(need[3][0]), need[3][1]])
            product(GLA_IN, X, "gla_in", width=2 * GLA_R)
            stages = {1: z_T, 2: pre_gates, 3: qk_T, 4: cumulate, 5: kD_T, 6: gla_scores}
            for t in range(1, 7):
                product(GLA_IN + t, X, "gla_in", hooks=[(2, stages[t])])

            def gla_u(hd):
                plan = ((4, 0, 0, 0), (4, 1, 0, 2), (5, 0, 1, 2), (6, 0, 0, 1), (6, 1, 1, 1), (7, 0, 1, 3))
                for b in T_BANKS:
                    claim(b)
                for n, (b, at, d, ch) in enumerate(plan):
                    t, r = ch // 2, (ch % 2) * GLA_C
                    last = T.matmul(bank[b][:, at * GLA_HV:(at + 1) * GLA_HV],
                                    kDt[r:r + GLA_C, d, t, hd * P:(hd + 1) * P],
                                    gv[r:r + GLA_C, t, hd * GLA_HV:(hd + 1) * GLA_HV], start=True, stop=True)
                    if n == len(plan) - 1 or plan[n + 1][0] != b:
                        last.then_inc(sem("gla_u"), 1)
                for b, after in ((4, 5), (5, 4), (6, 6), (7, 2)):
                    free[b] = ("gla_state", 6 * hd + after)

            def gla_o(hd):
                st = states[hd % 2]
                pe.wait_ge(sem("gla_state"), 6 * (hd + 1))
                pe.wait_ge(sem("gla_probs"), 4)
                at = slice((hd % 2) * GLA_HV, (hd % 2 + 1) * GLA_HV)
                for t in range(TT):
                    b = 2 * t + hd // 2
                    if hd % 2 == 0:
                        claim(b)
                    T.matmul(bank[b][:, at], probs[:, t, hd * P:(hd + 1) * P],
                             gv[:, t, hd * GLA_HV:(hd + 1) * GLA_HV], start=True, stop=True)
                    inter = [(ch, d) for ch in (2 * t, 2 * t + 1) for d in range(2)
                             if (ch > 0 if d == 0 else ch < 3)]
                    for n, (ch, d) in enumerate(inter):
                        r = (ch % 2) * GLA_C
                        last = T.matmul(bank[b][r:r + GLA_C, at],
                                        qE[:, d, hd * SEQ + ch * GLA_C:hd * SEQ + (ch + 1) * GLA_C],
                                        st[:, ch - 1 if d == 0 else 5 - ch, :], start=False, stop=True,
                                        skip_group_check=True)
                    if t == TT - 1:
                        last.then_inc(sem("gla_head"), 1)

            pe.wait_ge(sem("gla_kDt"), 4)
            pe.wait_ge(sem("gla_in"), 14)
            gla_u(0)
            for hd in range(GLA_H):
                if hd + 1 < GLA_H:
                    gla_u(hd + 1)
                gla_o(hd)
            for t in range(TT):
                for pair in range(2):
                    free[2 * t + pair] = ("gla_y", 4 * pair + 2 * t + 2)
            pe.wait_ge(sem("gla_y"), 8)
            need = lhs_T(gr, T_BANKS)
            got = []
            product(GLA_OUT, Y, None, need=need)
            for t in range(TT):
                free[2 * (GLA_OUT % 2) + t] = ("h_new", t + 1)
            product(GLA_OUT + 1, Y, None, hooks=[(2, lambda: got.extend(h_T(0, 1)))])
            for t in range(TT):
                free[2 * ((GLA_OUT + 1) % 2) + t] = ("h_new", TT + t + 1)
            c.up("h_new", 4)

            def ffn(n, src, got):
                tin, tout, tple = layer(n)
                other = Y if src is X else X

                def mid_T(t):
                    b = T_BANKS[(t - tin) % 2]
                    c.wait(pe, "ffn_mid", TT * (t - tin + 1) + TT * FT * n)
                    claim(b)
                    for k in range(2):
                        for tt in range(TT):
                            last = T.transpose(bank[b][:, k * SEQ + tt * P:k * SEQ + (tt + 1) * P],
                                               mid[:, (t - tin) % 2, tt, k * P:(k + 1) * P], ident)
                    last.then_inc(sem("ffn_T_filled"), 1)
                    free[b] = ("ffn_lhs", c.up("ffn_lhs"))

                more = list(got) + [None, None]

                def second_half():
                    more[2:4] = h_T(1, 3 * n + 1)

                product(tin, src, "ffn_mid", need=more, hooks=[(1, second_half)])
                for t in range(tin + 1, tin + 3):
                    product(t, src, "ffn_mid", hooks=[(2, lambda t=t: mid_T(t - 1))])
                turns = (FT - 5) // 2
                with pe.Fori(0, turns) as i:
                    c.enter(i, {"w_lo": 8, "w_used": 8, "ffn_mid": 4, "ffn_lhs": 2})
                    for t in (tin + 3, tin + 4):
                        product(t, src, "ffn_mid", hooks=[(2, lambda t=t: mid_T(t - 1))])
                    c.leave(turns)
                for b, (name, value) in list(free.items()):
                    free[b] = (name, value + (turns - 1) * {"ffn_mid": 4, "ffn_lhs": 2}.get(name, 0))
                for t in range(tin + 3 + 2 * turns, tin + FT):
                    product(t, src, "ffn_mid", hooks=[(2, lambda t=t: mid_T(t - 1))])

                def p_T():
                    pe.wait_ge(sem("p_in"), 16)
                    claim(6)
                    for k in range(2):
                        for t in range(TT):
                            last = T.transpose(bank[6][:, k * SEQ + t * P:k * SEQ + (t + 1) * P],
                                               p_tok[:, n, t, k * P:(k + 1) * P], ident)
                    last.then_inc(sem("pT_filled"), 1)
                    free[6] = ("pT", n + 1)

                half0 = []
                need = [("ffn_lhs", FT * n + k + 1) for k in range(FT)]
                product(tout, M, "h_new", need=need, hooks=[(2, lambda: mid_T(tin + FT - 1)), (5, p_T)])
                product(tout + 1, M, "h_new", hooks=[(2, lambda: half0.extend(h_T(0, 3 * n + 2)))])
                more2 = list(half0) + [None, None]

                def second_half2():
                    more2[2:4] = h_T(1, 3 * n + 2)

                product(tple, src, "ple_sig", need=more2, hooks=[(1, second_half2)])
                product(tple + 1, PT, "ple_gated", need=[("pT", n + 1)])
                half1 = []
                product(tple + 2, src, "ple_sig", hooks=[(2, lambda: half1.extend(h_T(0, 3 * n + 3)))])
                product(tple + 3, PT, "ple_gated")
                c.up("h_new", 4)
                return half1

            half = ffn(0, X, got)

            def df_T(t):
                pe.wait_ge(sem("df_rope"), TT * (t + 1))
                for b in range(2):
                    claim(6 + b)
                    for k in range(2):
                        for tt in range(TT):
                            last = T.transpose(bank[6 + b][:, k * SEQ + tt * P:k * SEQ + (tt + 1) * P],
                                               dtok[:, t % 2, tt, (2 * b + k) * P:(2 * b + k + 1) * P], ident)
                    last.then_inc(sem("df_T_filled"), 1)
                    free[6 + b] = ("df_T", 2 * t + b + 1)

            def df_scores(hd):
                if hd % 4 == 0:
                    pe.wait_ge(sem("df_T"), 4 * (hd // 4 + 1))
                for m in range(2):
                    claim(4 + m)
                    r = slice(m * DF_HD, (m + 1) * DF_HD)
                    for q in range(TT):
                        last = T.matmul(bank[4 + m][:, q * SEQ:(q + 1) * SEQ], dT[r, 0, hd, q * P:(q + 1) * P],
                                        dT[r, 1, hd, :], start=True, stop=True)
                    last.then_inc(sem("df_scores"), 1)
                    free[4 + m] = ("df_exp", 4 * hd + 2 * (m + 1))

            def df_aT(hd):
                pe.wait_ge(sem("df_a"), TT * (hd + 1))
                claim(6)
                for k in range(TT):
                    for q in range(TT):
                        last = T.transpose(bank[6][:, k * SEQ + q * P:k * SEQ + (q + 1) * P],
                                           dp[:, hd % 2, 0, q, k * P:(k + 1) * P], ident)
                last.then_inc(sem("df_aT_filled"), 1)
                free[6] = ("df_aT", hd + 1)

            def df_av(hd):
                pe.wait_ge(sem("df_aT"), hd + 1)
                b = 7 - hd // 2 % 2
                if hd % 4 == 0:
                    pe.wait_ge(sem("df_in"), TT * (5 + hd // 4))
                if hd % 2 == 0:
                    claim(b)
                for q in range(TT):
                    for k in range(TT):
                        last = T.matmul(bank[b][:, q * SEQ + (hd % 2) * P:q * SEQ + (hd % 2 + 1) * P],
                                        daT[:, hd % 4, k * SEQ + q * P:k * SEQ + (q + 1) * P],
                                        dv[:, k, hd * P:(hd + 1) * P], start=k == 0, stop=k == TT - 1)
                last.then_inc(sem("df_av"), 1)
                if hd % 2 == 1:
                    free[b] = ("df_o", hd // 2 + 1)

            df_half0, df_halves = list(half) + [None, None], [None] * 4

            def df_beside(u):
                for at, step, arg in DF_PLAN:
                    if at != u:
                        continue
                    if step == "second":
                        df_half0[2:4] = h_T(1, 3)
                    elif step == "qkT":
                        df_T(arg)
                    elif step == "scores":
                        df_scores(arg)
                    elif step == "aT":
                        df_aT(arg)
                    elif step == "av":
                        df_av(arg)
                    elif step == "half":
                        pe.wait_ge(sem("df_y"), arg + 1)
                        df_halves[2 * arg:2 * arg + 2] = lhs_T(do, (4, 5) if arg == 0 else (6, 7))

            product(DF_IN, Y, "df_in", need=df_half0, beside=df_beside)
            for t in range(1, 6):
                product(DF_IN + t, Y, "df_in", beside=df_beside)
            half = ffn(1, Y, parts(DF_OUT, X, df_halves, df_beside, 4))

            def cv_T(t):
                b = T_BANKS[(t - CV_IN) % 2]
                c.wait(pe, "cv_prod", TT * (t - CV_IN + 1))
                claim(b)
                for m in range(2):
                    for tt in range(TT):
                        last = T.transpose(bank[b][:, m * SEQ + tt * P:m * SEQ + (tt + 1) * P],
                                           cprod[:, (t - CV_IN) % 2, tt, m, :], ident)
                last.then_inc(sem("cv_T_filled"), 1)
                free[b] = ("cv_lhs", c.up("cv_lhs"))

            more3 = list(half) + [None, None]

            def cv_second():
                more3[2:4] = h_T(1, 6)

            product(CV_IN, X, "cv_prod", need=more3, hooks=[(1, cv_second)])
            for t in (CV_IN + 1, CV_IN + 2):
                product(t, X, "cv_prod", hooks=[(2, lambda t=t: cv_T(t - 1))])
            with pe.Fori(0, 2) as i:
                c.enter(i, {"w_lo": 8, "w_used": 8, "cv_prod": 4, "cv_lhs": 2})
                for t in (CV_IN + 3, CV_IN + 4):
                    product(t, X, "cv_prod", hooks=[(2, lambda t=t: cv_T(t - 1))])
                c.leave(2)
            for b, (name, value) in list(free.items()):
                free[b] = (name, value + {"cv_prod": 4, "cv_lhs": 2}.get(name, 0))
            product(CV_IN + 7, X, "cv_prod", hooks=[(2, lambda: cv_T(CV_IN + 6))])
            got = chained(CV_OUT, Y, "h_new", 7, need=[("cv_lhs", 2 * (k + 1)) for k in range(4)],
                          hooks=[(2, lambda: cv_T(CV_IN + 7))])

            def mb_T(m):
                pe.wait_ge(sem("mb_unit"), TT * (m + 1))
                for b in range(2):
                    claim(4 + b)
                    for k in range(2):
                        for tt in range(TT):
                            last = T.transpose(bank[4 + b][:, k * SEQ + tt * P:k * SEQ + (tt + 1) * P],
                                               mtok[:, m % 2, tt, (2 * b + k) * P:(2 * b + k + 1) * P], ident)
                    last.then_inc(sem("mb_T_filled"), 1)
                    free[4 + b] = ("mb_T", 2 * m + b + 1)

            def mb_scores(hd):
                b = 4 + hd % 2
                if hd % 8 == 0:
                    pe.wait_ge(sem("mb_T"), 4 * (hd // 8 + 1))
                claim(b)
                r, blk = slice((hd % 2) * MB_HD, (hd % 2 + 1) * MB_HD), hd // 2
                T.matmul(bank[b][:, 0:P], mT[r, 0, blk, 0:P], mT[r, 1, blk, 0:P], start=True, stop=True)
                T.matmul(bank[b][:, P:3 * P], mT[r, 0, blk, P:SEQ], mT[r, 1, blk, :], start=True, stop=True)\
                    .then_inc(sem("mb_scores"), 1)
                free[b] = ("mb_biased", hd + 1)

            def mb_pT(hd):
                pe.wait_ge(sem("mb_exp"), TT * (hd + 1))
                claim(6)
                for n in range(3):
                    last = T.transpose(bank[6][:, n * P:(n + 1) * P], mp[:, hd % 4, n * P:(n + 1) * P], ident)
                last.then_inc(sem("mb_pT_filled"), 1)
                free[6] = ("mb_pT", hd + 1)

            def mb_av(hd):
                if hd % 8 == 0:
                    pe.wait_ge(sem("mb_in"), TT * (3 + 3 * (hd // 8)))
                pe.wait_ge(sem("mb_pT"), hd + 1)
                if hd % 4 == 0:
                    claim(7)
                at = [slice(q * SEQ + (hd % 4) * MB_HD, q * SEQ + (hd % 4 + 1) * MB_HD) for q in range(TT)]
                T.matmul(bank[7][:, at[0]], mpT[:, hd % 3, 0:P], mv[:, 0, hd * MB_HD:(hd + 1) * MB_HD],
                         start=True, stop=True)
                for k in range(2):
                    last = T.matmul(bank[7][:, at[1]], mpT[:, hd % 3, (k + 1) * P:(k + 2) * P],
                                    mv[:, k, hd * MB_HD:(hd + 1) * MB_HD], start=k == 0, stop=k == 1)
                last.then_inc(sem("mb_av"), 1)
                if hd % 4 == 3:
                    free[7] = ("mb_o", hd // 4 + 1)

            half0, halves = list(got) + [None, None], [None] * 4

            def mb_beside(u):
                for at, step, arg in MB_PLAN:
                    if at != u:
                        continue
                    if step == "second":
                        half0[2:4] = h_T(1, 7)
                    elif step == "qkT":
                        mb_T(arg)
                    elif step == "scores":
                        mb_scores(arg)
                    elif step == "pT":
                        mb_pT(arg)
                    elif step == "av":
                        mb_av(arg)
                    elif step == "half":
                        pe.wait_ge(sem("mb_y"), arg + 1)
                        halves[2 * arg:2 * arg + 2] = lhs_T(mz, (4, 5) if arg == 0 else (6, 7))

            product(MB_IN, X, "mb_in", need=half0, beside=mb_beside)
            for t in range(1, 8):
                product(MB_IN + t, X, "mb_in", beside=mb_beside)
            parts(MB_OUT, Y, halves, mb_beside)


def _units(w, tiles):
    k = w.shape[0]
    return np.concatenate([w[:, t].reshape(k // 256, 2, P, NW).transpose(0, 2, 1, 3).reshape(k // 256, P, 2 * NW)
                           for t in tiles])


def _plain(n):
    return [slice(t, t + NW) for t in range(0, n, NW)]


def _ordered(width, *tiles):
    return [slice(t * width, (t + 1) * width) for t in tiles]


def _parts(w):
    return np.concatenate([_units(w[k:k + HALF], _plain(D)) for k in (0, HALF)])


def _grouped(n, parts, of):
    size = n // parts
    return [np.concatenate([np.arange(q * size + j, q * size + j + of) for q in range(parts)])
            for j in range(0, size, of)]


def _constants():
    i = np.arange(P)
    same = (i[:, None] // GLA_C) == (i[None, :] // GLA_C)
    up = same & (i[:, None] <= i[None, :])
    down = same & (i[:, None] >= i[None, :])
    strict = same & (i[:, None] > i[None, :])
    half = DF_HD // 2
    inv = np.float32(10000.0) ** (-np.arange(half, dtype=np.float32) * np.float32(2.0) / np.float32(DF_HD))
    ang = np.arange(SEQ, dtype=np.float32)[:, None] * inv[None, :].astype(np.float32)
    cos, sin = np.cos(ang), np.sin(ang)
    cos = np.concatenate([cos, cos], 1).reshape(TT, P, DF_HD).transpose(1, 0, 2).reshape(P, -1)
    sin = np.concatenate([-sin, sin], 1).reshape(TT, P, DF_HD).transpose(1, 0, 2).reshape(P, -1)
    k = np.arange(SEQ)
    dist = [np.where(k[None, :n] <= i[:, None] + q0, k[None, :n] - i[:, None] - q0, -1e32)
            for q0, n in ((0, P), (P, SEQ))]
    return np.concatenate([np.eye(P), up / 16.0, down / 16.0, up, strict, cos, sin] + dist, 1).astype(np.float32)


def kernel(**inputs):
    import concourse.bacc as _bacc
    from concourse.bass_utils import run_bass_kernel_spmd as _run

    a = {name: np.asarray(value) for name, value in inputs.items()}
    gla = a["gla_w_in"][0]
    z = gla[:, 3 * D:3 * D + 2 * GLA_R].reshape(KT, P, 2 * GLA_R).transpose(1, 0, 2).reshape(P, -1)
    first = np.zeros((1, P, 2 * NW), np.float32)
    first[0, :, :z.shape[1]] = z

    def layer(n):
        gate, proj = _units(a["ple_w_gate"][n], _plain(D)), _units(a["ple_w_proj"][n], _plain(D))
        return [_units(a["ffn_w_in"][n], _grouped(2 * FF, 2, 256)), _units(a["ffn_w_out"][n], _plain(D)),
                gate[:KT // 2], proj[:1], gate[KT // 2:], proj[1:]]

    stream = np.concatenate(
        [first, _units(gla, _plain(3 * D)), _units(a["gla_w_out"][0], _plain(D))] + layer(0)
        + [_units(a["diff_w_in"][0], _ordered(NW, 0, 2, 3, 1, 4, 5)), _parts(a["diff_w_out"][0])] + layer(1)
        + [_units(a["conv_w_in_2"][0], _grouped(4 * D, 4, P)), _units(a["conv_w_out_2"][0], _plain(D)),
           _units(a["attn_w_in_2"][0], _ordered(NW, 0, 2, 4, 1, 3, 5, 6, 7)), _parts(a["attn_w_out_2"][0])])
    norms = [a["norm_mix"][0], a["norm_ffn"][0], a["ple_norm"][0], a["norm_mix"][1], a["norm_ffn"][1],
             a["ple_norm"][1], a["norm_g_2"][0], a["norm_g_2"][1]]
    cols = np.concatenate(
        [g.reshape(-1, P).T for g in norms + [a["gla_g_out"][0], a["diff_g_sub"][0]]]
        + [np.concatenate([a[g][0]] * 2)[:, None] for g in ("q_norm_g_2", "k_norm_g_2")]
        + [a["conv_w_2"][0].reshape(CONV_K, KT, P).transpose(2, 1, 0).reshape(P, -1)], 1)
    rows = np.concatenate([a["diff_g_q"][0].ravel(), a["diff_g_k"][0].ravel()]
                          + [a[f"diff_lam_{n}"][0] for n in ("q1", "k1", "q2", "k2")])[None]
    wgate = np.zeros((33, 2 * GLA_K), np.float32)
    wgate[0:GLA_R, :GLA_K], wgate[GLA_R:2 * GLA_R, GLA_K:] = a["gla_w_gate_f"][0], a["gla_w_gate_b"][0]
    wgate[32, :GLA_K], wgate[32, GLA_K:] = a["gla_b_gate_f"][0], a["gla_b_gate_b"][0]
    arrays = {"stream": stream, "x": a["x"][0], "p": a["p"][:, 0], "cols": cols, "rows": rows,
              "consts": _constants(), "wgate": wgate}
    arrays = {name: np.ascontiguousarray(value) for name, value in arrays.items()}
    nc = _bacc.Bacc("TRN2", target_bir_lowering=False, num_devices=1)
    args = [nc.dram_tensor(f"{name}_dram", value.shape, F32, kind="ExternalInput").ap() for name, value in arrays.items()]
    out = nc.dram_tensor("out", (SEQ, D), F32, kind="ExternalOutput").ap()
    stream_, x_, p_, cols_, rows_, consts_, wgate_ = args
    build(nc, stream_, x_, p_, cols_, rows_, consts_, wgate_, out)
    r = _run(nc, [{f"{name}_dram": value for name, value in arrays.items()}], core_ids=[0])
    return r.results[0]["out"].reshape(1, SEQ, D)
```

```python
import math
from contextlib import ExitStack

import numpy as np

import concourse.bass as bass
from concourse import mybir
from concourse.alu_op_type import AluOpType as ALU

F32 = mybir.dt.float32
F32R = mybir.dt.float32r
U32 = mybir.dt.uint32
ACT = mybir.ActivationFunctionType
AXX = mybir.AxisListType.X

P = 128
SEQ, D = 256, 1024
TT = SEQ // P
KT = D // P
NW = 512
EPS = 1e-6
FF = (-((-8 * D) // 3) + 255) // 256 * 256
FKT = FF // P
FT = FF // 256
PLE = 256
HALF = D // 2

GLA_H, GLA_HK, GLA_HV, GLA_C, GLA_R = 4, 128, 256, 64, 16
GLA_K = GLA_H * GLA_HK
DF_H, DF_HD = 8, 64
LAMBDA_INIT = 0.8 - 0.6 * math.exp(-0.3)
MB_H, MB_HD = 16, 64
CONV_K = 3

IN, OUT = KT // 2, [KT // 4] * 4
LAYER = [IN] * FT + [FKT // 2] * 2 + [IN, 1] * 2
TILES = [1] + [IN] * 6 + OUT + LAYER
GLA_IN, GLA_OUT, FFN_IN0 = 0, 7, 11
FFN_OUT0 = FFN_IN0 + FT
PLE0 = FFN_OUT0 + 2
DF_IN = PLE0 + 4
TILES += [IN] * 6 + OUT + LAYER
DF_OUT = DF_IN + 6
FFN_IN1 = DF_OUT + 4
FFN_OUT1 = FFN_IN1 + FT
PLE1 = FFN_OUT1 + 2
CV_IN = PLE1 + 4
TILES += [IN] * 8 + [IN] * 2
CV_OUT = CV_IN + 8
MB_IN = CV_OUT + 2
TILES += [IN] * 8 + OUT
MB_OUT = MB_IN + 8
END = [0]
for _n in TILES:
    END.append(END[-1] + _n)
UNITS = END[-1]
Z_COLS = 2 * GLA_R * KT
RAW, RING = 4, 8
AHEAD = 6


def plan(first, tiles, steps, ends_first=False):
    base = END[first]
    found = [(base + u, 1, n, step, arg) for u, row in steps.items() for n, (step, arg) in enumerate(row)]
    found += [(END[first + t + 1], 0 if ends_first else 2, 0, "tile", t) for t in range(tiles)]
    return [(u, step, arg) for u, _, _, step, arg in sorted(found, key=lambda x: x[:3])]


GLA_PLAN = plan(GLA_IN, 7, {
    3: [("zT", 0)], 5: [("gates", 0)], 6: [("expabs", 0)], 7: [("ln", 0)], 10: [("qkT", 0)],
    11: [("cumulate", 0)], 12: [("cumulate", 1)], 14: [("kDT", 0)], 15: [("kDT", 1), ("scores", 0)],
    16: [("scores", 1)], 17: [("states", 0)], 19: [("states", 1), ("out", 0)], 20: [("y", 0)],
    21: [("out", 1)], 22: [("states", 2), ("y", 1)], 23: [("states", 3)], 24: [("half", 0), ("out", 2)],
    25: [("out", 3)], 26: [("y", 2), ("y", 3)], 28: [("half", 1)]}, ends_first=True)
_steps = {1: [("second", 0)], 21: [("av", 0), ("av", 1), ("osq", 0), ("av", 2), ("av", 3), ("osq", 1)],
          22: [("osums", 0)], 23: [("norm", 0), ("pair", 0)],
          24: [("pair", 1)], 25: [("av", 4), ("av", 5), ("osq", 2)], 26: [("av", 6), ("av", 7), ("osq", 3)]}
for _h, _u in enumerate((14, 16, 17, 18, 20, 21, 22, 23)):
    for _step, _at in (("scores", _u), ("soft", _u + 1), ("aT", _u + 2)):
        _steps.setdefault(_at, []).append((_step, _h))
for _n, _u in enumerate(((6, 5, 6, 8, 9), (8, 10, 12, 13, 14), (13, 15, 16, 17, 18), (18, 17, 18, 19, 20))):
    for _step, _at in zip((("sums", _n), ("rope", _n), ("add", _n), ("qkT", 2 * _n), ("qkT", 2 * _n + 1)), _u):
        _steps.setdefault(_at, []).append(_step)
for _u, _step in ((22, ("osums", 1)), (23, ("norm", 1)), (26, ("osums", 2)),
                  (27, ("norm", 2)), (27, ("osums", 3)), (27, ("pair", 2)), (28, ("norm", 3)), (28, ("pair", 3))):
    _steps.setdefault(_u, []).append(_step)
DF_PLAN = plan(DF_IN, 6, _steps, ends_first=True)

MB_QK = (0, 1, 3, 4)
_steps = {1: [("second", 0)], 12: [("qkT", 1)]}
for _h in range(MB_H):
    _u = 12 + _h if _h < 8 else 16 + _h
    _pT = _u + (3 if _h < 14 else 2)
    for _step, _at in (("scores", _u), ("exp", _u + 1), ("pT", _pT), ("av", _pT + (2 if _h < 14 else 1))):
        _steps.setdefault(_at, []).append((_step, _h))
for _n, _u in enumerate(((4, 6, 8), (8, 10), (17, 19, 20), (20, 22, 23))):
    for _step, _at in zip(("sums", "unit", "qkT"), _u):
        _steps.setdefault(_at, []).append((_step, _n))
for _u, _step in ((29, ("z", 0)), (31, ("half", 0)), (34, ("z", 1)), (35, ("half", 1))):
    _steps.setdefault(_u, []).append(_step)
MB_PLAN = plan(MB_IN, 8, _steps)

C_NORM, C_GLA, C_DF, C_QG, C_KG, C_CONV, N_COLS = 0, 64, 66, 67, 68, 69, 69 + KT * CONV_K
K_ID, K_TRI, K_MASK, K_COS, K_SIN, K_DIST, N_CONST = 0, 128, 384, 640, 768, 896, 896 + 384
R_GQ, R_GK, R_LAM, N_ROWS = 0, 128, 256, 512

T_BANKS = (4, 5, 6, 7)


class Count:

    def __init__(self, sem):
        self.sem, self.value, self.turn, self.rate = sem, {}, None, {}

    def up(self, name, by=1):
        self.value[name] = self.value.get(name, 0) + by
        return self.value[name]

    def wait(self, eng, name, value):
        if self.turn is not None:
            eng.wait_ge(self.sem(name), self.turn * self.rate[name] + value)
        elif value > 0:
            eng.wait_ge(self.sem(name), value)

    def enter(self, turn, rate):
        self.turn, self.rate, self.before = turn, rate, dict(self.value)

    def leave(self, turns):
        for name, value in self.value.items():
            step = value - self.before.get(name, 0)
            assert step in (0, self.rate.get(name, 0)), (name, step)
            self.value[name] = value + step * (turns - 1)
        self.turn = None


def build(nc, stream, x, p, cols_d, rows_d, consts_d, wgate_d, out):
    ctx = ExitStack()
    with ctx:
        def sb(name, shape, dt=F32, scope=ctx):
            return scope.enter_context(nc.sbuf_tensor(name, shape, dt))

        sems = {}

        def sem(name):
            if name not in sems:
                sems[name] = ctx.enter_context(nc.semaphore(name))
            return sems[name]

        bank = [ctx.enter_context(nc.psum_tensor(f"bank{b}", [P, NW], F32)) for b in range(8)]

        raw = sb("raw", [P, RAW, 2 * NW])
        whi = sb("whi", [P, RING, 2 * NW], F32R)
        wlo = sb("wlo", [P, RING, 2 * NW], F32R)
        h = sb("h", [P, TT, D])
        X = (sb("x_hi", [P, KT, SEQ], F32R), sb("x_lo", [P, KT, SEQ], F32R))
        Y = (sb("y_hi", [P, KT, SEQ], F32R), sb("y_lo", [P, KT, SEQ], F32R))
        PT = (sb("p_hi", [P, 2, SEQ], F32R), sb("p_lo", [P, 2, SEQ], F32R))
        p_tok = sb("p_tok", [P, 2, TT, PLE])
        cols = sb("cols", [P, N_COLS])
        consts = sb("consts", [P, N_CONST])
        rows = sb("rows", [P, N_ROWS])
        junk = sb("junk", [P, NW])
        stats = sb("stats", [P, 8, 2, TT])
        ms = sb("ms", [P, 8, 2, TT])
        rstd = sb("rstd", [P, 8, TT])
        neg_half = sb("neg_half", [P, 16])
        rstd_q = sb("rstd_q", [P, TT])
        ident = consts[:, K_ID:K_ID + P]

        def phase():
            return ExitStack()

        s = phase()
        qk_tok = sb("gla_qk_tok", [P, 2, TT, GLA_K], scope=s)
        la = sb("gla_log_a", [P, TT, 2 * GLA_K], scope=s)
        qkT = sb("gla_qkT", [P, 2, GLA_H * SEQ], scope=s)
        qE = sb("gla_qE", [P, 2, GLA_H * SEQ], scope=s)
        kE = sb("gla_kE", [P, 2, GLA_H * SEQ], scope=s)
        gv = sb("gla_v", [P, TT, D], scope=s)
        gr = sb("gla_r", [P, TT, D], scope=s)
        gtmp = sb("gla_tmp", [P, 4, NW], scope=s)
        wg = sb("gla_wgate", [33, 2 * GLA_K], scope=s)
        zT = sb("gla_zT", [33, SEQ], scope=s)
        decay = sb("gla_decay", [P, 2, GLA_H * 4], scope=s)
        oss = sb("gla_oss", [P, 3, TT * GLA_H], scope=s)
        s.close()
        kD = qk_tok[:, :, :, :].rearrange("p a t n -> p a (t n)")
        kDt = la[:, :, :].rearrange("p t n -> p (t n)").rearrange("p (d t n) -> p d t n", d=2, t=TT)
        probs = qkT[:, 0, :].rearrange("p (t n) -> p t n", t=TT)
        st_even = kE[:, :, :].rearrange("p a n -> p (a n)").rearrange("p (s n) -> p s n", n=GLA_HV)
        st_odd = gtmp[:, :, :].rearrange("p a n -> p (a n)").rearrange("p (s n) -> p s n", n=GLA_HV)
        states = (st_even, st_odd)
        grown = gtmp[:, :, :].rearrange("p (e a) n -> p e (a n)", e=2)

        s = phase()
        M = (sb("mid_hi", [P, FKT, SEQ], F32R, scope=s), sb("mid_lo", [P, FKT, SEQ], F32R, scope=s))
        sg = sb("ffn_silu", [P, 2, TT, 256], scope=s)
        mid = sb("ffn_mid", [P, 2, TT, 256], scope=s)
        s.close()

        s = phase()
        sig = sb("ple_gate", [P, TT, NW], scope=s)
        gated = sb("ple_gated", [P, TT, NW], scope=s)
        s.close()

        s = phase()
        dtok = sb("df_tok", [P, 2, TT, NW], scope=s)
        dsq = sb("df_sq", [P, TT, NW], scope=s)
        dp = sb("df_p", [P, 2, 2, TT, SEQ], scope=s)
        daT = sb("df_aT", [P, 4, NW], scope=s)
        dm2 = sb("df_m2", [P, TT, NW], scope=s)
        dT = sb("df_qkT", [P, 2, DF_H, SEQ], scope=s)
        dv = sb("df_v", [P, TT, D], scope=s)
        do = sb("df_o", [P, TT, D], scope=s)
        rot = sb("df_rot", [P, 2, 2, TT, P], scope=s)
        dss = sb("df_ss", [P, 3, TT * 8], scope=s)
        dqr = sb("df_q_rstd", [P, 2, TT * 8], scope=s)
        dstat = sb("df_stat", [P, DF_H, 16], scope=s)
        lam = sb("df_lam", [P, 8], scope=s)
        s.close()

        s = phase()
        cact = sb("cv_act", [P, 2, TT, 2, P], scope=s)
        cprod = sb("cv_prod", [P, 2, TT, 2, P], scope=s)
        cu = sb("cv_u", [P, 2, SEQ + CONV_K - 1], scope=s)
        cc = sb("cv_c", [P, 4, SEQ], scope=s)
        s.close()

        s = phase()
        mtok = sb("mb_tok", [P, 2, TT, NW], scope=s)
        msq = sb("mb_sq", [P, TT, NW], scope=s)
        mT = sb("mb_qkT", [P, 2, KT, SEQ], scope=s)
        mv = sb("mb_v", [P, TT, D], scope=s)
        mz = sb("mb_z", [P, TT, D], scope=s)
        mgain = sb("mb_gain", [P, 2], scope=s)
        mss = sb("mb_ss", [P, 3, TT * 8], scope=s)
        mstat = sb("mb_stat", [P, 2, 4], scope=s)
        msum = sb("mb_sum", [P, TT, MB_H], scope=s)
        mrec = sb("mb_rec", [P, TT, MB_H], scope=s)
        mo = sb("mb_o", [P, TT, D], scope=s)
        ms2 = sb("mb_s", [P, 2, 3 * P], scope=s)
        mp = sb("mb_p", [P, 4, 3 * P], scope=s)
        mpT = sb("mb_pT", [P, 3, 3 * P], scope=s)
        s.close()

        O_BANK = (4, 4, 4, 7)
        GLA_Y_BANKS = (((5, 6), 0), ((7, 4), 4))
        DF_Y_BANK = (7, 7, 4, 5)

        def gla_gain(kt):
            return cols[:, C_GLA + kt % 2:C_GLA + kt % 2 + 1]

        block = ctx.enter_context(nc.Block())

        def layer(n):
            return (FFN_IN0, FFN_OUT0, PLE0) if n == 0 else (FFN_IN1, FFN_OUT1, PLE1)

        @block.sync
        def _(sp):
            for n in range(4):
                at = slice(n * SEQ, (n + 1) * SEQ)
                sp.dma_start(h[:, :, at], x.rearrange("(t p) d -> p t d", p=P)[:, :, at]).then_inc(sem(f"x_in{n}"), 16)
                if n == 0:
                    sp.dma_start(ident, consts_d[:, K_ID:K_ID + P]).then_inc(sem("ident_in"), 16)
                    sp.dma_start(raw[:, 0, 0:Z_COLS], stream[0][:, 0:Z_COLS]).then_inc(sem("raw0"), 16)
                    sp.dma_start(cols[:, :], cols_d).then_inc(sem("cols_in"), 16)
            for u in range(1, RAW):
                sp.dma_start(raw[:, u, :], stream[u]).then_inc(sem(f"raw{u}"), 16)
            sp.dma_start(consts[:, P:], consts_d[:, P:]).then_inc(sem("consts_in"), 16)
            sp.dma_start(wg[:, :], wgate_d).then_inc(sem("wg_in"), 16)
            sp.dma_start(p_tok[:, :, :, :], p.rearrange("l (t p) d -> p l t d", p=P)).then_inc(sem("p_in"), 16)
            sp.dma_start(rows[:, :], rows_d.to_broadcast([P, N_ROWS])).then_inc(sem("rows_in"), 16)
            with sp.Fori(1, UNITS // RAW) as i:
                for u in range(RAW):
                    sp.wait_ge(sem("w_lo"), i * RAW + (u - RAW + 1))
                    sp.dma_start(raw[:, u, :], stream[i * RAW + u]).then_inc(sem(f"raw{u}"), 16)
            for n in range(UNITS // RAW * RAW, UNITS):
                sp.wait_ge(sem("w_lo"), n - RAW + 1)
                sp.dma_start(raw[:, n % RAW, :], stream[n]).then_inc(sem(f"raw{n % RAW}"), 16)
            for half in range(2):
                for t in range(TT):
                    sp.wait_ge(sem("h_new"), 28 + 2 * half + t + 1)
                    sp.dma_start(out[t * P:(t + 1) * P, half * HALF:(half + 1) * HALF],
                                 h[:, t, half * HALF:(half + 1) * HALF]).then_inc(sem("out_done"), 16)
            sp.wait_ge(sem("out_done"), 64)

        @block.gpsimd
        def _(pool):
            c = Count(sem)

            def step(ins):
                ins.then_inc(sem("pool_step"), 1)
                c.wait(pool, "pool_step", c.up("pool_step"))

            def power(src, mean, dst, n, scale, eps=EPS):
                step(nc.gpsimd.tensor_scalar(mean, src, scale, eps, ALU.mult, ALU.add))
                return nc.gpsimd.tensor_tensor(dst, mean, neg_half[:, 0:n], ALU.pow)

            def row_norm(j):
                pool.wait_ge(sem("stats"), 4 * (j + 1))
                step(nc.gpsimd.tensor_tensor(ms[:, j, 0, :], stats[:, j, 0, :], stats[:, j, 1, :], ALU.add))
                power(ms[:, j, 0, :], ms[:, j, 1, :], rstd[:, j, :], TT, 1.0 / D).then_inc(sem("rstd"), 1)

            nc.gpsimd.memset(neg_half[:, :], -0.5).then_inc(sem("pool_step"), 1)
            c.wait(pool, "pool_step", c.up("pool_step"))
            row_norm(0)
            pool.wait_ge(sem("rstd"), 1)
            nc.gpsimd.tensor_scalar(rstd_q[:, :], rstd[:, 0, :], GLA_HK ** -0.5, None, ALU.mult)\
                .then_inc(sem("rstd_q"), 1)
            for hd in range(GLA_H):
                pool.wait_ge(sem("gla_sq"), TT * (hd + 1))
                both = slice(hd, TT * GLA_H, GLA_H)
                power(oss[:, 0, both], oss[:, 1, both], oss[:, 2, both], TT, 1.0 / GLA_HV)\
                    .then_inc(sem("gla_rstd"), 1)
            for j in (1, 2, 3):
                row_norm(j)

            def df_power(m):
                pool.wait_ge(sem("df_ss"), TT * (m + 1))
                dst, by = (dqr[:, m // 3, :], DF_HD ** 0.5) if m in (0, 3) else (dss[:, 2, :], 1.0)
                power(dss[:, 0, :], dss[:, 1, :], dst, TT * 8, by * by / DF_HD, by * by * EPS)\
                    .then_inc(sem("df_rstd"), 1)

            def df_cos(m):
                for k in range(TT):
                    xt = dtok[:, m % 2, k, :].rearrange("p (a e) -> p a e", a=4)
                    pool.wait_ge(sem("df_swap"), TT * m + k + 1)
                    cos = rot[:, (0, 1, 1, 0)[m], 0, k, :].unsqueeze(1).to_broadcast([P, 4, P])
                    nc.gpsimd.tensor_tensor(xt, xt, cos, ALU.mult).then_inc(sem("df_cos"), 1)

            def df_onorm(n):
                r0 = dstat[:, 2 * n:2 * n + 2, 12:14].rearrange("p a q -> p q a")
                view = [dss[:, i, 0:4].rearrange("p (q a) -> p q a", q=TT) for i in range(3)]
                pool.wait_ge(sem("df_recip"), 2 * 2 * (n + 1))
                if n == 0:
                    pool.wait_ge(sem("df_rstd"), 4)
                else:
                    pool.wait_ge(sem("df_y"), n)
                step(nc.gpsimd.tensor_tensor(view[1], r0, r0, ALU.mult))
                pool.wait_ge(sem("df_oss"), n + 1)
                step(nc.gpsimd.tensor_tensor(view[0], view[0], view[1], ALU.mult))
                by = 1.0 / (1.0 - LAMBDA_INIT)
                step(power(dss[:, 0, 0:4], dss[:, 1, 0:4], dss[:, 2, 0:4], 4, by * by / (2 * DF_HD), by * by * EPS))
                nc.gpsimd.tensor_tensor(view[2], view[2], r0, ALU.mult).then_inc(sem("df_orstd"), 1)

            for _, what, arg in DF_PLAN:
                if what == "sums":
                    df_power(arg)
                elif what == "rope":
                    df_cos(arg)
                elif what == "osums":
                    df_onorm(arg)
            for j in (4, 5, 6, 7):
                row_norm(j)
            for t in range(4):
                pool.wait_ge(sem("mb_ss"), TT * (t + 1))
                power(mss[:, 0, :], mss[:, 1, :], mss[:, 2, :], TT * 8, 1.0 / MB_HD).then_inc(sem("mb_rstd"), 1)

        @block.scalar
        def _(act):
            c = Count(sem)
            pos = [0]
            A = nc.scalar.activation

            def split_to(end):
                for u in range(pos[0], min(end, UNITS)):
                    c.wait(act, f"raw{u % RAW}", 16 * (u // RAW + 1))
                    if u >= RING:
                        c.wait(act, "w_used", u - RING + 1)
                    w = Z_COLS if u == 0 else 2 * NW
                    A(whi[:, u % RING, 0:w], raw[:, u % RAW, 0:w], ACT.Copy).then_inc(sem("w_hi"), 1)
                pos[0] = max(pos[0], min(end, UNITS))

            def lhs_hi(dst, gain, banks, kt0=None):
                kt0 = 2 * (banks[0] - T_BANKS[0]) if kt0 is None else kt0
                for n, b in enumerate(banks):
                    c.wait(act, "lhs_filled", c.up("lhs_filled"))
                    kt = kt0 + 2 * n
                    for k in range(2):
                        scale = 1.0 if gain is None else gain(kt + k)
                        last = A(dst[0][:, kt + k, :], bank[b][:, k * SEQ:(k + 1) * SEQ], ACT.Copy, scale=scale)
                    last.then_inc(sem("lhs_hi"), 1)

            def norm_gain(j):
                return lambda kt: cols[:, C_NORM + j * KT + kt:C_NORM + j * KT + kt + 1]

            def mixer_lhs(j, dst, out):
                split_to(END[out + 4] - 1 + AHEAD + 1)
                lhs_hi(dst, norm_gain(j), (4, 5))
                squares(j, 0)
                split_to(END[out + 4] + 1 + AHEAD)
                lhs_hi(dst, norm_gain(j), (6, 7))
                squares(j, 1)

            def squares(j, half):
                if j:
                    act.wait_ge(sem("h_new"), 4 * (j - 1) + 2 * (half + 1))
                for t in range(TT):
                    c.wait(act, "stats", c.value.get("stats", 0))
                    A(junk[:, :], h[:, t, half * HALF:(half + 1) * HALF], ACT.Square,
                      accum_out=stats[:, j, half, t:t + 1]).then_inc(sem("stats"), 1)
                    c.up("stats")

            def next_lhs(j, dst, tile):
                first = tile + 1
                split_to(END[first] + 2 + AHEAD)
                lhs_hi(dst, norm_gain(j), (4, 5))
                squares(j, 0)
                split_to(END[first + 1] + 1 + AHEAD)
                lhs_hi(dst, norm_gain(j), (6, 7))
                squares(j, 1)

            def evacuate(tile, j, dst, width, signal, func=ACT.Copy, scale=None):
                act.wait_ge(sem("rstd"), j + 1)
                c.wait(act, "w_used", END[tile + 1])
                for t in range(TT):
                    A(dst(t), bank[2 * (tile % 2) + t][:, 0:width], func,
                      scale=(scale if scale is not None else rstd[:, j, :])[:, t:t + 1]).then_inc(sem(signal), 1)

            split_to(1)
            act.wait_ge(sem("cols_in"), 16)
            lhs_hi(X, norm_gain(0), (4, 5, 6, 7))
            split_to(3)
            for n in range(4):
                act.wait_ge(sem(f"x_in{n}"), 16)
            squares(0, 0)
            split_to(4)
            squares(0, 1)

            def gla_tile(t):
                half = slice((t - 3) // 2 * NW, ((t - 3) // 2 + 1) * NW)
                if t == 0:
                    return
                if t <= 2:
                    act.wait_ge(sem("rstd_q"), 1)
                    evacuate(GLA_IN + t, 0, lambda k: qk_tok[:, t - 1, k, :], NW, "gla_in",
                             scale=rstd_q if t == 1 else None)
                elif t % 2 == 1:
                    evacuate(GLA_IN + t, 0, lambda k: gv[:, k, half], NW, "gla_in")
                else:
                    evacuate(GLA_IN + t, 0, lambda k: gr[:, k, half], NW, "gla_in", func=ACT.Silu)

            for u, step, arg in GLA_PLAN:
                split_to(u + AHEAD + (-1 if step == "tile" else 1))
                if step == "tile":
                    gla_tile(arg)
                elif step == "expabs":
                    for g in range(4):
                        act.wait_ge(sem("gla_abs"), g + 1)
                        A(gtmp[:, g, :], gtmp[:, g, :], ACT.Exp).then_inc(sem("gla_expabs"), 1)
                elif step == "ln":
                    for g in range(4):
                        act.wait_ge(sem("gla_expabs"), g + 1)
                        A(gtmp[:, g, :], gtmp[:, g, :], ACT.Ln, bias=1.0).then_inc(sem("gla_ln"), 1)
                elif step == "qkT":
                    for g in range(4):
                        act.wait_ge(sem("gla_qkT_filled"), g + 1)
                        A(qkT[:, g // 2, (g % 2) * NW:(g % 2 + 1) * NW], bank[T_BANKS[g]][:, :], ACT.Copy)\
                            .then_inc(sem("gla_qkT"), 1)
                elif step == "cumulate":
                    for g in (2 * arg, 2 * arg + 1):
                        act.wait_ge(sem("gla_cum"), g + 1)
                        act.wait_ge(sem("gla_la"), 4)
                        if arg:
                            act.wait_ge(sem("gla_gated"), 4)
                        for e, sign in enumerate((1.0, -1.0)):
                            A(grown[:, e, (g % 2) * NW:(g % 2 + 1) * NW], bank[T_BANKS[g]][:, :], ACT.Exp, scale=sign)\
                                .then_inc(sem("gla_exp"), 1)
                elif step == "kDT":
                    for g in (2 * arg, 2 * arg + 1):
                        act.wait_ge(sem("gla_kDt_filled"), g + 1)
                        A(kDt[:, arg, g % 2, :], bank[T_BANKS[g]][:, :], ACT.Copy).then_inc(sem("gla_kDt"), 1)
                elif step == "out":
                    act.wait_ge(sem("gla_head"), arg + 1)
                    for t in range(TT):
                        c.wait(act, "gla_sq", c.value.get("gla_sq", 0))
                        A(junk[:, 0:GLA_HV], bank[O_BANK[arg]][:, t * GLA_HV:(t + 1) * GLA_HV], ACT.Square,
                          accum_out=oss[:, 0, t * GLA_H + arg:t * GLA_H + arg + 1]).then_inc(sem("gla_sq"), 1)
                        c.up("gla_sq")
                elif step == "half":
                    lhs_hi(Y, gla_gain, *GLA_Y_BANKS[arg])

            def ffn(n, src):
                tin, tout, tple = layer(n)
                j = 3 * n + 1
                mixer_lhs(j, src, tin - 4)

                def tile(t):
                    split_to(END[t + 1] + AHEAD)
                    c.wait(act, "w_used", END[t + 1])
                    for k in range(TT):
                        A(sg[:, (t - tin) % 2, k, :], bank[2 * (t % 2) + k][:, 0:256], ACT.Silu,
                          scale=rstd[:, j, k:k + 1]).then_inc(sem("ffn_silu"), 1)
                        c.up("ffn_silu")

                act.wait_ge(sem("rstd"), j + 1)
                for t in range(tin, tin + 3):
                    tile(t)
                turns = (FT - 5) // 2
                with act.Fori(0, turns) as i:
                    c.enter(i, {"w_used": 8, "w_hi": 8, "ffn_silu": 4, **{f"raw{r}": 32 for r in range(RAW)}})
                    tile(tin + 3)
                    tile(tin + 4)
                    c.leave(turns)
                pos[0] += 8 * (turns - 1)
                for t in range(tin + 3 + 2 * turns, tin + FT):
                    tile(t)
                split_to(END[tout] + 5 + AHEAD)
                act.wait_ge(sem("pT_filled"), n + 1)
                A(PT[0][:, :, :], bank[6][:, :].rearrange("p (k s) -> p k s", k=2), ACT.Copy)\
                    .then_inc(sem("pT_hi"), 1)
                j += 1
                split_to(END[tout + 1] + 2 + AHEAD)
                lhs_hi(src, norm_gain(j), (4, 5))
                squares(j, 0)
                split_to(END[tple] + 1 + AHEAD)
                lhs_hi(src, norm_gain(j), (6, 7))
                squares(j, 1)
                act.wait_ge(sem("rstd"), j + 1)
                for half in range(2):
                    t = tple + 2 * half
                    split_to(END[t + 1] + AHEAD)
                    c.wait(act, "w_used", END[t + 1])
                    if half:
                        act.wait_ge(sem("ple_gated"), TT * (2 * n + 1))
                    for k in range(TT):
                        A(sig[:, k, :], bank[2 * (t % 2) + k][:, :], ACT.Sigmoid, scale=rstd[:, j, k:k + 1])\
                            .then_inc(sem("ple_sig"), 1)
                    if half == 0:
                        split_to(END[t + 2] + 2 + AHEAD)
                        lhs_hi(Y if src is X else X, norm_gain(j + 1), (4, 5))
                        squares(j + 1, 0)
                split_to(END[tple + 4] + 1 + AHEAD)
                lhs_hi(Y if src is X else X, norm_gain(j + 1), (6, 7))
                squares(j + 1, 1)

            ffn(0, X)

            def df_tile(t):
                if t >= 4:
                    evacuate(DF_IN + t, 3, lambda k: dv[:, k, (t - 4) * NW:(t - 3) * NW], NW, "df_in")
                    return
                if t >= 2:
                    act.wait_ge(sem("df_T_filled"), 2 * (t - 1))
                evacuate(DF_IN + t, 3, lambda k: dtok[:, t % 2, k, :], NW, "df_in")
                if t:
                    act.wait_ge(sem("df_ss"), TT * t)
                act.wait_ge(sem("df_in"), TT * (t + 1))
                for k in range(TT):
                    A(dsq[:, k, :], dtok[:, t % 2, k, :], ACT.Square).then_inc(sem("df_sq"), 1)

            def df_qkT(n):
                act.wait_ge(sem("df_T_filled"), n + 1)
                hd = 4 * (n // 4) + 2 * (n % 2)
                A(dT[:, (0, 1, 1, 0)[n // 2], hd:hd + 2, :], bank[7][:, :].rearrange("p (a s) -> p a s", a=2),
                  ACT.Copy).then_inc(sem("df_T"), 1)

            def df_exp(hd):
                if hd >= 2:
                    act.wait_ge(sem("df_aT_filled"), hd - 1)
                for m in range(2):
                    act.wait_ge(sem("df_max"), 4 * hd + 2 * (m + 1))
                    for q in range(TT):
                        col = q * 8 + 2 * (hd % 4) + m
                        A(dp[:, hd % 2, m, q, :], bank[4 + m][:, q * SEQ:(q + 1) * SEQ], ACT.Exp,
                          scale=dqr[:, hd // 4, col:col + 1], bias=dstat[:, hd, 4 + 2 * m + q:5 + 2 * m + q],
                          accum_out=dstat[:, hd, 8 + 2 * m + q:9 + 2 * m + q]).then_inc(sem("df_exp"), 1)

            def df_copy(hd):
                act.wait_ge(sem("df_aT_filled"), hd + 1)
                if hd >= 4:
                    act.wait_ge(sem("df_av"), hd - 3)
                A(daT[:, hd % 4, :], bank[6][:, :], ACT.Copy).then_inc(sem("df_aT"), 1)

            def df_out(hd):
                act.wait_ge(sem("df_av"), hd + 1)
                A(do[:, :, (hd - 1) * P:(hd + 1) * P], bank[7 - hd // 2 % 2][:, :].rearrange("p (q n) -> p q n", q=TT),
                  ACT.Copy).then_inc(sem("df_o"), 1)

            def df_osq(n):
                act.wait_ge(sem("df_ss"), TT * 4)
                act.wait_ge(sem("df_o"), n + 1)
                if n >= 2:
                    act.wait_ge(sem("df_oss"), n - 1)
                A(dsq[:, :, n % 2 * SEQ:(n % 2 + 1) * SEQ], do[:, :, n * SEQ:(n + 1) * SEQ], ACT.Square)\
                    .then_inc(sem("df_osq"), 1)

            act.wait_ge(sem("df_lam"), 2)
            A(lam[:, 2:4], lam[:, 0:2], ACT.Exp).then_inc(sem("df_lamexp"), 1)
            for u, step, arg in DF_PLAN:
                split_to(u + AHEAD + 1)
                if step == "tile":
                    df_tile(arg)
                elif step == "qkT":
                    df_qkT(arg)
                elif step == "scores":
                    df_exp(arg)
                elif step == "aT":
                    df_copy(arg)
                elif step == "av" and arg % 2 == 1:
                    df_out(arg)
                elif step == "osq":
                    df_osq(arg)
                elif step == "pair":
                    lhs_hi(X, lambda kt: cols[:, C_DF:C_DF + 1], (DF_Y_BANK[arg],), 2 * arg)
            ffn(1, Y)

            def conv_tile(t):
                split_to(END[t + 1] + AHEAD)
                c.wait(act, "w_used", END[t + 1])
                for k in range(TT):
                    A(cact[:, (t - CV_IN) % 2, k, 0, :], bank[2 * (t % 2) + k][:, 2 * P:3 * P], ACT.Copy,
                      scale=rstd[:, 6, k:k + 1])
                    A(cact[:, (t - CV_IN) % 2, k, 1, :], bank[2 * (t % 2) + k][:, 3 * P:4 * P], ACT.Silu,
                      scale=rstd[:, 6, k:k + 1]).then_inc(sem("cv_act"), 1)
                    c.up("cv_act")

            act.wait_ge(sem("rstd"), 7)
            for t in range(CV_IN, CV_IN + 3):
                conv_tile(t)
            with act.Fori(0, 2) as i:
                c.enter(i, {"w_used": 8, "w_hi": 8, "cv_act": 4, **{f"raw{r}": 32 for r in range(RAW)}})
                conv_tile(CV_IN + 3)
                conv_tile(CV_IN + 4)
                c.leave(2)
            pos[0] += 8
            conv_tile(CV_IN + 7)
            next_lhs(7, X, CV_OUT)

            def mb_tile(t):
                m = MB_QK.index(t) if t in MB_QK else None
                if m is not None:
                    if m >= 2:
                        act.wait_ge(sem("mb_T_filled"), 2 * (m - 1))
                    evacuate(MB_IN + t, 7, lambda k: mtok[:, m % 2, k, :], NW, "mb_in")
                    if m:
                        act.wait_ge(sem("mb_ss"), TT * m)
                    act.wait_ge(sem("mb_in"), TT * (t + 1))
                    for k in range(TT):
                        A(msq[:, k, :], mtok[:, m % 2, k, :], ACT.Square).then_inc(sem("mb_sq"), 1)
                elif t < 6:
                    evacuate(MB_IN + t, 7, lambda k: mv[:, k, t // 3 * NW:(t // 3 + 1) * NW], NW, "mb_in")
                else:
                    evacuate(MB_IN + t, 7, lambda k: mz[:, k, (t - 6) * NW:(t - 5) * NW], NW, "mb_in",
                             func=ACT.Silu)

            def mb_qkT(m):
                for b in range(2):
                    act.wait_ge(sem("mb_T_filled"), 2 * m + b + 1)
                    blk = 4 * (m // 2) + 2 * b
                    A(mT[:, m % 2, blk:blk + 2, :], bank[4 + b][:, :].rearrange("p (a s) -> p a s", a=2),
                      ACT.Copy, scale=mgain[:, m % 2:m % 2 + 1]).then_inc(sem("mb_T"), 1)

            def mb_exp(hd):
                act.wait_ge(sem("mb_max"), hd + 1)
                if hd >= 4:
                    act.wait_ge(sem("mb_pT_filled"), hd - 3)
                for q in range(TT):
                    lo, hi = (0, P) if q == 0 else (P, 3 * P)
                    A(mp[:, hd % 4, lo:hi], ms2[:, hd % 2, lo:hi], ACT.Exp, bias=mstat[:, hd % 2, 2 + q:3 + q],
                      accum_out=msum[:, q, hd:hd + 1]).then_inc(sem("mb_exp"), 1)

            def mb_copy(hd):
                act.wait_ge(sem("mb_pT_filled"), hd + 1)
                if hd >= 3:
                    act.wait_ge(sem("mb_av"), hd - 2)
                A(mpT[:, hd % 3, :], bank[6][:, 0:3 * P], ACT.Copy).then_inc(sem("mb_pT"), 1)

            act.wait_ge(sem("mb_gain"), 1)
            for u, step, arg in MB_PLAN:
                split_to(u + AHEAD + 1)
                if step == "tile":
                    mb_tile(arg)
                elif step == "qkT":
                    mb_qkT(arg)
                elif step == "exp":
                    mb_exp(arg)
                elif step == "pT":
                    mb_copy(arg)
                elif step == "half":
                    lhs_hi(Y, None, (4, 5) if arg == 0 else (6, 7))
            split_to(UNITS)

        @block.vector
        def _(dve):
            c = Count(sem)
            pos = [0]
            V = nc.vector

            def split_to(end):
                for u in range(pos[0], min(end, UNITS)):
                    c.wait(dve, "w_hi", u + 1)
                    w = Z_COLS if u == 0 else 2 * NW
                    V.tensor_tensor(wlo[:, u % RING, 0:w], raw[:, u % RAW, 0:w],
                                    whi[:, u % RING, 0:w].bitcast(F32), ALU.subtract).then_inc(sem("w_lo"), 1)
                pos[0] = max(pos[0], min(end, UNITS))

            def lhs_lo(dst, gain, banks, kt0=None):
                kt0 = 2 * (banks[0] - T_BANKS[0]) if kt0 is None else kt0
                for n, b in enumerate(banks):
                    c.wait(dve, "lhs_hi", c.up("lhs_hi"))
                    kt = kt0 + 2 * n
                    if gain is None:
                        V.tensor_tensor(dst[1][:, kt:kt + 2, :], bank[b][:, :].rearrange("p (k s) -> p k s", k=2),
                                        dst[0][:, kt:kt + 2, :].bitcast(F32), ALU.subtract)\
                            .then_inc(sem("lhs"), 1)
                        continue
                    for k in range(2):
                        last = V.scalar_tensor_tensor(dst[1][:, kt + k, :], bank[b][:, k * SEQ:(k + 1) * SEQ],
                                                      gain(kt + k), dst[0][:, kt + k, :].bitcast(F32),
                                                      ALU.mult, ALU.subtract)
                    last.then_inc(sem("lhs"), 1)

            def norm_gain(j):
                return lambda kt: cols[:, C_NORM + j * KT + kt:C_NORM + j * KT + kt + 1]

            def residual(tile, half):
                split_to(END[tile + 1] + AHEAD - 2)
                c.wait(dve, "w_used", END[tile + 1])
                for t in range(TT):
                    V.tensor_tensor(h[:, t, half * HALF:(half + 1) * HALF], h[:, t, half * HALF:(half + 1) * HALF],
                                    bank[2 * (tile % 2) + t][:, :], ALU.add).then_inc(sem("h_new"), 1)

            def mixer_out(tile, j, dst):
                residual(tile, 0)
                split_to(END[tile + 1] + 2 + AHEAD)
                lhs_lo(dst, norm_gain(j), (4, 5))
                residual(tile + 1, 1)
                split_to(END[tile + 2] + 1 + AHEAD)
                lhs_lo(dst, norm_gain(j), (6, 7))

            def parts_out(out, j, dst):
                residual(out + 2, 0)
                split_to(END[out + 4] - 1 + AHEAD)
                lhs_lo(dst, norm_gain(j), (4, 5))
                residual(out + 3, 1)
                split_to(END[out + 4] + 1 + AHEAD)
                lhs_lo(dst, norm_gain(j), (6, 7))

            V.memset(zT[32:33, :], 1.0).then_inc(sem("gla_ones"), 1)
            split_to(1)
            dve.wait_ge(sem("cols_in"), 16)
            lhs_lo(X, norm_gain(0), (4, 5, 6, 7))
            split_to(4)

            def gla_grown(d):
                dve.wait_ge(sem("gla_qkT"), 4)
                dve.wait_ge(sem("gla_exp"), 4 * (d + 1))
                V.tensor_tensor(qE[:, d, :], qkT[:, 0, :], grown[:, 0, :], ALU.mult).then_inc(sem("gla_gated"), 1)
                V.tensor_tensor(kE[:, d, :], qkT[:, 1, :], grown[:, 1, :], ALU.mult).then_inc(sem("gla_gated"), 1)
                edge = GLA_C - 1 if d == 0 else 0
                V.tensor_copy(decay[:, d, :], grown[:, 0, :].rearrange("p (a i) -> p a i", i=GLA_C)[:, :, edge])\
                    .then_inc(sem("gla_gated"), 1)
                dve.wait_ge(sem("gla_gated"), 4 * d + 3)
                V.tensor_tensor(kD[:, d, :].rearrange("p (a i) -> p a i", i=GLA_C),
                                kE[:, d, :].rearrange("p (a i) -> p a i", i=GLA_C),
                                decay[:, d, :].unsqueeze(2).to_broadcast([P, GLA_H * 4, GLA_C]), ALU.mult)\
                    .then_inc(sem("gla_gated"), 1)

            def gla_probs(d):
                if d == 0:
                    dve.wait_ge(sem("gla_gated"), 8)
                    V.memset(probs, 0.0).then_inc(sem("gla_zero"), 1)
                    dve.wait_ge(sem("gla_zero"), 1)
                    dve.wait_ge(sem("consts_in"), 16)
                for t in range(TT):
                    g = 2 * d + t
                    dve.wait_ge(sem("gla_scores"), g + 1)
                    if d:
                        dve.wait_ge(sem("gla_probs"), g - 1)
                    mask = consts[:, K_MASK + d * P:K_MASK + (d + 1) * P].bitcast(U32).unsqueeze(1)\
                        .to_broadcast([P, GLA_H, P])
                    V.copy_predicated(probs[:, t, :].rearrange("p (a i) -> p a i", a=GLA_H), mask,
                                      bank[T_BANKS[g]][:, :].rearrange("p (a i) -> p a i", a=GLA_H))\
                        .then_inc(sem("gla_probs"), 1)

            def gla_states(hd):
                st = states[hd % 2]

                def dec(d, ch):
                    return decay[:, d, hd * 4 + ch:hd * 4 + ch + 1]
                base = 6 * hd
                dve.wait_ge(sem("gla_u"), 2 * (hd + 1))
                if hd >= 2:
                    dve.wait_ge(sem("gla_head"), hd - 1)
                V.tensor_copy(st[:, 0, :], bank[5][:, 0:256]).then_inc(sem("gla_state"), 1)
                V.tensor_copy(st[:, 3, :], bank[6][:, 256:512]).then_inc(sem("gla_state"), 1)
                dve.wait_ge(sem("gla_state"), base + 1)
                V.scalar_tensor_tensor(st[:, 1, :], st[:, 0, :], dec(0, 1), bank[7][:, 0:256], ALU.mult, ALU.add)\
                    .then_inc(sem("gla_state"), 1)
                dve.wait_ge(sem("gla_state"), base + 2)
                V.scalar_tensor_tensor(st[:, 4, :], st[:, 3, :], dec(1, 2), bank[6][:, 0:256], ALU.mult, ALU.add)\
                    .then_inc(sem("gla_state"), 1)
                dve.wait_ge(sem("gla_state"), base + 3)
                V.scalar_tensor_tensor(st[:, 2, :], st[:, 1, :], dec(0, 2), bank[5][:, 256:512], ALU.mult, ALU.add)\
                    .then_inc(sem("gla_state"), 1)
                dve.wait_ge(sem("gla_state"), base + 4)
                V.scalar_tensor_tensor(st[:, 5, :], st[:, 4, :], dec(1, 1), bank[7][:, 256:512], ALU.mult, ALU.add)\
                    .then_inc(sem("gla_state"), 1)

            def gla_y(hd):
                dve.wait_ge(sem("gla_rstd"), hd + 1)
                dve.wait_ge(sem("gla_in"), 8 + 4 * (hd // 2))
                for t in range(TT):
                    at = slice(hd * GLA_HV, (hd + 1) * GLA_HV)
                    V.scalar_tensor_tensor(gr[:, t, at], bank[O_BANK[hd]][:, t * GLA_HV:(t + 1) * GLA_HV],
                                           oss[:, 2, t * GLA_H + hd:t * GLA_H + hd + 1], gr[:, t, at],
                                           ALU.mult, ALU.mult).then_inc(sem("gla_y"), 1)

            for u, step, arg in GLA_PLAN:
                split_to(u + AHEAD if u > END[GLA_IN + 1] + 2 else u + 1)
                if step == "zT":
                    V.memset(gtmp[:, 2, 0:2 * GLA_R], 1.0).then_inc(sem("gla_diag"), 1)
                    dve.wait_ge(sem("ident_in"), 16)
                    dve.wait_ge(sem("rstd"), 1)
                    for t in range(TT):
                        V.tensor_scalar(gtmp[:, t, 0:P], ident, rstd[:, 0, t:t + 1], None, ALU.mult)\
                            .then_inc(sem("gla_diag"), 1)
                    dve.wait_ge(sem("gla_diag"), 3)
                    dve.wait_ge(sem("w_used"), 1)
                    V.tensor_copy(zT[0:32, :], bank[0][0:32, 0:SEQ]).then_inc(sem("gla_z"), 1)
                    dve.wait_ge(sem("gla_factors"), 1)
                    dve.wait_ge(sem("gla_z"), 1)
                    V.tensor_tensor(zT[0:32, :], zT[0:32, :], bank[4][0:32, 0:SEQ], ALU.mult)\
                        .then_inc(sem("gla_zT"), 1)
                elif step == "gates":
                    dve.wait_ge(sem("gla_zT"), 1)
                    for g in range(4):
                        dve.wait_ge(sem("gla_pre"), g + 1)
                        V.tensor_scalar(la[:, g % 2, (g // 2) * GLA_K:(g // 2 + 1) * GLA_K], bank[T_BANKS[g]][:, :],
                                        0.0, None, ALU.min).then_inc(sem("gla_min"), 1)
                    for g in range(4):
                        dve.wait_ge(sem("gla_min"), g + 1)
                        V.scalar_tensor_tensor(gtmp[:, g, :], la[:, g % 2, (g // 2) * GLA_K:(g // 2 + 1) * GLA_K], 2.0,
                                               bank[T_BANKS[g]][:, :], ALU.mult, ALU.subtract)\
                            .then_inc(sem("gla_abs"), 1)
                elif step == "ln":
                    for g in range(4):
                        at = slice((g // 2) * GLA_K, (g // 2 + 1) * GLA_K)
                        dve.wait_ge(sem("gla_ln"), g + 1)
                        V.tensor_tensor(la[:, g % 2, at], la[:, g % 2, at], gtmp[:, g, :], ALU.subtract)\
                            .then_inc(sem("gla_la"), 1)
                elif step == "cumulate":
                    gla_grown(arg)
                elif step == "scores":
                    gla_probs(arg)
                elif step == "states":
                    gla_states(arg)
                elif step == "y":
                    gla_y(arg)
                elif step == "half":
                    lhs_lo(Y, gla_gain, *GLA_Y_BANKS[arg])
            parts_out(GLA_OUT, 1, X)

            def ffn(n, src):
                tin, tout, tple = layer(n)
                j = 3 * n + 1

                def product(t):
                    split_to(END[t + 1] + AHEAD)
                    for k in range(TT):
                        c.wait(dve, "ffn_silu", c.up("ffn_silu"))
                        V.scalar_tensor_tensor(mid[:, (t - tin) % 2, k, :], bank[2 * (t % 2) + k][:, 256:512],
                                               rstd[:, j, k:k + 1], sg[:, (t - tin) % 2, k, :],
                                               ALU.mult, ALU.mult).then_inc(sem("ffn_mid"), 1)

                def parts(t, kt, at):
                    b = T_BANKS[(t - tin) % 2]
                    src_ap = bank[b][:, :].rearrange("p (k s) -> p k s", k=2)
                    split_to(at + AHEAD)
                    c.wait(dve, "ffn_T_filled", c.up("ffn_T_filled"))
                    V.tensor_scalar(M[0][:, bass.ds(kt, 2), :], src_ap, 1.0, None, ALU.mult)\
                        .then_inc(sem("ffn_hi"), 1)
                    c.wait(dve, "ffn_hi", c.up("ffn_hi"))
                    V.tensor_tensor(M[1][:, bass.ds(kt, 2), :], src_ap, M[0][:, bass.ds(kt, 2), :].bitcast(F32),
                                    ALU.subtract).then_inc(sem("ffn_lhs"), 1)

                product(tin)
                for t in range(tin + 1, tin + 3):
                    parts(t - 1, 2 * (t - 1 - tin), END[t] + 2)
                    product(t)
                turns = (FT - 5) // 2
                with dve.Fori(0, turns) as i:
                    c.enter(i, {"w_hi": 8, "w_lo": 8, "ffn_silu": 4, "ffn_mid": 4, "ffn_T_filled": 2, "ffn_hi": 2,
                                "ffn_lhs": 2})
                    for t in (tin + 3, tin + 4):
                        parts(t - 1, i * 4 + 2 * (t - 1 - tin), END[t] + 2)
                        product(t)
                    c.leave(turns)
                pos[0] += 8 * (turns - 1)
                for t in range(tin + 3 + 2 * turns, tin + FT):
                    parts(t - 1, 2 * (t - 1 - tin), END[t] + 2)
                    product(t)
                parts(tin + FT - 1, FKT - 2, END[tout] + 2)
                split_to(END[tout] + 5 + AHEAD)
                dve.wait_ge(sem("pT_hi"), n + 1)
                V.tensor_tensor(PT[1][:, :, :], bank[6][:, :].rearrange("p (k s) -> p k s", k=2),
                                PT[0][:, :, :].bitcast(F32), ALU.subtract).then_inc(sem("pT"), 1)
                j += 1
                mixer_out(tout, j, src)
                for half in range(2):
                    t = tple + 2 * half
                    split_to(END[t + 2] + AHEAD - 2)
                    dve.wait_ge(sem("ple_sig"), TT * (2 * n + half + 1))
                    c.wait(dve, "w_used", END[t + 2])
                    for k in range(TT):
                        V.tensor_tensor(gated[:, k, :], sig[:, k, :], bank[2 * ((t + 1) % 2) + k][:, :], ALU.mult)\
                            .then_inc(sem("ple_gated"), 1)
                    for k in range(TT):
                        dve.wait_ge(sem("ple_gated"), TT * (2 * n + half) + k + 1)
                        V.tensor_tensor(h[:, k, half * HALF:(half + 1) * HALF], h[:, k, half * HALF:(half + 1) * HALF],
                                        gated[:, k, :], ALU.add).then_inc(sem("h_new"), 1)
                    split_to(END[t + 2] + (2 if half == 0 else 1) + AHEAD)
                    lhs_lo(Y if src is X else X, norm_gain(j + 1), (4, 5) if half == 0 else (6, 7))

            ffn(0, X)

            dve.wait_ge(sem("rows_in"), 16)
            cos = consts[:, K_COS:K_COS + 2 * DF_HD].rearrange("p (t e) -> p t e", t=TT)
            sin = consts[:, K_SIN:K_SIN + 2 * DF_HD].rearrange("p (t e) -> p t e", t=TT)
            HD2 = DF_HD // 2
            for w in range(2):
                for m in range(2):
                    g = rows[:, (R_GQ, R_GK)[w] + m * DF_HD:(R_GQ, R_GK)[w] + (m + 1) * DF_HD]
                    lo, hi = m * DF_HD, (m + 1) * DF_HD
                    V.tensor_tensor(rot[:, w, 0, :, lo:hi], cos, g.unsqueeze(1).to_broadcast([P, TT, DF_HD]), ALU.mult)
                    V.tensor_tensor(rot[:, w, 1, :, lo:lo + HD2], sin[:, :, 0:HD2],
                                    g[:, HD2:DF_HD].unsqueeze(1).to_broadcast([P, TT, HD2]), ALU.mult)
                    V.tensor_tensor(rot[:, w, 1, :, lo + HD2:hi], sin[:, :, HD2:DF_HD],
                                    g[:, 0:HD2].unsqueeze(1).to_broadcast([P, TT, HD2]), ALU.mult)\
                        .then_inc(sem("df_rot"), 1)
            lrow = rows[:, R_LAM:R_LAM + 4 * DF_HD].rearrange("p (a b e) -> p a b e", a=2, b=2)
            V.tensor_tensor(do[:, 0, 0:2 * DF_HD].rearrange("p (a e) -> p a e", a=2),
                            lrow[:, :, 0, :], lrow[:, :, 1, :], ALU.mult).then_inc(sem("df_lam"), 1)
            dve.wait_ge(sem("df_lam"), 1)
            V.tensor_reduce(lam[:, 0:2], do[:, 0, 0:2 * DF_HD].rearrange("p (a e) -> p a e", a=2), AXX, ALU.add)\
                .then_inc(sem("df_lam"), 1)

            def head_sums(t, sq, ss, sig_sq, sig_ss, sig_rstd):
                if t:
                    dve.wait_ge(sem(sig_rstd), t)
                dve.wait_ge(sem(sig_sq), TT * (t + 1))
                for k in range(TT):
                    V.tensor_reduce(ss[:, 0, k * 8:(k + 1) * 8], sq[:, k, :].rearrange("p (a e) -> p a e", a=8),
                                    AXX, ALU.add).then_inc(sem(sig_ss), 1)

            def head_unit(t, tok, ss, sig_rstd, signal):
                dve.wait_ge(sem(sig_rstd), t + 1)
                for k in range(TT):
                    x3 = tok[:, t % 2, k, :].rearrange("p (a e) -> p a e", a=8)
                    V.tensor_tensor(x3, x3, ss[:, 2, k * 8:(k + 1) * 8].unsqueeze(2).to_broadcast([P, 8, NW // 8]),
                                    ALU.mult).then_inc(sem(signal), 1)

            def df_rope(t):
                w = (0, 1, 1, 0)[t]
                if w:
                    head_unit(t, dtok, dss, "df_rstd", "df_unit")
                else:
                    dve.wait_ge(sem("df_sq"), TT * (t + 1))
                for k in range(TT):
                    x4 = dtok[:, t % 2, k, :].rearrange("p (a u e) -> p a u e", a=8, u=2)
                    m4 = dm2[:, k, :].rearrange("p (a u e) -> p a u e", a=8, u=2)
                    sn = rot[:, w, 1, k, :].rearrange("p (m u e) -> p m u e", m=2, u=2)
                    if w:
                        dve.wait_ge(sem("df_unit"), TT * (t - 1) + k + 1)
                    if t:
                        dve.wait_ge(sem("df_rope"), TT * (t - 1) + k + 1)
                    for u in range(2):
                        for m in range(2):
                            last = V.tensor_tensor(m4[:, m:8:2, u, :], x4[:, m:8:2, 1 - u, :],
                                                   sn[:, m, u, :].unsqueeze(1).to_broadcast([P, 4, HD2]), ALU.mult)
                    last.then_inc(sem("df_swap"), 1)

            def df_add(t):
                for k in range(TT):
                    xt = dtok[:, t % 2, k, :]
                    dve.wait_ge(sem("df_cos"), TT * t + k + 1)
                    V.tensor_tensor(xt, xt, dm2[:, k, :], ALU.add).then_inc(sem("df_rope"), 1)

            def df_lambda():
                dve.wait_ge(sem("df_lamexp"), 1)
                V.tensor_tensor(lam[:, 4:5], lam[:, 3:4], lam[:, 2:3], ALU.subtract).then_inc(sem("df_lam"), 1)
                dve.wait_ge(sem("df_lam"), 3)
                V.tensor_scalar(lam[:, 5:6], lam[:, 4:5], LAMBDA_INIT, None, ALU.subtract).then_inc(sem("df_lam"), 1)
                dve.wait_ge(sem("df_lam"), 4)

            def df_max(hd):
                stt = dstat[:, hd, :]
                factors = dqr[:, hd // 4, :].rearrange("p (q a m) -> p q a m", q=TT, a=4)
                if hd % 4 == 0:
                    dve.wait_ge(sem("df_rstd"), (1, 4)[hd // 4])
                for m in range(2):
                    dve.wait_ge(sem("df_scores"), 2 * hd + m + 1)
                    V.tensor_reduce(stt[:, 2 * m:2 * m + 2], bank[4 + m][:, :].rearrange("p (q k) -> p q k", q=TT),
                                    AXX, ALU.max).then_inc(sem("df_max"), 1)
                    dve.wait_ge(sem("df_max"), 4 * hd + 2 * m + 1)
                    V.scalar_tensor_tensor(stt[:, 4 + 2 * m:6 + 2 * m], stt[:, 2 * m:2 * m + 2], -1.0,
                                           factors[:, :, hd % 4, m], ALU.mult, ALU.mult).then_inc(sem("df_max"), 1)

            def df_soft(hd):
                stt = dstat[:, hd, :]
                dve.wait_ge(sem("df_exp"), 4 * (hd + 1))
                V.reciprocal(stt[:, 12:16], stt[:, 8:12]).then_inc(sem("df_recip"), 1)
                dve.wait_ge(sem("df_recip"), 2 * hd + 1)
                V.scalar_tensor_tensor(stt[:, 0:2], stt[:, 14:16], lam[:, 5:6], stt[:, 8:10], ALU.mult, ALU.mult)\
                    .then_inc(sem("df_recip"), 1)
                dve.wait_ge(sem("df_recip"), 2 * hd + 2)
                for q in range(TT):
                    V.scalar_tensor_tensor(dp[:, hd % 2, 0, q, :], dp[:, hd % 2, 1, q, :], stt[:, q:q + 1],
                                           dp[:, hd % 2, 0, q, :], ALU.mult, ALU.add).then_inc(sem("df_a"), 1)

            def df_osums(n):
                dve.wait_ge(sem("df_osq"), n + 1)
                dve.wait_ge(sem("df_rstd"), 4)
                if n:
                    dve.wait_ge(sem("df_orstd"), n)
                V.tensor_reduce(dss[:, 0, 0:4].rearrange("p (q a) -> p q a", q=TT),
                                dsq[:, :, n % 2 * SEQ:(n % 2 + 1) * SEQ].rearrange("p q (a e) -> p q a e", a=2),
                                AXX, ALU.add).then_inc(sem("df_oss"), 1)

            def df_y(n):
                dve.wait_ge(sem("df_orstd"), n + 1)
                o4 = do[:, :, n * SEQ:(n + 1) * SEQ].rearrange("p q (a e) -> p q a e", a=2)
                f4 = dss[:, 2, 0:4].rearrange("p (q a) -> p q a", q=TT)
                V.tensor_tensor(o4, o4, f4.unsqueeze(3).to_broadcast([P, TT, 2, P]), ALU.mult)\
                    .then_inc(sem("df_y"), 1)

            dve.wait_ge(sem("df_rot"), 4)
            df_lambda()
            for u, step, arg in DF_PLAN:
                split_to(u + AHEAD)
                if step == "sums":
                    head_sums(arg, dsq, dss, "df_sq", "df_ss", "df_rstd")
                elif step == "rope":
                    df_rope(arg)
                elif step == "add":
                    df_add(arg)
                elif step == "scores":
                    df_max(arg)
                elif step == "soft":
                    df_soft(arg)
                elif step == "osums":
                    df_osums(arg)
                elif step == "norm":
                    df_y(arg)
                elif step == "pair":
                    lhs_lo(X, lambda kt: cols[:, C_DF:C_DF + 1], (DF_Y_BANK[arg],), 2 * arg)
            parts_out(DF_OUT, 4, Y)
            ffn(1, Y)

            V.memset(cu[:, :, 0:CONV_K - 1], 0.0).then_inc(sem("cv_pad"), 1)

            def conv_product(t):
                split_to(END[t + 1] + AHEAD)
                for k in range(TT):
                    c.wait(dve, "cv_act", c.up("cv_act"))
                    for m in range(2):
                        src = bank[2 * (t % 2) + k][:, (1 - m) * P:(2 - m) * P]
                        last = V.scalar_tensor_tensor(cprod[:, (t - CV_IN) % 2, k, m, :], src, rstd[:, 6, k:k + 1],
                                                      cact[:, (t - CV_IN) % 2, k, m, :], ALU.mult, ALU.mult)
                    last.then_inc(sem("cv_prod"), 1)

            def conv_parts(t, blk, at):
                par = (t - CV_IN) % 2
                b = T_BANKS[par]
                split_to(at + AHEAD)
                c.wait(dve, "cv_T_filled", c.up("cv_T_filled"))

                def tap(k):
                    return cols[:, bass.ds(blk * CONV_K + (C_CONV + k), 1)]

                def step(ins):
                    ins.then_inc(sem("cv_step"), 1)
                    c.wait(dve, "cv_step", c.up("cv_step"))

                step(V.tensor_copy(cu[:, par, CONV_K - 1:], bank[b][:, 0:SEQ]))
                step(V.tensor_scalar(cc[:, 0, :], cu[:, par, 0:SEQ], tap(0), None, ALU.mult))
                step(V.scalar_tensor_tensor(cc[:, 1, :], cu[:, par, 1:SEQ + 1], tap(1), cc[:, 0, :],
                                            ALU.mult, ALU.add))
                step(V.scalar_tensor_tensor(cc[:, 2, :], cu[:, par, 2:SEQ + 2], tap(2), cc[:, 1, :],
                                            ALU.mult, ALU.add))
                step(V.tensor_tensor(cc[:, 3, :], cc[:, 2, :], bank[b][:, SEQ:2 * SEQ], ALU.mult))
                step(V.tensor_scalar(Y[0][:, bass.ds(blk, 1), :], cc[:, 3, :].unsqueeze(1), 1.0, None, ALU.mult))
                V.tensor_tensor(Y[1][:, bass.ds(blk, 1), :], cc[:, 3, :].unsqueeze(1),
                                Y[0][:, bass.ds(blk, 1), :].bitcast(F32), ALU.subtract).then_inc(sem("cv_lhs"), 1)

            dve.wait_ge(sem("cv_pad"), 1)
            conv_product(CV_IN)
            for t in range(CV_IN + 1, CV_IN + 3):
                conv_parts(t - 1, t - 1 - CV_IN, END[t] + 2)
                conv_product(t)
            with dve.Fori(0, 2) as i:
                c.enter(i, {"w_hi": 8, "w_lo": 8, "cv_act": 4, "cv_prod": 4, "cv_T_filled": 2, "cv_step": 12,
                            "cv_lhs": 2})
                for t in (CV_IN + 3, CV_IN + 4):
                    conv_parts(t - 1, i * 2 + (t - 1 - CV_IN), END[t] + 2)
                    conv_product(t)
                c.leave(2)
            pos[0] += 8
            conv_parts(CV_IN + 6, 6, END[CV_IN + 7] + 2)
            conv_product(CV_IN + 7)
            conv_parts(CV_IN + 7, 7, END[CV_OUT] + 2)
            mixer_out(CV_OUT, 7, X)

            V.tensor_scalar(mgain[:, 0:1], cols[:, C_QG:C_QG + 1], MB_HD ** -0.5, None, ALU.mult)
            V.tensor_copy(mgain[:, 1:2], cols[:, C_KG:C_KG + 1]).then_inc(sem("mb_gain"), 1)

            def mb_max(hd):
                slope = 2.0 ** (-8.0 * (hd + 1) / MB_H)
                dve.wait_ge(sem("mb_scores"), hd + 1)
                if hd >= 2:
                    dve.wait_ge(sem("mb_exp"), TT * (hd - 1))
                V.scalar_tensor_tensor(ms2[:, hd % 2, 0:3 * P], consts[:, K_DIST:K_DIST + 3 * P], slope,
                                       bank[4 + hd % 2][:, 0:3 * P], ALU.mult, ALU.add)\
                    .then_inc(sem("mb_biased"), 1)
                dve.wait_ge(sem("mb_biased"), hd + 1)
                V.tensor_reduce(mstat[:, hd % 2, 0:1], ms2[:, hd % 2, 0:P], AXX, ALU.max)
                V.tensor_reduce(mstat[:, hd % 2, 1:2], ms2[:, hd % 2, P:3 * P], AXX, ALU.max)\
                    .then_inc(sem("mb_rowmax"), 1)
                dve.wait_ge(sem("mb_rowmax"), hd + 1)
                V.tensor_scalar(mstat[:, hd % 2, 2:4], mstat[:, hd % 2, 0:2], -1.0, None, ALU.mult)\
                    .then_inc(sem("mb_max"), 1)

            def mb_o(hd):
                g = hd // 4
                dve.wait_ge(sem("mb_exp"), TT * (hd + 1))
                V.reciprocal(mrec[:, :, 4 * g:4 * g + 4], msum[:, :, 4 * g:4 * g + 4]).then_inc(sem("mb_recip"), 1)
                dve.wait_ge(sem("mb_recip"), g + 1)
                dve.wait_ge(sem("mb_av"), hd + 1)
                V.tensor_tensor(mo[:, :, g * SEQ:(g + 1) * SEQ].rearrange("p q (a e) -> p q a e", a=4),
                                bank[7][:, :].rearrange("p (q a e) -> p q a e", q=TT, a=4),
                                mrec[:, :, 4 * g:4 * g + 4].unsqueeze(3).to_broadcast([P, TT, 4, MB_HD]), ALU.mult)\
                    .then_inc(sem("mb_o"), 1)

            def mb_y(g):
                dve.wait_ge(sem("mb_o"), 2 * (g + 1))
                dve.wait_ge(sem("mb_in"), TT * (7 + g))
                V.tensor_tensor(mz[:, :, g * NW:(g + 1) * NW], mz[:, :, g * NW:(g + 1) * NW],
                                mo[:, :, g * NW:(g + 1) * NW], ALU.mult).then_inc(sem("mb_y"), 1)

            for u, step, arg in MB_PLAN:
                split_to(u + AHEAD)
                if step == "sums":
                    head_sums(arg, msq, mss, "mb_sq", "mb_ss", "mb_rstd")
                elif step == "unit":
                    head_unit(arg, mtok, mss, "mb_rstd", "mb_unit")
                elif step == "scores":
                    mb_max(arg)
                elif step == "av" and arg % 4 == 3:
                    mb_o(arg)
                elif step == "z":
                    mb_y(arg)
                elif step == "half":
                    lhs_lo(Y, None, (4, 5) if arg == 0 else (6, 7))
            split_to(UNITS)
            residual(MB_OUT + 2, 0)
            for t in range(TT):
                dve.wait_ge(sem("last"), t + 1)
                V.tensor_tensor(h[:, t, HALF:], h[:, t, HALF:], bank[2 * ((MB_OUT + 3) % 2) + t][:, :], ALU.add)\
                    .then_inc(sem("h_new"), 1)

        @block.tensor
        def _(pe):
            c = Count(sem)
            T = nc.tensor
            free = {}

            def claim(b):
                if b in free:
                    c.wait(pe, *free[b])

            def product(tile, lhs, signal, kt0=0, need=None, hooks=(), beside=None, part=None):
                pair = 2 * (tile % 2)
                hooks = dict(hooks)
                n = TILES[tile]
                for k in range(n):
                    if beside is not None:
                        beside(END[tile] + k)
                    if k in hooks:
                        hooks[k]()
                    if k == 0 and part != 1:
                        claim(pair)
                        claim(pair + 1)
                    if need is not None and need[kt0 // 2 + k] is not None:
                        c.wait(pe, *need[kt0 // 2 + k])
                    u = END[tile] + k
                    c.wait(pe, "w_lo", u + 1)
                    for t in range(TT):
                        for kk in range(2):
                            kt = kt0 + 2 * k + kk
                            for i, (a, w) in enumerate(((0, whi), (0, wlo), (1, whi))):
                                last = T.matmul(bank[pair + t][:, :],
                                                lhs[a][:, kt, t * P:(t + 1) * P],
                                                w[:, u % RING, kk * NW:(kk + 1) * NW],
                                                start=part != 1 and k == kk == i == 0,
                                                stop=part != 0 and k == n - 1 and kk == 1 and i == 2)
                        if u == UNITS - 1:
                            last.then_inc(sem("last"), 1)
                    if u != UNITS - 1:
                        last.then_inc(sem("w_used"), 1)
                if signal is not None:
                    for t in range(TT):
                        free[pair + t] = (signal, c.up(signal))

            def lhs_T(src, banks, kt0=None):
                need = []
                kt0 = 2 * (banks[0] - T_BANKS[0]) if kt0 is None else kt0
                for n, b in enumerate(banks):
                    claim(b)
                    for k in range(2):
                        for t in range(TT):
                            kt = kt0 + 2 * n + k
                            last = T.transpose(bank[b][:, k * SEQ + t * P:k * SEQ + (t + 1) * P],
                                               src[:, t, kt * P:(kt + 1) * P], ident)
                    last.then_inc(sem("lhs_filled"), 1)
                    free[b] = ("lhs", c.up("lhs"))
                    need.append(free[b])
                return need

            def h_T(half, version):
                pe.wait_ge(sem("h_new"), 4 * (version - 1) + 2 * (half + 1))
                return lhs_T(h, (4, 5) if half == 0 else (6, 7))

            def parts(tile, lhs, need, beside, version=None):
                got = []
                for part in range(2):
                    for t in range(2):
                        hooks = [(1, lambda: got.extend(h_T(0, version)))] if version and part == t == 1 else ()
                        product(tile + 2 * part + t, lhs, "h_new" if part else None, kt0=4 * part, part=part,
                                need=need if t == 0 else None, beside=beside, hooks=hooks)
                return got

            def chained(tile, lhs, signal, version, need=None, hooks=()):
                got = []
                product(tile, lhs, signal, need=need, hooks=hooks)
                product(tile + 1, lhs, signal, hooks=[(2, lambda: got.extend(h_T(0, version)))])
                return got

            pe.wait_ge(sem("ident_in"), 16)
            need = []
            for n in range(4):
                pe.wait_ge(sem(f"x_in{n}"), 16)
                need += lhs_T(h, (T_BANKS[n],))

            def z_product():
                pe.wait_ge(sem("w_lo"), 1)
                for kt in range(KT):
                    c.wait(pe, *need[kt // 2])
                    for i, (a, w) in enumerate(((0, whi), (0, wlo), (1, whi))):
                        last = T.matmul(bank[0][0:2 * GLA_R, 0:SEQ], w[:, 0, kt * 2 * GLA_R:(kt + 1) * 2 * GLA_R],
                                        X[a][:, kt, :], start=kt == i == 0, stop=kt == KT - 1 and i == 2)
                last.then_inc(sem("w_used"), 1)
                free[0] = ("gla_zT", 1)

            def z_factors():
                pe.wait_ge(sem("gla_diag"), 3)
                claim(4)
                for t in range(TT):
                    last = T.matmul(bank[4][0:2 * GLA_R, t * P:(t + 1) * P], gtmp[:, 2, 0:2 * GLA_R],
                                    gtmp[:, t, 0:P], start=True, stop=True)
                last.then_inc(sem("gla_factors"), 1)
                free[4] = ("gla_zT", 1)

            def pre_gates():
                pe.wait_ge(sem("gla_zT"), 1)
                pe.wait_ge(sem("gla_ones"), 1)
                pe.wait_ge(sem("wg_in"), 16)
                for g in range(4):
                    claim(T_BANKS[g])
                    T.matmul(bank[T_BANKS[g]][:, :], zT[0:33, (g % 2) * P:(g % 2 + 1) * P],
                             wg[0:33, (g // 2) * GLA_K:(g // 2 + 1) * GLA_K], start=True, stop=True)\
                        .then_inc(sem("gla_pre"), 1)
                    free[T_BANKS[g]] = ("gla_abs", g + 1)

            def qk_T():
                pe.wait_ge(sem("gla_in"), 4)
                for g in range(4):
                    claim(T_BANKS[g])
                    for k in range(2):
                        for t in range(TT):
                            hd = 2 * (g % 2) + k
                            last = T.transpose(bank[T_BANKS[g]][:, k * SEQ + t * P:k * SEQ + (t + 1) * P],
                                               qk_tok[:, g // 2, t, hd * P:(hd + 1) * P], ident)
                    last.then_inc(sem("gla_qkT_filled"), 1)
                    free[T_BANKS[g]] = ("gla_qkT", g + 1)

            def cumulate(d):
                pe.wait_ge(sem("gla_la"), 4)
                pe.wait_ge(sem("consts_in"), 16)
                for g in (2 * d, 2 * d + 1):
                    claim(T_BANKS[g])
                    for k in range(2):
                        for t in range(TT):
                            hd = 2 * (g % 2) + k
                            last = T.matmul(bank[T_BANKS[g]][:, k * SEQ + t * P:k * SEQ + (t + 1) * P],
                                            la[:, t, d * GLA_K + hd * P:d * GLA_K + (hd + 1) * P],
                                            consts[:, K_TRI + d * P:K_TRI + (d + 1) * P], start=True, stop=True)
                    last.then_inc(sem("gla_cum"), 1)
                    free[T_BANKS[g]] = ("gla_exp", 2 * (g + 1))

            def kD_T(d):
                pe.wait_ge(sem("gla_gated"), 4 * (d + 1))
                for t in range(TT):
                    g = 2 * d + t
                    claim(T_BANKS[g])
                    for hd in range(GLA_H):
                        last = T.transpose(bank[T_BANKS[g]][:, hd * P:(hd + 1) * P],
                                           kD[:, d, hd * SEQ + t * P:hd * SEQ + (t + 1) * P], ident)
                    last.then_inc(sem("gla_kDt_filled"), 1)
                    free[T_BANKS[g]] = ("gla_kDt", g + 1)

            def gla_scores(d):
                for t in range(TT):
                    g = 2 * d + t
                    claim(T_BANKS[g])
                    for hd in range(GLA_H):
                        at = slice(hd * SEQ + t * P, hd * SEQ + (t + 1) * P)
                        last = T.matmul(bank[T_BANKS[g]][:, hd * P:(hd + 1) * P], kE[:, d, at], qE[:, d, at],
                                        start=True, stop=True)
                    last.then_inc(sem("gla_scores"), 1)
                    free[T_BANKS[g]] = ("gla_probs", g + 1)

            def gla_u(hd):
                if hd == 0:
                    pe.wait_ge(sem("gla_kDt"), 4)
                if hd % 2 == 0:
                    pe.wait_ge(sem("gla_in"), 6 + 2 * hd)
                for b in (5, 6, 7):
                    claim(b)
                order = ((5, 0, 0, 0), (7, 0, 0, 1), (5, 1, 0, 2), (7, 1, 1, 1), (6, 0, 1, 2), (6, 1, 1, 3))
                for n, (b, at, d, ch) in enumerate(order):
                    t, r = ch // 2, (ch % 2) * GLA_C
                    if n == 5:
                        pe.wait_ge(sem("gla_u"), 2 * hd + 1)
                    last = T.matmul(bank[b][:, at * GLA_HV:(at + 1) * GLA_HV],
                                    kDt[r:r + GLA_C, d, t, hd * P:(hd + 1) * P],
                                    gv[r:r + GLA_C, t, hd * GLA_HV:(hd + 1) * GLA_HV], start=True, stop=True)
                    if n >= 4:
                        last.then_inc(sem("gla_u"), 1)
                for b, after in ((5, 5), (6, 4), (7, 6)):
                    free[b] = ("gla_state", 6 * hd + after)

            def gla_o(hd):
                st = states[hd % 2]
                b = O_BANK[hd]
                pe.wait_ge(sem("gla_state"), 6 * (hd + 1))
                pe.wait_ge(sem("gla_probs"), 4)
                claim(b)
                for t in range(TT):
                    at = slice(t * GLA_HV, (t + 1) * GLA_HV)
                    T.matmul(bank[b][:, at], probs[:, t, hd * P:(hd + 1) * P],
                             gv[:, t, hd * GLA_HV:(hd + 1) * GLA_HV], start=True, stop=True)
                    inter = [(ch, d) for d in range(2) for ch in (2 * t, 2 * t + 1)
                             if (ch > 0 if d == 0 else ch < 3)]
                    for n, (ch, d) in enumerate(inter):
                        r = (ch % 2) * GLA_C
                        last = T.matmul(bank[b][r:r + GLA_C, at],
                                        qE[:, d, hd * SEQ + ch * GLA_C:hd * SEQ + (ch + 1) * GLA_C],
                                        st[:, ch - 1 if d == 0 else 5 - ch, :], start=False, stop=True,
                                        skip_group_check=True)
                last.then_inc(sem("gla_head"), 1)
                free[b] = ("gla_y", 2 * hd + 2)

            gla_halves = [None] * 4

            def gla_beside(u):
                for at, step, arg in GLA_PLAN:
                    if at != u:
                        continue
                    if step == "zT":
                        z_factors()
                    elif step == "gates":
                        pre_gates()
                    elif step == "qkT":
                        qk_T()
                    elif step == "cumulate":
                        cumulate(arg)
                    elif step == "kDT":
                        kD_T(arg)
                    elif step == "scores":
                        gla_scores(arg)
                    elif step == "states":
                        gla_u(arg)
                    elif step == "out":
                        gla_o(arg)
                    elif step == "half":
                        pe.wait_ge(sem("gla_y"), 4 * (arg + 1))
                        gla_halves[2 * arg:2 * arg + 2] = lhs_T(gr, *GLA_Y_BANKS[arg])

            z_product()
            for t in range(1, 7):
                product(GLA_IN + t, X, "gla_in", beside=gla_beside)
            got = parts(GLA_OUT, Y, gla_halves, gla_beside, 1)

            def ffn(n, src, got):
                tin, tout, tple = layer(n)
                other = Y if src is X else X

                def mid_T(t):
                    b = T_BANKS[(t - tin) % 2]
                    c.wait(pe, "ffn_mid", TT * (t - tin + 1) + TT * FT * n)
                    claim(b)
                    for k in range(2):
                        for tt in range(TT):
                            last = T.transpose(bank[b][:, k * SEQ + tt * P:k * SEQ + (tt + 1) * P],
                                               mid[:, (t - tin) % 2, tt, k * P:(k + 1) * P], ident)
                    last.then_inc(sem("ffn_T_filled"), 1)
                    free[b] = ("ffn_lhs", c.up("ffn_lhs"))

                more = list(got) + [None, None]

                def second_half():
                    more[2:4] = h_T(1, 3 * n + 1)

                product(tin, src, "ffn_mid", need=more, hooks=[(1, second_half)])
                for t in range(tin + 1, tin + 3):
                    product(t, src, "ffn_mid", hooks=[(2, lambda t=t: mid_T(t - 1))])
                turns = (FT - 5) // 2
                with pe.Fori(0, turns) as i:
                    c.enter(i, {"w_lo": 8, "w_used": 8, "ffn_mid": 4, "ffn_lhs": 2})
                    for t in (tin + 3, tin + 4):
                        product(t, src, "ffn_mid", hooks=[(2, lambda t=t: mid_T(t - 1))])
                    c.leave(turns)
                for b, (name, value) in list(free.items()):
                    free[b] = (name, value + (turns - 1) * {"ffn_mid": 4, "ffn_lhs": 2}.get(name, 0))
                for t in range(tin + 3 + 2 * turns, tin + FT):
                    product(t, src, "ffn_mid", hooks=[(2, lambda t=t: mid_T(t - 1))])

                def p_T():
                    pe.wait_ge(sem("p_in"), 16)
                    claim(6)
                    for k in range(2):
                        for t in range(TT):
                            last = T.transpose(bank[6][:, k * SEQ + t * P:k * SEQ + (t + 1) * P],
                                               p_tok[:, n, t, k * P:(k + 1) * P], ident)
                    last.then_inc(sem("pT_filled"), 1)
                    free[6] = ("pT", n + 1)

                half0 = []
                need = [("ffn_lhs", FT * n + k + 1) for k in range(FT)]
                product(tout, M, "h_new", need=need, hooks=[(2, lambda: mid_T(tin + FT - 1)), (5, p_T)])
                product(tout + 1, M, "h_new", hooks=[(2, lambda: half0.extend(h_T(0, 3 * n + 2)))])
                more2 = list(half0) + [None, None]

                def second_half2():
                    more2[2:4] = h_T(1, 3 * n + 2)

                product(tple, src, "ple_sig", need=more2, hooks=[(1, second_half2)])
                product(tple + 1, PT, "ple_gated", need=[("pT", n + 1)])
                half1 = []
                product(tple + 2, src, "ple_sig", hooks=[(2, lambda: half1.extend(h_T(0, 3 * n + 3)))])
                product(tple + 3, PT, "ple_gated")
                c.up("h_new", 4)
                return half1

            half = ffn(0, X, got)

            def df_T(n):
                t, b = divmod(n, 2)
                pe.wait_ge(sem("df_rope"), TT * (t + 1))
                claim(7)
                for k in range(2):
                    for tt in range(TT):
                        last = T.transpose(bank[7][:, k * SEQ + tt * P:k * SEQ + (tt + 1) * P],
                                           dtok[:, t % 2, tt, (2 * b + k) * P:(2 * b + k + 1) * P], ident)
                last.then_inc(sem("df_T_filled"), 1)
                free[7] = ("df_T", n + 1)

            def df_scores(hd):
                if hd % 2 == 0:
                    pe.wait_ge(sem("df_T"), (3, 4, 7, 8)[hd // 2])
                claim(4)
                claim(5)
                for q in range(TT):
                    for m in range(2):
                        r = slice(m * DF_HD, (m + 1) * DF_HD)
                        last = T.matmul(bank[4 + m][:, q * SEQ:(q + 1) * SEQ], dT[r, 0, hd, q * P:(q + 1) * P],
                                        dT[r, 1, hd, :], start=True, stop=True)
                        if q == TT - 1:
                            last.then_inc(sem("df_scores"), 1)
                            free[4 + m] = ("df_exp", 4 * hd + 2 * (m + 1))

            def df_aT(hd):
                pe.wait_ge(sem("df_a"), TT * (hd + 1))
                claim(6)
                for k in range(TT):
                    for q in range(TT):
                        last = T.transpose(bank[6][:, k * SEQ + q * P:k * SEQ + (q + 1) * P],
                                           dp[:, hd % 2, 0, q, k * P:(k + 1) * P], ident)
                last.then_inc(sem("df_aT_filled"), 1)
                free[6] = ("df_aT", hd + 1)

            def df_av(hd):
                pe.wait_ge(sem("df_aT"), hd + 1)
                b = 7 - hd // 2 % 2
                if hd % 4 == 0:
                    pe.wait_ge(sem("df_in"), TT * (5 + hd // 4))
                if hd % 2 == 0:
                    claim(b)
                for q in range(TT):
                    for k in range(TT):
                        last = T.matmul(bank[b][:, q * SEQ + (hd % 2) * P:q * SEQ + (hd % 2 + 1) * P],
                                        daT[:, hd % 4, k * SEQ + q * P:k * SEQ + (q + 1) * P],
                                        dv[:, k, hd * P:(hd + 1) * P], start=k == 0, stop=k == TT - 1)
                last.then_inc(sem("df_av"), 1)
                if hd % 2 == 1:
                    free[b] = ("df_o", hd // 2 + 1)

            df_half0, df_pairs = list(half) + [None, None], [None] * 4

            def df_beside(u):
                for at, step, arg in DF_PLAN:
                    if at != u:
                        continue
                    if step == "second":
                        df_half0[2:4] = h_T(1, 3)
                    elif step == "qkT":
                        df_T(arg)
                    elif step == "scores":
                        df_scores(arg)
                    elif step == "aT":
                        df_aT(arg)
                    elif step == "av":
                        df_av(arg)
                    elif step == "pair":
                        pe.wait_ge(sem("df_y"), arg + 1)
                        df_pairs[arg:arg + 1] = lhs_T(do, (DF_Y_BANK[arg],), 2 * arg)

            product(DF_IN, Y, "df_in", need=df_half0, beside=df_beside)
            for t in range(1, 6):
                product(DF_IN + t, Y, "df_in", beside=df_beside)
            half = ffn(1, Y, parts(DF_OUT, X, df_pairs, df_beside, 4))

            def cv_T(t):
                b = T_BANKS[(t - CV_IN) % 2]
                c.wait(pe, "cv_prod", TT * (t - CV_IN + 1))
                claim(b)
                for m in range(2):
                    for tt in range(TT):
                        last = T.transpose(bank[b][:, m * SEQ + tt * P:m * SEQ + (tt + 1) * P],
                                           cprod[:, (t - CV_IN) % 2, tt, m, :], ident)
                last.then_inc(sem("cv_T_filled"), 1)
                free[b] = ("cv_lhs", c.up("cv_lhs"))

            more3 = list(half) + [None, None]

            def cv_second():
                more3[2:4] = h_T(1, 6)

            product(CV_IN, X, "cv_prod", need=more3, hooks=[(1, cv_second)])
            for t in (CV_IN + 1, CV_IN + 2):
                product(t, X, "cv_prod", hooks=[(2, lambda t=t: cv_T(t - 1))])
            with pe.Fori(0, 2) as i:
                c.enter(i, {"w_lo": 8, "w_used": 8, "cv_prod": 4, "cv_lhs": 2})
                for t in (CV_IN + 3, CV_IN + 4):
                    product(t, X, "cv_prod", hooks=[(2, lambda t=t: cv_T(t - 1))])
                c.leave(2)
            for b, (name, value) in list(free.items()):
                free[b] = (name, value + {"cv_prod": 4, "cv_lhs": 2}.get(name, 0))
            product(CV_IN + 7, X, "cv_prod", hooks=[(2, lambda: cv_T(CV_IN + 6))])
            got = chained(CV_OUT, Y, "h_new", 7, need=[("cv_lhs", 2 * (k + 1)) for k in range(4)],
                          hooks=[(2, lambda: cv_T(CV_IN + 7))])

            def mb_T(m):
                pe.wait_ge(sem("mb_unit"), TT * (m + 1))
                for b in range(2):
                    claim(4 + b)
                    for k in range(2):
                        for tt in range(TT):
                            last = T.transpose(bank[4 + b][:, k * SEQ + tt * P:k * SEQ + (tt + 1) * P],
                                               mtok[:, m % 2, tt, (2 * b + k) * P:(2 * b + k + 1) * P], ident)
                    last.then_inc(sem("mb_T_filled"), 1)
                    free[4 + b] = ("mb_T", 2 * m + b + 1)

            def mb_scores(hd):
                b = 4 + hd % 2
                if hd % 8 == 0:
                    pe.wait_ge(sem("mb_T"), 4 * (hd // 8 + 1))
                claim(b)
                r, blk = slice((hd % 2) * MB_HD, (hd % 2 + 1) * MB_HD), hd // 2
                T.matmul(bank[b][:, 0:P], mT[r, 0, blk, 0:P], mT[r, 1, blk, 0:P], start=True, stop=True)
                T.matmul(bank[b][:, P:3 * P], mT[r, 0, blk, P:SEQ], mT[r, 1, blk, :], start=True, stop=True)\
                    .then_inc(sem("mb_scores"), 1)
                free[b] = ("mb_biased", hd + 1)

            def mb_pT(hd):
                pe.wait_ge(sem("mb_exp"), TT * (hd + 1))
                claim(6)
                for n in range(3):
                    last = T.transpose(bank[6][:, n * P:(n + 1) * P], mp[:, hd % 4, n * P:(n + 1) * P], ident)
                last.then_inc(sem("mb_pT_filled"), 1)
                free[6] = ("mb_pT", hd + 1)

            def mb_av(hd):
                if hd % 8 == 0:
                    pe.wait_ge(sem("mb_in"), TT * (3 + 3 * (hd // 8)))
                pe.wait_ge(sem("mb_pT"), hd + 1)
                if hd % 4 == 0:
                    claim(7)
                at = [slice(q * SEQ + (hd % 4) * MB_HD, q * SEQ + (hd % 4 + 1) * MB_HD) for q in range(TT)]
                T.matmul(bank[7][:, at[0]], mpT[:, hd % 3, 0:P], mv[:, 0, hd * MB_HD:(hd + 1) * MB_HD],
                         start=True, stop=True)
                for k in range(2):
                    last = T.matmul(bank[7][:, at[1]], mpT[:, hd % 3, (k + 1) * P:(k + 2) * P],
                                    mv[:, k, hd * MB_HD:(hd + 1) * MB_HD], start=k == 0, stop=k == 1)
                last.then_inc(sem("mb_av"), 1)
                if hd % 4 == 3:
                    free[7] = ("mb_o", hd // 4 + 1)

            half0, halves = list(got) + [None, None], [None] * 4

            def mb_beside(u):
                for at, step, arg in MB_PLAN:
                    if at != u:
                        continue
                    if step == "second":
                        half0[2:4] = h_T(1, 7)
                    elif step == "qkT":
                        mb_T(arg)
                    elif step == "scores":
                        mb_scores(arg)
                    elif step == "pT":
                        mb_pT(arg)
                    elif step == "av":
                        mb_av(arg)
                    elif step == "half":
                        pe.wait_ge(sem("mb_y"), arg + 1)
                        halves[2 * arg:2 * arg + 2] = lhs_T(mz, (4, 5) if arg == 0 else (6, 7))

            product(MB_IN, X, "mb_in", need=half0, beside=mb_beside)
            for t in range(1, 8):
                product(MB_IN + t, X, "mb_in", beside=mb_beside)
            parts(MB_OUT, Y, halves, mb_beside)


def _units(w, tiles):
    k = w.shape[0]
    return np.concatenate([w[:, t].reshape(k // 256, 2, P, NW).transpose(0, 2, 1, 3).reshape(k // 256, P, 2 * NW)
                           for t in tiles])


def _plain(n):
    return [slice(t, t + NW) for t in range(0, n, NW)]


def _ordered(width, *tiles):
    return [slice(t * width, (t + 1) * width) for t in tiles]


def _parts(w):
    return np.concatenate([_units(w[k:k + HALF], _plain(D)) for k in (0, HALF)])


def _grouped(n, parts, of):
    size = n // parts
    return [np.concatenate([np.arange(q * size + j, q * size + j + of) for q in range(parts)])
            for j in range(0, size, of)]


def _constants():
    i = np.arange(P)
    same = (i[:, None] // GLA_C) == (i[None, :] // GLA_C)
    up = same & (i[:, None] <= i[None, :])
    down = same & (i[:, None] >= i[None, :])
    strict = same & (i[:, None] > i[None, :])
    half = DF_HD // 2
    inv = np.float32(10000.0) ** (-np.arange(half, dtype=np.float32) * np.float32(2.0) / np.float32(DF_HD))
    ang = np.arange(SEQ, dtype=np.float32)[:, None] * inv[None, :].astype(np.float32)
    cos, sin = np.cos(ang), np.sin(ang)
    cos = np.concatenate([cos, cos], 1).reshape(TT, P, DF_HD).transpose(1, 0, 2).reshape(P, -1)
    sin = np.concatenate([-sin, sin], 1).reshape(TT, P, DF_HD).transpose(1, 0, 2).reshape(P, -1)
    k = np.arange(SEQ)
    dist = [np.where(k[None, :n] <= i[:, None] + q0, k[None, :n] - i[:, None] - q0, -1e32)
            for q0, n in ((0, P), (P, SEQ))]
    return np.concatenate([np.eye(P), up / 16.0, down / 16.0, up, strict, cos, sin] + dist, 1).astype(np.float32)


def kernel(**inputs):
    import concourse.bacc as _bacc
    from concourse.bass_utils import run_bass_kernel_spmd as _run

    a = {name: np.asarray(value) for name, value in inputs.items()}
    gla = a["gla_w_in"][0]
    z = gla[:, 3 * D:3 * D + 2 * GLA_R].reshape(KT, P, 2 * GLA_R).transpose(1, 0, 2).reshape(P, -1)
    first = np.zeros((1, P, 2 * NW), np.float32)
    first[0, :, :z.shape[1]] = z

    def layer(n):
        gate, proj = _units(a["ple_w_gate"][n], _plain(D)), _units(a["ple_w_proj"][n], _plain(D))
        return [_units(a["ffn_w_in"][n], _grouped(2 * FF, 2, 256)), _units(a["ffn_w_out"][n], _plain(D)),
                gate[:KT // 2], proj[:1], gate[KT // 2:], proj[1:]]

    stream = np.concatenate(
        [first, _units(gla, _ordered(NW, 0, 1, 2, 4, 3, 5)), _parts(a["gla_w_out"][0])] + layer(0)
        + [_units(a["diff_w_in"][0], _ordered(NW, 0, 2, 3, 1, 4, 5)), _parts(a["diff_w_out"][0])] + layer(1)
        + [_units(a["conv_w_in_2"][0], _grouped(4 * D, 4, P)), _units(a["conv_w_out_2"][0], _plain(D)),
           _units(a["attn_w_in_2"][0], _ordered(NW, 0, 2, 4, 1, 3, 5, 6, 7)), _parts(a["attn_w_out_2"][0])])
    norms = [a["norm_mix"][0], a["norm_ffn"][0], a["ple_norm"][0], a["norm_mix"][1], a["norm_ffn"][1],
             a["ple_norm"][1], a["norm_g_2"][0], a["norm_g_2"][1]]
    cols = np.concatenate(
        [g.reshape(-1, P).T for g in norms + [a["gla_g_out"][0], a["diff_g_sub"][0]]]
        + [np.concatenate([a[g][0]] * 2)[:, None] for g in ("q_norm_g_2", "k_norm_g_2")]
        + [a["conv_w_2"][0].reshape(CONV_K, KT, P).transpose(2, 1, 0).reshape(P, -1)], 1)
    rows = np.concatenate([a["diff_g_q"][0].ravel(), a["diff_g_k"][0].ravel()]
                          + [a[f"diff_lam_{n}"][0] for n in ("q1", "k1", "q2", "k2")])[None]
    wgate = np.zeros((33, 2 * GLA_K), np.float32)
    wgate[0:GLA_R, :GLA_K], wgate[GLA_R:2 * GLA_R, GLA_K:] = a["gla_w_gate_f"][0], a["gla_w_gate_b"][0]
    wgate[32, :GLA_K], wgate[32, GLA_K:] = a["gla_b_gate_f"][0], a["gla_b_gate_b"][0]
    arrays = {"stream": stream, "x": a["x"][0], "p": a["p"][:, 0], "cols": cols, "rows": rows,
              "consts": _constants(), "wgate": wgate}
    arrays = {name: np.ascontiguousarray(value) for name, value in arrays.items()}
    nc = _bacc.Bacc("TRN2", target_bir_lowering=False, num_devices=1)
    args = [nc.dram_tensor(f"{name}_dram", value.shape, F32, kind="ExternalInput").ap() for name, value in arrays.items()]
    out = nc.dram_tensor("out", (SEQ, D), F32, kind="ExternalOutput").ap()
    stream_, x_, p_, cols_, rows_, consts_, wgate_ = args
    build(nc, stream_, x_, p_, cols_, rows_, consts_, wgate_, out)
    r = _run(nc, [{f"{name}_dram": value for name, value in arrays.items()}], core_ids=[0])
    return r.results[0]["out"].reshape(1, SEQ, D)
```
